# Optimizing a Trainium2 kernel written in Bass

```python
import math
import jax, jax.numpy as jnp
from jax import lax
import numpy as np

D_MODEL = 1024
BATCH = 1
SEQ = 512
DEPTH = 1

PLE_DIM = 256
ATTN_WIDTH = D_MODEL // 2
DIFF_HEADS = 4
DIFF_HEAD_DIM = ATTN_WIDTH // DIFF_HEADS // 2
CONV_WIDTH = D_MODEL // 2
CONV_KERNEL = 31
N_EXPERTS = 32
TOP_K = 4
EXPERT_FF = D_MODEL
SWIGLU_ALPHA = 1.702
SWIGLU_LIMIT = 7.0
Q_BLOCK = 128
MOE_BLOCK = 128
EPS = 1e-5
IN_COLS = 3 * ATTN_WIDTH + 2 * CONV_WIDTH + 2 * D_MODEL

kernel_name = "hybrid_diffattn_conformer_moe_ple"

def rms_norm(x, g):
    x32 = x.astype(jnp.float32)
    y = x32 * lax.rsqrt(jnp.mean(x32 * x32, axis=-1, keepdims=True) + EPS)
    return (y * g.astype(jnp.float32)).astype(x.dtype)

def layer_norm(x, g, b):
    x32 = x.astype(jnp.float32)
    mu = jnp.mean(x32, axis=-1, keepdims=True)
    xc = x32 - mu
    y = xc * lax.rsqrt(jnp.mean(xc * xc, axis=-1, keepdims=True) + EPS)
    return (y * g.astype(jnp.float32) + b.astype(jnp.float32)).astype(x.dtype)

def diff_attention(q, k, v, lam, lam_init, g_subln):
    B, S, _ = q.shape
    H, d = DIFF_HEADS, DIFF_HEAD_DIM
    q32 = q.reshape(B, S, H, 2, d).astype(jnp.float32)
    k32 = k.reshape(B, S, H, 2, d).astype(jnp.float32)
    v = v.reshape(B, S, H, 2 * d)
    scale = d ** -0.5
    kpos = jnp.arange(S)

    def block(i):
        q0 = i * Q_BLOCK
        qb = lax.dynamic_slice_in_dim(q32, q0, Q_BLOCK, axis=1)
        s = jnp.einsum('bqhcd,bkhcd->bhcqk', qb, k32) * scale
        qpos = q0 + jnp.arange(Q_BLOCK)
        s = jnp.where(qpos[:, None] >= kpos[None, :], s, -jnp.inf)
        pr = jax.nn.softmax(s, axis=-1)
        attn = pr[:, :, 0] - lam * pr[:, :, 1]
        return jnp.einsum('bhqk,bkhe->bqhe', attn.astype(v.dtype), v)

    o = lax.map(block, jnp.arange(S // Q_BLOCK))
    o = jnp.transpose(o, (1, 0, 2, 3, 4)).reshape(B, S, H, 2 * d)
    o = rms_norm(o, g_subln) * (1.0 - lam_init)
    return o.reshape(B, S, H * 2 * d)

def conformer_conv(c, w_dw, b_dw, g_ln, b_ln):
    z = c[..., :CONV_WIDTH] * jax.nn.sigmoid(c[..., CONV_WIDTH:])
    z = lax.conv_general_dilated(
        z, w_dw[:, None, :], window_strides=(1,),
        padding=[(CONV_KERNEL - 1, 0)],
        dimension_numbers=('NWC', 'WIO', 'NWC'),
        feature_group_count=CONV_WIDTH) + b_dw
    z = layer_norm(z, g_ln, b_ln)
    return jax.nn.silu(z)

def moe(u, w_router, b_router, w_gu, b_gu, w_down, b_down):
    B, S, D = u.shape
    N = B * S
    A = N * TOP_K
    xt = u.reshape(N, D)
    logits = (xt @ w_router + b_router).astype(jnp.float32)
    top_val, top_idx = lax.top_k(logits, TOP_K)
    gates = jax.nn.softmax(top_val, axis=-1).astype(xt.dtype)

    e_flat = top_idx.reshape(A)
    order = jnp.argsort(e_flat)
    e_sorted = e_flat[order]
    tok_sorted = order // TOP_K
    g_sorted = gates.reshape(A)[order]
    counts = jnp.bincount(e_flat, length=N_EXPERTS)
    start = jnp.cumsum(counts) - counts
    padded = (counts + MOE_BLOCK - 1) // MOE_BLOCK * MOE_BLOCK
    pend = jnp.cumsum(padded)
    pstart = pend - padded
    pos_sorted = pstart[e_sorted] + (jnp.arange(A) - start[e_sorted])

    n_blocks = -(-A // MOE_BLOCK) + N_EXPERTS
    R = n_blocks * MOE_BLOCK
    row_tok = jnp.zeros((R,), jnp.int32).at[pos_sorted].set(tok_sorted.astype(jnp.int32))
    row_gate = jnp.zeros((R,), xt.dtype).at[pos_sorted].set(g_sorted)
    block_expert = jnp.clip(
        jnp.searchsorted(pend, jnp.arange(n_blocks) * MOE_BLOCK, side='right'),
        0, N_EXPERTS - 1)

    def expert_block(args):
        e, rows = args
        xb = xt[rows]
        gu = xb @ w_gu[e] + b_gu[e]
        gate = jnp.minimum(gu[:, ::2], SWIGLU_LIMIT)
        lin = jnp.clip(gu[:, 1::2], -SWIGLU_LIMIT, SWIGLU_LIMIT)
        glu = gate * jax.nn.sigmoid(gate * SWIGLU_ALPHA)
        return ((lin + 1.0) * glu) @ w_down[e] + b_down[e]

    y = lax.map(expert_block, (block_expert, row_tok.reshape(n_blocks, MOE_BLOCK)))
    y = y.reshape(R, D) * row_gate[:, None]
    out = jnp.zeros((N, D), xt.dtype).at[row_tok].add(y)
    return out.reshape(B, S, D)

def setup_inputs(seed: int = 0) -> dict:
    key = jax.random.key(seed)
    ks = iter(jax.random.split(key, 32))

    def nrm(shape, fan_in):
        return jax.random.normal(next(ks), shape, jnp.float32) * (fan_in ** -0.5)

    def gain(shape):
        return 1.0 + 0.02 * jax.random.normal(next(ks), shape, jnp.float32)

    def small(shape, s=0.02):
        return s * jax.random.normal(next(ks), shape, jnp.float32)

    L, D, E, F = DEPTH, D_MODEL, N_EXPERTS, EXPERT_FF
    return {
        "x": jax.random.normal(next(ks), (BATCH, SEQ, D), jnp.float32),
        "p": jax.random.normal(next(ks), (DEPTH, BATCH, SEQ, PLE_DIM), jnp.float32),
        "g_mix": gain((L, D)),
        "w_in": nrm((L, D, IN_COLS), D),
        "lambda_q1": small((L, DIFF_HEAD_DIM), 0.1),
        "lambda_k1": small((L, DIFF_HEAD_DIM), 0.1),
        "lambda_q2": small((L, DIFF_HEAD_DIM), 0.1),
        "lambda_k2": small((L, DIFF_HEAD_DIM), 0.1),
        "g_subln": gain((L, 2 * DIFF_HEAD_DIM)),
        "w_attn_out": nrm((L, ATTN_WIDTH, D), ATTN_WIDTH),
        "w_dw": nrm((L, CONV_KERNEL, CONV_WIDTH), CONV_KERNEL),
        "b_dw": small((L, CONV_WIDTH)),
        "g_conv_ln": gain((L, CONV_WIDTH)),
        "b_conv_ln": small((L, CONV_WIDTH)),
        "w_conv_out": nrm((L, CONV_WIDTH, D), CONV_WIDTH),
        "w_o": nrm((L, D, D), D),
        "g_ffn": gain((L, D)),
        "w_router": nrm((L, D, E), D),
        "b_router": small((L, E), 0.01),
        "w_gate_up": nrm((L, E, D, 2 * F), D),
        "b_gate_up": small((L, E, 2 * F)),
        "w_down": nrm((L, E, F, D), F),
        "b_down": small((L, E, D)),
        "w_ple": nrm((L, PLE_DIM, D), PLE_DIM),
        "g_ple": gain((L, D)),
        "w_ple_gate": nrm((L, D, D), D),
        "g_final": gain((D,)),
    }

def reference(x, p, g_mix, w_in, lambda_q1, lambda_k1, lambda_q2, lambda_k2, g_subln,
              w_attn_out, w_dw, b_dw, g_conv_ln, b_conv_ln, w_conv_out, w_o, g_ffn,
              w_router, b_router, w_gate_up, b_gate_up, w_down, b_down,
              w_ple, g_ple, w_ple_gate, g_final):
    h = x
    splits = np.cumsum([ATTN_WIDTH, ATTN_WIDTH, ATTN_WIDTH, 2 * CONV_WIDTH, D_MODEL]).tolist()
    for i in range(DEPTH):
        u = rms_norm(h, g_mix[i])
        proj = u @ w_in[i]
        q, k, v, c_in, gate_a, gate_b = jnp.split(proj, splits, axis=-1)

        lam_init = 0.8 - 0.6 * math.exp(-0.3 * i)
        lam = (jnp.exp(jnp.sum(lambda_q1[i] * lambda_k1[i]).astype(jnp.float32))
               - jnp.exp(jnp.sum(lambda_q2[i] * lambda_k2[i]).astype(jnp.float32))
               + lam_init)
        a = diff_attention(q, k, v, lam, lam_init, g_subln[i]) @ w_attn_out[i]
        b = conformer_conv(c_in, w_dw[i], b_dw[i], g_conv_ln[i], b_conv_ln[i]) @ w_conv_out[i]
        m = jax.nn.sigmoid(gate_a) * a + jax.nn.sigmoid(gate_b) * b
        h = h + m @ w_o[i]

        h = h + moe(rms_norm(h, g_ffn[i]), w_router[i], b_router[i],
                    w_gate_up[i], b_gate_up[i], w_down[i], b_down[i])

        h = h + (p[i] @ w_ple[i]) * jax.nn.sigmoid(rms_norm(h, g_ple[i]) @ w_ple_gate[i])
    return rms_norm(h, g_final)


_drawn_inputs = setup_inputs


def setup_inputs(seed=0):
    import zlib

    import numpy as np

    out = dict(_drawn_inputs(seed))
    spreads = {}
    factors = {'b_conv_ln': 3.356,
     'b_gate_up': 6.061,
     'b_down': 6.936,
     'g_ple': 131.88,
     'g_final': 22.187,
     'g_conv_ln': 2.7,
     'g_subln': 2.771}
    for name, (base, spread) in spreads.items():
        noise = np.random.default_rng([zlib.crc32(name.encode()), seed]).standard_normal(out[name].shape)
        drawn = base * np.exp(spread * noise) if base else spread * noise
        out[name] = __import__('jax').numpy.asarray(drawn.astype(out[name].dtype))
    for name, factor in factors.items():
        out[name] = (out[name] * factor).astype(out[name].dtype)
    return out
```

```python
from contextlib import ExitStack

import concourse.bass as bass
from concourse import mybir

F32 = mybir.dt.float32
I32 = mybir.dt.int32
U32 = mybir.dt.uint32
ALU = mybir.AluOpType
ACT = mybir.ActivationFunctionType
AX_X = mybir.AxisListType.X

P = 128
BANK = 512
EPS = 1e-5
NEG = -1e30
SLOTS = 6
BT = P


def trunk_layer(nc, x, p, g_mix, w_in, lambda_q1, lambda_k1, lambda_q2, lambda_k2, g_subln,
                w_attn_out, w_dw, b_dw, g_conv_ln, b_conv_ln, w_conv_out, w_o, g_ffn,
                w_router, b_router, w_gate_up, b_gate_up, w_down, b_down,
                w_ple, g_ple, w_ple_gate, g_final, out):
    S, D = x.shape[1], x.shape[2]
    AW = w_attn_out.shape[1]
    CW = w_conv_out.shape[1]
    PLE = p.shape[3]
    E = w_router.shape[2]
    F = w_down.shape[2]
    TAPS = w_dw.shape[1]
    HD = g_subln.shape[1]
    H = AW // HD
    QD = HD // 2
    TOP = 4
    TB = S // P
    KD = D // P
    FT = F // P
    CT = CW // P
    PAD = TAPS - 1
    ZW = S + PAD + 2
    MAXB = S * TOP // BT + E
    SCALE = float(QD) ** -0.5
    LAM_INIT = 0.2
    ALPHA, LIMIT = 1.702, 7.0
    assert (S, D, AW, CW, E, F, H) == (512, 1024, 512, 512, 32, 1024, 4) and TB == 4

    x_t = x.rearrange("a (t q) d -> q (a t) d", q=P)
    p_t = p.rearrange("l a (t q) d -> q (l a t) d", q=P)
    out_t = out.rearrange("a (t q) d -> q (a t) d", q=P)

    u_rows = nc.dram_tensor("u_rows", (S, D), F32, kind="Internal").ap()
    sum_rows = nc.dram_tensor("sum_rows", (S + BT, D), F32, kind="Internal").ap()

    w_in_v = w_in.rearrange("l (k q) n -> q (l k) n", q=P)
    w_ao_v = w_attn_out.rearrange("l (k q) n -> q (l k) n", q=P)
    w_co_v = w_conv_out.rearrange("l (k q) n -> q (l k) n", q=P)
    w_o_v = w_o.rearrange("l (k q) n -> q (l k) n", q=P)
    w_ple_v = w_ple.rearrange("l (k q) n -> q (l k) n", q=P)
    w_pg_v = w_ple_gate.rearrange("l (k q) n -> q (l k) n", q=P)

    def cols(view, c):
        return view[:, :, c * 512:(c + 1) * 512]

    dense = [("conv_a", cols(w_in_v, 3)), ("conv_g", cols(w_in_v, 4)), ("q", cols(w_in_v, 0)),
             ("k", cols(w_in_v, 1)), ("v", cols(w_in_v, 2)),
             ("ga0", cols(w_in_v, 5)), ("ao", w_ao_v), ("gb0", cols(w_in_v, 7)), ("co", w_co_v),
             ("ga1", cols(w_in_v, 6)), ("gb1", cols(w_in_v, 8)),
             ("wo0", cols(w_o_v, 0)), ("wo1", cols(w_o_v, 1)), ("ple", w_ple_v)]
    at = {name: i for i, (name, _) in enumerate(dense)}
    uses = [len([i for i in range(len(dense)) if i % SLOTS == s]) for s in range(SLOTS)]

    with ExitStack() as ctx:
        def sb(name, shape, dt=F32):
            return ctx.enter_context(nc.sbuf_tensor(name, shape, dt))

        def sem(name):
            return ctx.enter_context(nc.semaphore(name))

        ps = ctx.enter_context(nc.psum_tensor("ps", [P, 8, BANK], F32))

        ring = sb("ring", [P, SLOTS, 4096])
        X = sb("X", [P, TB * D])
        UT = sb("UT", [P, KD * S])
        R1 = sb("R1", [P, 4096])
        R2 = sb("R2", [P, 2048 + CT * ZW + 2048])
        R4 = sb("R4", [P, 5120])
        gB = [sb("gB0", [P, D]), sb("gB1", [P, D])]

        x_sb = X[:, :].rearrange("p (t d) -> p t d", t=TB)
        o_tok = X[:, 0:2048].rearrange("p (t d) -> p t d", t=TB)
        o_T = X[:, 2048:4096].rearrange("p (h s) -> p h s", h=H)
        uT = UT[:, :].rearrange("p (k s) -> p k s", k=KD)
        qT = R1[:, 0:2048].rearrange("p (h s) -> p h s", h=H)
        kT = R1[:, 2048:4096].rearrange("p (h s) -> p h s", h=H)
        vecs = R1[0:TAPS + 3, 0:512]
        bgu = R1[:, 512:1024].rearrange("p (a n) -> p a n", a=2)
        lamb = R1[:, 1024:1280].rearrange("p (a n) -> p a n", a=4)
        lprod = R1[:, 1280:1408].rearrange("p (a n) -> p a n", a=2)
        mT = R1[:, :].rearrange("p (k s) -> p k s", k=KD)
        pple = R1[:, :].rearrange("p (t d) -> p t d", t=TB)
        v_sb = R2[:, 0:2048].rearrange("p (t n) -> p t n", t=TB)
        z = R2[:, 2048:2048 + CT * ZW].rearrange("p (t s) -> p t s", t=CT)
        C0 = 2048 + CT * ZW
        conv = R2[:, C0:C0 + 2048].rearrange("p (t s) -> p t s", t=CT)
        u_tok = R2[:, 0:4096].rearrange("p (t d) -> p t d", t=TB)
        ex = R4[:, 0:2048].rearrange("p (b c k) -> p b c k", b=2, c=2)
        a_T = R4[:, 2048:3072].rearrange("p (b s) -> p b s", b=2)
        sg = R4[:, 3072:5120].rearrange("p (t s) -> p t s", t=4)
        junk = R4[:, 0:D]
        xg = R4[0:BT, 0:1024]
        b_dn = R4[0:E, 0:1024]
        y_sb = R4[0:BT, 1024:2048]
        xT = R4[:, 2048:3072].rearrange("p (k n) -> p k n", k=KD)
        hT = R4[:, 3072:4096].rearrange("p (k n) -> p k n", k=FT)
        gl_b = R4[:, 4096:5120].rearrange("p (b t g n) -> p b t g n", b=2, t=2, g=2)
        gate_b, lin_b, sig_b, lg_b = (R2[:, 4096 + 512 * i:4608 + 512 * i].rearrange("p (b t n) -> p b t n", b=2, t=2)
                                      for i in range(4))
        q0 = C0

        def rt(n):
            nonlocal q0
            q0 += n
            return R2[:, q0 - n:q0]

        lg = rt(TB * E).rearrange("p (t e) -> p t e", t=TB)
        eq = rt(TB * TOP * E).rearrange("p (t k e) -> p t k e", t=TB, k=TOP)
        eqs = rt(TB * TOP * E).rearrange("p (t k e) -> p t k e", t=TB, k=TOP)
        mask = rt(TB * E).rearrange("p (t e) -> p t e", t=TB)
        slot = rt(TB * E).rearrange("p (t e) -> p t e", t=TB)
        big = rt((TB - 1) * E).rearrange("p (a e) -> p a e", a=TB - 1)
        assert q0 <= C0 + 2048
        oh_j = UT[:, 0:16 * BT].rearrange("p (t k j) -> p t k j", t=TB, k=TOP)
        oh_r = R2[:, 0:16 * 3 * MAXB].rearrange("p (t k a b) -> p t k a b", t=TB, k=TOP, a=3)

        ident = sb("ident", [P, P])
        ones = sb("ones", [P, P])
        before = sb("before", [P, P])
        cmask = sb("cmask", [P, P])
        iota = sb("iota", [P, BT])
        tokid = sb("tokid", [P, TB])
        spare = sb("spare", [BT, 1])
        gsub = sb("gsub", [P, HD])
        cvec = sb("cvec", [P, CT, TAPS + 3])
        bias = sb("bias", [P, E, FT, 2])
        bias_e = sb("bias_e", [P, FT, 2])
        b_rt = sb("b_rt", [P, E])
        w_rt = sb("w_rt", [P, KD, E])
        ss = sb("ss", [P, TB])
        rs = sb("rs", [P, TB])
        rr = sb("rr", [P, TB])
        oss = sb("oss", [P, TB, H])
        ors = sb("ors", [P, TB, H])
        orr = sb("orr", [P, TB, H])
        epsc = sb("epsc", [P, 2])
        lam2 = sb("lam2", [P, 2])
        lame = sb("lame", [P, 2])
        nlam = sb("nlam", [P, 2])
        mx = sb("mx", [P, 2, 2])
        nmx = sb("nmx", [P, 2, 2])
        den = sb("den", [P, 2, 2])
        rden = sb("rden", [P, 2, 2])
        nrl = sb("nrl", [P, 2])
        top = sb("top", [P, TB, 8])
        topi = sb("topi", [P, TB, 8], U32)
        topf = sb("topf", [P, TB, TOP])
        gd = sb("gd", [P, TB, TOP])
        ge = sb("ge", [P, TB, TOP])
        gs = sb("gs", [P, TB])
        gr = sb("gr", [P, TB])
        gate = sb("gate", [P, TB, TOP])
        gdense = sb("gdense", [P, TB, E])
        gdT = R4[0:E, 2048:2560]
        nblk = sb("nblk", [P, E])
        cum = sb("cum", [P, E])
        startf = sb("startf", [P, E + 1])
        starti = sb("starti", [P, E + 1], I32)
        slk = sb("slk", [P, TB * TOP])
        sli = sb("sli", [P, TB * TOP], I32)
        slj = sb("slj", [P, 2, TB * TOP], I32)
        slf = sb("slf", [P, 2, TB * TOP])
        tabf = R4[0:BT, 2560:2560 + 2 * MAXB].rearrange("p (a b) -> p a b", a=2)
        inval = R4[0:BT, 2688:2688 + MAXB]
        gate_tab = sb("gate_tab", [BT, MAXB])
        from_tab = sb("from_tab", [BT, MAXB], I32)
        to_tab = sb("to_tab", [BT, MAXB], I32)
        from_c = sb("from_c", [BT, 1], I32)
        to_c = sb("to_c", [BT, 1], I32)
        gate_c = sb("gate_c", [BT, 1])

        x_in = sem("x_in")
        small_in = sem("small_in")
        gains_in = [sem("gain0_in"), sem("gain1_in")]
        p_in = sem("p_in")
        bdn_in = sem("bdn_in")
        ring_in = [sem(f"ring_in{s}") for s in range(SLOTS)]
        consts = sem("consts")
        zpad0 = sem("zpad0")
        dve_step = sem("dve_step")
        act_step = sem("act_step")
        pool_step = sem("pool_step")
        squares = sem("squares")
        roots = sem("roots")
        normed = sem("normed")
        turned = sem("turned")
        turned_out = sem("turned_out")
        setup_tr = sem("setup_tr")
        setup_out = sem("setup_out")
        proj = sem("proj")
        proj_out = sem("proj_out")
        z_ready = sem("z_ready")
        conv_tap = sem("conv_tap")
        conv_mean = sem("conv_mean")
        conv_c = sem("conv_c")
        conv_sq = sem("conv_sq")
        conv_var = sem("conv_var")
        conv_sd = sem("conv_sd")
        conv_n = sem("conv_n")
        conv_ready = sem("conv_ready")
        conv_out = sem("conv_out")
        lam_dot = sem("lam_dot")
        lam_exp = sem("lam_exp")
        scores = sem("scores")
        maxed = sem("maxed")
        exped = sem("exped")
        mixed = sem("mixed")
        a_turned = sem("a_turned")
        a_out = sem("a_out")
        pv = sem("pv")
        o_sq = sem("o_sq")
        o_cp = sem("o_cp")
        o_root = sem("o_root")
        o_normed = sem("o_normed")
        o_turned = sem("o_turned")
        o_out = sem("o_out")
        gates = sem("gates")
        gates_sig = sem("gates_sig")
        branch = sem("branch")
        m_ready = sem("m_ready")
        wo_done = sem("wo_done")
        h1_half = sem("h1_half")
        x_again = sem("x_again")
        logits = sem("logits")
        top_ready = sem("top_ready")
        gexp = sem("gexp")
        mask_ready = sem("mask_ready")
        counts = sem("counts")
        onehots = sem("onehots")
        table = sem("table")
        tables = sem("tables")
        gd_ready = sem("gd_ready")
        gd_turned = sem("gd_turned")
        gdT_out = sem("gdT_out")
        bdn = sem("bdn")
        base_ready = sem("base_ready")
        ptr = sem("ptr")
        pT_out = sem("pT_out")
        ple_mm = sem("ple_mm")
        ple_out = sem("ple_out")
        u_stored = sem("u_stored")
        sum_stored = sem("sum_stored")
        gathered = sem("gathered")
        scattered = sem("scattered")
        cols_ready = sem("cols_ready")
        x_turned = sem("x_turned")
        xT_ready = sem("xT_ready")
        gu_done = sem("gu_done")
        gu_read = sem("gu_read")
        gate_ready = sem("gate_ready")
        sig_ready = sem("sig_ready")
        h_ready = sem("h_ready")
        dve_block = sem("dve_block")
        down_done = sem("down_done")
        y_read = sem("y_read")
        y_ready = sem("y_ready")
        y_free = sem("y_free")
        passed = {"pe": sem("pe_passed"), "pool": sem("pool_passed")}
        h2_in = sem("h2_in")
        pg = sem("pg")
        pg_sig = sem("pg_sig")
        h3_half = sem("h3_half")
        out_ready = sem("out_ready")
        out_stored = sem("out_stored")

        SMALL = 12 * 16
        multiplied = {"conv_a": (proj, 4), "conv_g": (proj, 8), "q": (proj, 12), "k": (proj, 16), "v": (proj, 20),
                      "ga0": (gates, 4), "gb0": (gates, 4), "ga1": (gates, 8), "gb1": (gates, 8),
                      "ao": (branch, 8), "co": (branch, 8), "wo0": (wo_done, 7), "wo1": (wo_done, 8),
                      "ple": (ple_mm, 8)}

        block = ctx.enter_context(nc.Block())

        def slot_of(name):
            return ring[:, at[name] % SLOTS, :]

        def flat(dst, k):
            return dst.rearrange("p (k n) -> p k n", k=k)

        ple_slot = slot_of("ple")
        w_ple_sb = flat(ple_slot[:, 0:2048], PLE // P)
        p_sb = ple_slot[:, 2048:3072].rearrange("p (t d) -> p t d", t=TB)
        pT = ple_slot[:, 3072:4096].rearrange("p (k s) -> p k s", k=PLE // P)

        GUC, DNC = 4, 2
        w_gu_v = w_gate_up.rearrange("l e (k q) n -> q (l e) k n", q=P)
        w_dn_v = w_down.rearrange("l e (k q) n -> q (l e) k n", q=P)

        def expert_chunk(e, c):
            if c < GUC:
                return w_gu_v[:, bass.ds(e, 1), :, c * 512:(c + 1) * 512].rearrange("q e k n -> q (e k) n")
            c -= GUC
            return w_dn_v[:, bass.ds(e, 1), c * 4:(c + 1) * 4, :].rearrange("q e k n -> q (e k) n")

        def chunk_slot(c):
            return flat(ring[:, c, :], 8 if c < GUC else 4)

        @block.sync
        def _(sp):
            sp.dma_start(x_sb, x_t).then_inc(x_in, 16)
            for i, (name, src) in enumerate(dense):
                if i >= SLOTS:
                    sp.wait_ge(*multiplied[dense[i - SLOTS][0]])
                k = src.shape[1]
                n = k * src.shape[2]
                sp.dma_start(flat(slot_of(name)[:, 0:n], k), src).then_inc(ring_in[i % SLOTS], 16)
                if name == "wo1":
                    sp.wait_ge(branch, KD)
                    sp.dma_start(x_sb, x_t).then_inc(x_again, 16)
                if name == "ple":
                    sp.dma_start(p_sb, p_t).then_inc(p_in, 16)
            for c in range(SLOTS):
                lies = max(i for i in range(len(dense)) if i % SLOTS == c)
                sp.wait_ge(*multiplied[dense[lies][0]])
                sp.dma_start(chunk_slot(c), expert_chunk(0, c)).then_inc(ring_in[c], 16)
            sp.wait_ge(tables, 1)
            with sp.Fori(1, E) as e:
                first = sp.value_load(starti[0:1, bass.ds(e, 1)], min_val=1, max_val=MAXB - 1)
                for c in range(SLOTS):
                    if c < GUC:
                        sp.wait_ge(gu_done, first * GUC + (c + 1))
                    else:
                        sp.wait_ge(down_done, first * DNC + (c + 1 - GUC))
                    sp.dma_start(chunk_slot(c), expert_chunk(e, c)).then_inc(ring_in[c], 16)
            total = sp.value_load(starti[0:1, E:E + 1], min_val=1, max_val=MAXB - 1)
            for c in range(2):
                sp.wait_ge(gu_done, total * GUC + (c + 1))
                sp.dma_start(flat(ring[:, c, :], KD), cols(w_pg_v, c)).then_inc(ring_in[c], 16)
            sp.wait_ge(y_free, total + 1)
            sp.dma_start(x_sb, sum_rows[0:S, :].rearrange("(t q) d -> q t d", q=P)).then_inc(h2_in, 16)
            for t in range(TB):
                sp.wait_ge(out_ready, t + 1)
                sp.dma_start(out_t[:, t, :], u_tok[:, t, :]).then_inc(out_stored, 16)
            sp.wait_ge(out_stored, 16 * TB)

        @block.gpsimd
        def _(pool):
            n = 0

            def link(ins):
                nonlocal n
                n += 1
                ins.then_inc(pool_step, 1)
                pool.wait_ge(pool_step, n)

            nc.gpsimd.memset(ones[:, :], 1.0).then_inc(consts, 1)
            link(nc.gpsimd.memset(ident[:, :], 0.0))
            link(nc.gpsimd.memset(before[:, :], 1.0))
            link(nc.gpsimd.memset(cmask[:, :], 0.0))
            nc.gpsimd.affine_select(out=ident[:, :], in_=ident[:, :], compare_op=ALU.not_equal, fill=1.0,
                                    base=0, pattern=[[-1, P]], channel_multiplier=1).then_inc(consts, 1)
            nc.gpsimd.affine_select(out=before[:, :], in_=before[:, :], compare_op=ALU.is_gt, fill=0.0,
                                    base=0, pattern=[[1, P]], channel_multiplier=-1).then_inc(consts, 1)
            nc.gpsimd.affine_select(out=cmask[:, :], in_=cmask[:, :], compare_op=ALU.is_ge, fill=NEG,
                                    base=0, pattern=[[-1, P]], channel_multiplier=1).then_inc(consts, 1)
            nc.gpsimd.iota(iota[:, :], pattern=[[1, BT]], base=0, channel_multiplier=0,
                           allow_small_or_imprecise_dtypes=True).then_inc(consts, 1)
            nc.gpsimd.iota(tokid[:, :], pattern=[[P, TB]], base=0, channel_multiplier=1,
                           allow_small_or_imprecise_dtypes=True).then_inc(consts, 1)
            nc.gpsimd.iota(spare[:, :], pattern=[[0, 1]], base=S, channel_multiplier=1,
                           allow_small_or_imprecise_dtypes=True).then_inc(consts, 1)
            nc.gpsimd.memset(epsc[:, 0:1], EPS).then_inc(consts, 1)
            nc.gpsimd.memset(epsc[:, 1:2], EPS / (1.0 - LAM_INIT) ** 2).then_inc(consts, 1)
            nc.gpsimd.memset(z[:, :, 0:PAD], 0.0).then_inc(zpad0, 1)

            pool.wait_ge(normed, 2 * TB)
            nc.gpsimd.dma_start(u_rows.rearrange("(t q) d -> q t d", q=P), u_tok).then_inc(u_stored, 16)
            link(nc.gpsimd.memset(y_sb, 0.0))
            nc.gpsimd.dma_start(sum_rows[S:S + BT, :], y_sb).then_inc(sum_stored, 16)
            pool.wait_ge(sum_stored, 16)
            pool.wait_ge(base_ready, 2 * TB)
            nc.gpsimd.dma_start(sum_rows[0:S, :].rearrange("(t q) d -> q t d", q=P), x_sb)\
                .then_inc(sum_stored, 16)
            pool.wait_ge(u_stored, 16)
            pool.wait_ge(tables, 1)
            total = pool.value_load(starti[0:1, E:E + 1], min_val=1, max_val=MAXB - 1)
            link(nc.gpsimd.tensor_copy(from_c[:, :], from_tab[:, 0:1]))
            nc.gpsimd.indirect_dma_start(out=xg, out_offset=None, in_=u_rows[:, :],
                                         in_offset=bass.IndirectOffsetOnAxis(ap=from_c[:, 0:1], axis=0))\
                .then_inc(gathered, 16)
            pool.wait_ge(sum_stored, 32)
            nc.gpsimd.sem_inc(y_free, 1)
            with pool.Fori(0, total) as b:
                pool.wait_ge(gathered, (b + 1) * 16)
                pool.wait_ge(x_turned, b + 1)
                nc.gpsimd.tensor_copy(from_c[:, :], from_tab[:, bass.ds(b + 1, 1)]).then_inc(cols_ready, 1)
                pool.wait_ge(cols_ready, b * 3 + 1)
                nc.gpsimd.sem_inc(passed["pool"], 1)
                nc.gpsimd.indirect_dma_start(out=xg, out_offset=None, in_=u_rows[:, :],
                                             in_offset=bass.IndirectOffsetOnAxis(ap=from_c[:, 0:1], axis=0))\
                    .then_inc(gathered, 16)
                nc.gpsimd.tensor_copy(to_c[:, :], to_tab[:, bass.ds(b, 1)]).then_inc(cols_ready, 1)
                nc.gpsimd.tensor_copy(gate_c[:, :], gate_tab[:, bass.ds(b, 1)]).then_inc(cols_ready, 1)
                pool.wait_ge(cols_ready, b * 3 + 3)
                pool.wait_ge(y_ready, (b + 1) * 2)
                nc.gpsimd.sem_inc(passed["pool"], 1)
                nc.gpsimd.indirect_dma_start(out=sum_rows[:, :],
                                             out_offset=bass.IndirectOffsetOnAxis(ap=to_c[:, 0:1], axis=0),
                                             in_=y_sb, in_offset=None, compute_op=ALU.add)\
                    .then_inc(scattered, 16)
                pool.wait_ge(scattered, (b + 1) * 16)
                nc.gpsimd.sem_inc(y_free, 1)
            pool.wait_ge(gathered, (total + 1) * 16)

        @block.scalar
        def _(act):
            n = 0

            def link(ins):
                nonlocal n
                n += 1
                ins.then_inc(act_step, 1)
                act.wait_ge(act_step, n)

            def row(v):
                return v.rearrange("(a n) -> a n", a=1) if len(v.shape) == 1 else v

            def load(dst, src):
                act.dma_start(dst, src).then_inc(small_in, 16)

            act.dma_start(gB[0][:, :], g_mix.to_broadcast([P, D])).then_inc(gains_in[0], 16)
            act.dma_start(gB[1][:, :], g_ffn.to_broadcast([P, D])).then_inc(gains_in[1], 16)
            load(R1[0:TAPS, 0:512], w_dw.rearrange("l j c -> (l j) c"))
            load(R1[TAPS:TAPS + 1, 0:512], b_dw)
            load(R1[TAPS + 1:TAPS + 2, 0:512], g_conv_ln)
            load(R1[TAPS + 2:TAPS + 3, 0:512], b_conv_ln)
            load(bgu, b_gate_up.rearrange("l e (i n) -> (l e i) n", i=FT).rearrange("(a r) n -> r a n", a=2))
            for j, v in enumerate((lambda_q1, lambda_k1, lambda_q2, lambda_k2)):
                load(lamb[:, j, :], v.to_broadcast([P, QD]))
            load(gsub[:, :], g_subln.to_broadcast([P, HD]))
            load(b_rt[:, :], b_router.to_broadcast([P, E]))
            load(w_rt[:, :, :], w_router.rearrange("l (k q) e -> q (l k) e", q=P))

            act.wait_ge(consts, 9)

            act.wait_ge(x_in, 16)
            for t in range(TB):
                link(nc.scalar.activation(junk, x_sb[:, t, :], ACT.Square, accum_out=ss[:, t:t + 1]))
            nc.scalar.activation(rs[:, :], ss[:, :], ACT.Sqrt, bias=epsc[:, 0:1], scale=1.0 / D)\
                .then_inc(roots, 1)
            for t in range(TB):
                for h in range(2):
                    act.wait_ge(turned, 2 * t + h + 1)
                    nc.scalar.activation(uT[:, 4 * h:4 * h + 4, t * P:(t + 1) * P],
                                         ps[:, 4 + (2 * t + h) % 4, :].rearrange("p (k s) -> p k s", k=4),
                                         ACT.Copy).then_inc(turned_out, 1)
            act.wait_ge(zpad0, 1)
            for i in range(20):
                j, t = i // 4, i % 4
                act.wait_ge(proj, i + 1)
                src = ps[:, i % 4, :]
                if j == 0:
                    ins = nc.scalar.activation(z[:, t, PAD:PAD + S], src, ACT.Copy)
                elif j == 1:
                    ins = nc.scalar.activation(sg[:, t, :], src, ACT.Sigmoid)
                elif j == 2:
                    if t == 0:
                        act.wait_ge(setup_out, 2)
                        act.wait_ge(lam_dot, 1)
                    ins = nc.scalar.activation(qT[:, t, :], src, ACT.Copy, scale=SCALE)
                elif j == 3:
                    ins = nc.scalar.activation(kT[:, t, :], src, ACT.Copy)
                else:
                    ins = nc.scalar.activation(v_sb[:, t, :], src, ACT.Copy)
                ins.then_inc(proj_out, 1)
            nc.scalar.activation(lame[:, :], lam2[:, :], ACT.Exp).then_inc(lam_exp, 1)

            def exps(i):
                w = (i % TB + 1) * P
                act.wait_ge(maxed, i + 1)
                if i >= 2:
                    act.wait_ge(a_turned, i - 1)
                for c in range(2):
                    nc.scalar.activation(ex[:, i % 2, c, 0:w], ps[:, 4 + 2 * (i % 2) + c, 0:w], ACT.Exp,
                                         bias=nmx[:, i % 2, c:c + 1],
                                         accum_out=den[:, i % 2, c:c + 1]).then_inc(exped, 1)

            def turned_a(i):
                w = (i % TB + 1) * P
                act.wait_ge(a_turned, i + 1)
                if i >= 2:
                    act.wait_ge(pv, i - 1)
                nc.scalar.activation(a_T[:, i % 2, 0:w], ps[:, i % 2, 0:w], ACT.Copy).then_inc(a_out, 1)

            def results(i):
                h, t = i // TB, i % TB
                act.wait_ge(pv, i + 1)
                nc.scalar.activation(o_tok[:, t, h * HD:(h + 1) * HD], ps[:, 2, (i % 4) * P:(i % 4 + 1) * P],
                                     ACT.Copy).then_inc(o_cp, 1)
                act.wait_ge(o_cp, i + 1)
                nc.scalar.activation(ps[:, 2, (i % 4) * P:(i % 4 + 1) * P],
                                     o_tok[:, t, h * HD:(h + 1) * HD],
                                     ACT.Square, accum_out=oss[:, t, h:h + 1]).then_inc(o_sq, 1)

            NI = H * TB
            for i in range(NI + 2):
                if i < NI:
                    exps(i)
                if 1 <= i <= NI:
                    turned_a(i - 1)
                if i >= 2:
                    results(i - 2)
            act.wait_ge(conv_c, CT)
            for t in range(CT):
                nc.scalar.activation(sg[:, t, :], conv[:, t, :], ACT.Square).then_inc(conv_sq, 1)
            act.wait_ge(conv_var, 1)
            nc.scalar.activation(ex[:, 0, 0, :], ps[:, 3, :], ACT.Sqrt, bias=epsc[:, 0:1], scale=1.0 / CW)\
                .then_inc(conv_sd, 1)
            act.wait_ge(o_sq, NI)
            nc.scalar.activation(ors[:, :, :], oss[:, :, :], ACT.Sqrt, bias=epsc[:, 1:2],
                                 scale=1.0 / (HD * (1.0 - LAM_INIT) ** 2)).then_inc(o_root, 1)
            for t in range(CT):
                act.wait_ge(conv_n, t + 1)
                nc.scalar.activation(sg[:, t, :], conv[:, t, :], ACT.Sigmoid,
                                     bias=cvec[:, t, TAPS + 2:TAPS + 3],
                                     scale=cvec[:, t, TAPS + 1:TAPS + 2]).then_inc(conv_ready, 1)
            for h in range(H):
                act.wait_ge(o_turned, h + 1)
                nc.scalar.activation(o_T[:, h, :], ps[:, h, :], ACT.Copy).then_inc(o_out, 1)
            for k in range(KD):
                b = 4 * ((k + 1) % 2)
                act.wait_ge(gates, k + 1)
                if k >= 2:
                    act.wait_ge(m_ready, k - 1)
                for c in range(2):
                    nc.scalar.activation(ex[:, k % 2, c, :], ps[:, b + c, :], ACT.Sigmoid)\
                        .then_inc(gates_sig, 1)
            act.wait_ge(m_ready, KD)
            for t in range(TB):
                act.wait_ge(h1_half, 2 * t + 2)
                link(nc.scalar.activation(junk, x_sb[:, t, :], ACT.Square, accum_out=ss[:, t:t + 1]))
                nc.scalar.activation(rs[:, t:t + 1], ss[:, t:t + 1], ACT.Sqrt, bias=epsc[:, 0:1],
                                     scale=1.0 / D).then_inc(roots, 1)
                for h in range(2):
                    act.wait_ge(turned, 8 + 2 * t + h + 1)
                    nc.scalar.activation(uT[:, 4 * h:4 * h + 4, t * P:(t + 1) * P],
                                         ps[:, 4 + (2 * t + h) % 4, :].rearrange("p (k s) -> p k s", k=4),
                                         ACT.Copy).then_inc(turned_out, 1)
            act.dma_start(gB[0][:, :], g_ple.to_broadcast([P, D])).then_inc(gains_in[0], 16)
            act.wait_ge(normed, 2 * TB)
            act.dma_start(gB[1][:, :], row(g_final).to_broadcast([P, D])).then_inc(gains_in[1], 16)
            act.dma_start(b_dn, b_down.rearrange("l e d -> (l e) d")).then_inc(bdn_in, 16)
            act.wait_ge(top_ready, 1)
            nc.scalar.activation(ge[:, :, :], gd[:, :, :], ACT.Exp).then_inc(gexp, 1)
            for k in range(PLE // P):
                act.wait_ge(ptr, k + 1)
                nc.scalar.activation(pT[:, k, :], ps[:, 2 + k, :], ACT.Copy).then_inc(pT_out, 1)
            for i in range(2 * TB):
                act.wait_ge(ple_mm, i + 1)
                nc.scalar.activation(pple[:, i // 2, (i % 2) * 512:(i % 2 + 1) * 512], ps[:, 4 + i % 2, :],
                                     ACT.Copy).then_inc(ple_out, 1)
            act.wait_ge(gd_turned, 1)
            nc.scalar.activation(gdT, ps[0:E, 6, :], ACT.Copy).then_inc(gdT_out, 1)
            act.wait_ge(tables, 1)
            total = act.value_load(starti[0:1, E:E + 1], min_val=1, max_val=MAXB - 1)
            with act.Fori(0, total) as b:
                act.wait_ge(x_turned, b + 1)
                nc.scalar.activation(xT, ps[:, 4:6, :].rearrange("p a (k n) -> p (a k) n", n=BT), ACT.Copy)\
                    .then_inc(xT_ready, 1)
                for c in range(GUC):
                    act.wait_ge(gate_ready, b * GUC + c + 1)
                    nc.scalar.activation(sig_b[:, c % 2], gate_b[:, c % 2], ACT.Sigmoid, scale=ALPHA)\
                        .then_inc(sig_ready, 1)
                act.wait_ge(cols_ready, b * 3 + 3)
                act.wait_ge(y_free, b + 1)
                act.wait_ge(down_done, b * DNC + 2 * DNC)
                for h in range(2):
                    nc.scalar.activation(y_sb[:, h * 512:(h + 1) * 512], ps[0:BT, 6 + h, :], ACT.Copy,
                                         scale=gate_c[:, 0:1]).then_inc(y_ready, 1)
                act.wait_ge(y_ready, b * 2 + 2)
                nc.scalar.sem_inc(y_read, 2)
            act.wait_ge(h2_in, 16)
            act.wait_ge(x_turned, total + 1)
            for t in range(TB):
                link(nc.scalar.activation(junk, x_sb[:, t, :], ACT.Square, accum_out=ss[:, t:t + 1]))
            nc.scalar.activation(rs[:, :], ss[:, :], ACT.Sqrt, bias=epsc[:, 0:1], scale=1.0 / D)\
                .then_inc(roots, 1)
            for t in range(TB):
                for h in range(2):
                    act.wait_ge(turned, 16 + 2 * t + h + 1)
                    nc.scalar.activation(uT[:, 4 * h:4 * h + 4, t * P:(t + 1) * P],
                                         ps[:, 4 + (2 * t + h) % 4, :].rearrange("p (k s) -> p k s", k=4),
                                         ACT.Copy).then_inc(turned_out, 1)
            for i in range(2 * TB):
                act.wait_ge(pg, i + 1)
                if i >= 4:
                    act.wait_ge(h3_half, i - 3)
                nc.scalar.activation(sg[:, i % 4, :], ps[:, i % 4, :], ACT.Sigmoid).then_inc(pg_sig, 1)
            for t in range(TB):
                act.wait_ge(h3_half, 2 * t + 2)
                link(nc.scalar.activation(junk, x_sb[:, t, :], ACT.Square, accum_out=ss[:, t:t + 1]))
                nc.scalar.activation(rs[:, t:t + 1], ss[:, t:t + 1], ACT.Sqrt, bias=epsc[:, 0:1],
                                     scale=1.0 / D).then_inc(roots, 1)

        @block.vector
        def _(dve):
            n = 0

            def link(ins):
                nonlocal n
                n += 1
                ins.then_inc(dve_step, 1)
                dve.wait_ge(dve_step, n)

            def norm(src, dst, g):
                for t in range(TB):
                    nc.vector.scalar_tensor_tensor(dst[:, t, :], src[:, t, :], rr[:, t:t + 1], g[:, :],
                                                   ALU.mult, ALU.mult).then_inc(normed, 1)

            dve.wait_ge(roots, 1)
            dve.wait_ge(gains_in[0], 16)
            link(nc.vector.reciprocal(rr[:, :], rs[:, :]))
            norm(x_sb, x_sb, gB[0])
            dve.wait_ge(setup_tr, 1)
            nc.vector.tensor_copy(cvec[:, :, :], ps[:, 0, 0:CT * (TAPS + 3)].rearrange("p (t j) -> p t j", t=CT))\
                .then_inc(setup_out, 1)
            nc.vector.tensor_copy(bias[:, :, :, :].rearrange("p (a e) i g -> p a g (e i)", a=2),
                                  ps[:, 1, :].rearrange("p (a g r) -> p a g r", a=2, g=2)).then_inc(setup_out, 1)
            dve.wait_ge(small_in, SMALL)
            link(nc.vector.tensor_tensor(lprod, lamb[:, 0:4:2, :], lamb[:, 1:4:2, :], ALU.mult))
            nc.vector.tensor_reduce(lam2[:, :], lprod, AX_X, ALU.add).then_inc(lam_dot, 1)
            for t in range(CT):
                dve.wait_ge(proj_out, CT + t + 1)
                nc.vector.tensor_tensor(z[:, t, PAD:PAD + S], z[:, t, PAD:PAD + S], sg[:, t, :], ALU.mult)\
                    .then_inc(z_ready, 1)
            dve.wait_ge(setup_out, 2)
            for t in range(CT):
                dve.wait_ge(z_ready, t + 1)
                nc.vector.tensor_scalar(conv[:, t, :], z[:, t, 0:S], cvec[:, t, 0:1],
                                        cvec[:, t, TAPS:TAPS + 1], ALU.mult, ALU.add).then_inc(conv_tap, 1)
            with dve.Fori(1, TAPS) as j:
                for t in range(CT):
                    dve.wait_ge(conv_tap, j * CT + (t + 1 - CT))
                    nc.vector.scalar_tensor_tensor(conv[:, t, :], z[:, t, bass.ds(j, S)],
                                                   cvec[:, t, bass.ds(j, 1)], conv[:, t, :],
                                                   ALU.mult, ALU.add).then_inc(conv_tap, 1)
            dve.wait_ge(conv_tap, TAPS * CT)
            dve.wait_ge(lam_exp, 1)
            link(nc.vector.tensor_tensor(nlam[:, 0:1], lame[:, 1:2], lame[:, 0:1], ALU.subtract))
            link(nc.vector.tensor_scalar(nlam[:, 1:2], nlam[:, 0:1], -LAM_INIT, None, ALU.add))

            def maxes(i):
                w = (i % TB + 1) * P
                s2 = ps[:, 4 + 2 * (i % 2):6 + 2 * (i % 2), :]
                dve.wait_ge(scores, i + 1)
                link(nc.vector.tensor_tensor(s2[:, :, w - P:w], s2[:, :, w - P:w],
                                             cmask[:, :].unsqueeze(1).to_broadcast([P, 2, P]), ALU.add))
                if i >= 2:
                    dve.wait_ge(exped, 2 * (i - 1))
                link(nc.vector.tensor_reduce(mx[:, i % 2, :], s2[:, :, 0:w], AX_X, ALU.max))
                nc.vector.tensor_scalar(nmx[:, i % 2, :], mx[:, i % 2, :], -1.0, None, ALU.mult)\
                    .then_inc(maxed, 1)

            def mix(i):
                w = (i % TB + 1) * P
                b = i % 2
                dve.wait_ge(exped, 2 * i + 2)
                link(nc.vector.reciprocal(rden[:, b, :], den[:, b, :]))
                link(nc.vector.tensor_tensor(nrl[:, b:b + 1], rden[:, b, 1:2], nlam[:, 1:2], ALU.mult))
                link(nc.vector.tensor_scalar(ex[:, b, 0, 0:w], ex[:, b, 0, 0:w], rden[:, b, 0:1], None, ALU.mult))
                nc.vector.scalar_tensor_tensor(ex[:, b, 0, 0:w], ex[:, b, 1, 0:w], nrl[:, b:b + 1],
                                               ex[:, b, 0, 0:w], ALU.mult, ALU.add).then_inc(mixed, 1)

            NI = H * TB
            for i in range(NI + 1):
                if i < NI:
                    maxes(i)
                if i >= 1:
                    mix(i - 1)
                if i == 2:
                    dve.wait_ge(conv_mean, 1)
                    link(nc.vector.tensor_scalar(R2[:, 2048:2048 + S], ps[:, 3, :], 1.0 / CW, None, ALU.mult))
                    for t in range(CT):
                        nc.vector.tensor_tensor(conv[:, t, :], conv[:, t, :], R2[:, 2048:2048 + S], ALU.subtract)\
                            .then_inc(conv_c, 1)
            dve.wait_ge(conv_sd, 1)
            link(nc.vector.reciprocal(ex[:, 0, 1, :], ex[:, 0, 0, :]))
            for t in range(CT):
                nc.vector.tensor_tensor(conv[:, t, :], conv[:, t, :], ex[:, 0, 1, :], ALU.mult).then_inc(conv_n, 1)
            dve.wait_ge(o_root, 1)
            link(nc.vector.reciprocal(orr[:, :, :], ors[:, :, :]))
            for h in range(H):
                for t in range(TB):
                    o = o_tok[:, t, h * HD:(h + 1) * HD]
                    nc.vector.scalar_tensor_tensor(o, o, orr[:, t, h:h + 1], gsub[:, :], ALU.mult, ALU.mult)\
                        .then_inc(o_normed, 1)
            for t in range(CT):
                dve.wait_ge(conv_ready, t + 1)
                link(nc.vector.tensor_scalar(conv[:, t, :], conv[:, t, :], cvec[:, t, TAPS + 1:TAPS + 2],
                                             cvec[:, t, TAPS + 2:TAPS + 3], ALU.mult, ALU.add))
                nc.vector.tensor_tensor(conv[:, t, :], conv[:, t, :], sg[:, t, :], ALU.mult).then_inc(conv_out, 1)
            for k in range(KD):
                b = 4 * ((k + 1) % 2)
                dve.wait_ge(gates_sig, 2 * k + 2)
                dve.wait_ge(branch, k + 1)
                link(nc.vector.tensor_tensor(mT[:, k, :], ex[:, k % 2, 0, :], ps[:, b + 2, :], ALU.mult))
                link(nc.vector.tensor_tensor(sg[:, k % 2, :], ex[:, k % 2, 1, :], ps[:, b + 3, :], ALU.mult))
                nc.vector.tensor_tensor(mT[:, k, :], mT[:, k, :], sg[:, k % 2, :], ALU.add).then_inc(m_ready, 1)
            dve.wait_ge(x_again, 16)
            dve.wait_ge(gains_in[1], 16)
            for t in range(TB):
                for h in range(2):
                    i = 2 * t + h
                    dve.wait_ge(wo_done, i + 1)
                    xs = x_sb[:, t, h * 512:(h + 1) * 512]
                    nc.vector.tensor_tensor(xs, xs, ps[:, i % 4, :], ALU.add).then_inc(h1_half, 1)
                dve.wait_ge(roots, 1 + t + 1)
                link(nc.vector.reciprocal(rr[:, t:t + 1], rs[:, t:t + 1]))
                nc.vector.scalar_tensor_tensor(u_tok[:, t, :], x_sb[:, t, :], rr[:, t:t + 1], gB[1][:, :],
                                               ALU.mult, ALU.mult).then_inc(normed, 1)
            dve.wait_ge(logits, 1)
            link(nc.vector.tensor_tensor(lg, ps[:, 0, 0:TB * E].rearrange("p (t e) -> p t e", t=TB),
                                         b_rt[:, :].unsqueeze(1).to_broadcast([P, TB, E]), ALU.add))
            for t in range(TB):
                link(nc.vector.max(top[:, t, :], lg[:, t, :]))
            nc.vector.tensor_tensor(gd[:, :, :], top[:, :, 0:TOP],
                                    top[:, :, 0:1].to_broadcast([P, TB, TOP]), ALU.subtract)\
                .then_inc(top_ready, 1)
            for t in range(TB):
                link(nc.vector.max_index(topi[:, t, :], top[:, t, :], lg[:, t, :]))
            link(nc.vector.tensor_copy(topf[:, :, :], topi[:, :, 0:TOP]))
            for t in range(TB):
                link(nc.vector.tensor_tensor(eq[:, t], iota[:, 0:E].unsqueeze(1).to_broadcast([P, TOP, E]),
                                             topf[:, t, :].unsqueeze(2).to_broadcast([P, TOP, E]),
                                             ALU.is_equal))
            nc.vector.tensor_reduce(mask, eq.rearrange("p t k e -> p t e k"), AX_X, ALU.add)\
                .then_inc(mask_ready, 1)
            dve.wait_ge(gexp, 1)
            link(nc.vector.tensor_reduce(gs[:, :], ge[:, :, :], AX_X, ALU.add))
            link(nc.vector.reciprocal(gr[:, :], gs[:, :]))
            link(nc.vector.tensor_tensor(gate[:, :, :], ge[:, :, :],
                                         gr[:, :].unsqueeze(2).to_broadcast([P, TB, TOP]), ALU.mult))
            for t in range(TB):
                link(nc.vector.tensor_tensor(eqs[:, t], eq[:, t],
                                             gate[:, t, :].unsqueeze(2).to_broadcast([P, TOP, E]), ALU.mult))
            nc.vector.tensor_reduce(gdense[:, :, :], eqs.rearrange("p t k e -> p t e k"), AX_X, ALU.add)\
                .then_inc(gd_ready, 1)
            dve.wait_ge(gd_ready, 1)
            dve.wait_ge(counts, 1)
            cnt = ps[:, 1, TB * E:(TB + 1) * E]
            for a in range(TB - 1):
                nc.vector.tensor_scalar(big[:, a, :], cnt, float(BT * (a + 1)), None, ALU.is_gt)\
                    .then_inc(dve_step, 1)
            n += TB - 1
            dve.wait_ge(dve_step, n)
            link(nc.vector.tensor_reduce(nblk[:, :], big.rearrange("p a e -> p e a"), AX_X, ALU.add))
            link(nc.vector.tensor_scalar(nblk[:, :], nblk[:, :], 1.0, None, ALU.add))
            link(nc.vector.memset(startf[:, 0:1], 0.0))
            link(nc.vector.tensor_tensor_scan(startf[:, 1:E + 1], ones[:, 0:E], nblk[:, :], 0.0, ALU.mult, ALU.add))
            link(nc.vector.tensor_copy(starti[:, :], startf[:, :]))
            for t in range(TB):
                link(nc.vector.scalar_tensor_tensor(slot[:, t, :], startf[:, 0:E], float(BT),
                                                    ps[:, 1, t * E:(t + 1) * E], ALU.mult, ALU.add))
            for t in range(TB):
                link(nc.vector.tensor_tensor(eqs[:, t], eq[:, t],
                                             slot[:, t, :].unsqueeze(1).to_broadcast([P, TOP, E]), ALU.mult))
            link(nc.vector.tensor_reduce(slk[:, :].rearrange("p (t k) -> p t k", t=TB), eqs, AX_X, ALU.add))
            link(nc.vector.tensor_copy(sli[:, :], slk[:, :]))
            link(nc.vector.tensor_scalar(slj[:, 0, :], sli[:, :], BT - 1, None, ALU.bitwise_and))
            link(nc.vector.tensor_scalar(slj[:, 1, :], sli[:, :], BT.bit_length() - 1, None, ALU.logical_shift_right))
            link(nc.vector.tensor_copy(slf[:, :, :], slj[:, :, :]))
            dve.wait_ge(u_stored, 16)
            nj = TB * TOP
            link(nc.vector.tensor_tensor(oh_j.rearrange("p t k j -> p (t k) j"),
                                         iota[:, :].unsqueeze(1).to_broadcast([P, nj, BT]),
                                         slf[:, 0, :].unsqueeze(2).to_broadcast([P, nj, BT]), ALU.is_equal))
            link(nc.vector.tensor_tensor(oh_r[:, :, :, 2, :].rearrange("p t k b -> p (t k) b"),
                                         iota[:, 0:MAXB].unsqueeze(1).to_broadcast([P, nj, MAXB]),
                                         slf[:, 1, :].unsqueeze(2).to_broadcast([P, nj, MAXB]), ALU.is_equal))
            link(nc.vector.tensor_tensor(oh_r[:, :, :, 1, :].rearrange("p t k b -> p (t k) b"),
                                         oh_r[:, :, :, 2, :].rearrange("p t k b -> p (t k) b"),
                                         gate[:, :, :].rearrange("p t k -> p (t k)").unsqueeze(2)
                                         .to_broadcast([P, nj, MAXB]), ALU.mult))
            for t in range(TB):
                nc.vector.tensor_scalar(oh_r[:, t, :, 0, :], oh_r[:, t, :, 2, :], tokid[:, t:t + 1], None, ALU.mult)\
                    .then_inc(onehots, 1)
            dve.wait_ge(table, 1)
            tab = ps[0:BT, 7, 0:3 * MAXB].rearrange("p (a b) -> p a b", a=3)
            link(nc.vector.tensor_copy(tabf[:, 0, :], tab[:, 0, :]))
            link(nc.vector.tensor_copy(gate_tab[:, :], tab[:, 1, :]))
            link(nc.vector.tensor_scalar(inval, tab[:, 2, :], -1.0, 1.0, ALU.mult, ALU.add))
            link(nc.vector.scalar_tensor_tensor(tabf[:, 1, :], inval, spare[:, 0:1], tabf[:, 0, :],
                                                ALU.mult, ALU.add))
            link(nc.vector.tensor_copy(from_tab[:, :], tabf[:, 0, :]))
            nc.vector.tensor_copy(to_tab[:, :], tabf[:, 1, :]).then_inc(tables, 1)
            for i in range(2 * TB):
                dve.wait_ge(bdn, i + 1)
                xs = x_sb[:, i // 2, (i % 2) * 512:(i % 2 + 1) * 512]
                nc.vector.tensor_tensor(xs, xs, ps[:, 2 + i % 2, :], ALU.add).then_inc(base_ready, 1)
            dve.wait_ge(tables, 1)
            nc.vector.sem_inc(gu_read, GUC)
            with dve.Fori(0, E) as e:
                first = dve.value_load(starti[0:1, bass.ds(e, 1)], min_val=0, max_val=MAXB - 1)
                last = dve.value_load(starti[0:1, bass.ds(e + 1, 1)], min_val=1, max_val=MAXB - 1)
                nc.vector.tensor_copy(bias_e[:, :, :], bias[:, bass.ds(e, 1), :, :]
                                      .rearrange("p a i g -> p (a i) g")).then_inc(setup_out, 1)
                with dve.Fori(first, last) as b:
                    for c in range(GUC):
                        o = c % 2
                        dve.wait_ge(gu_done, b * GUC + (c + 1 + GUC))
                        if c == 0:
                            dve.wait_ge(setup_out, e + 3)
                        g4 = ps[:, c, 0:4 * BT].rearrange("p (t g n) -> p t g n", t=2, g=2)
                        nc.vector.tensor_tensor(gl_b[:, o], g4,
                                                bias_e[:, 2 * c:2 * c + 2, :].unsqueeze(3)
                                                .to_broadcast([P, 2, 2, BT]), ALU.add).then_inc(gu_read, 1)
                        dve.wait_ge(gu_read, b * GUC + (c + 1 + GUC))
                        nc.vector.tensor_scalar(gate_b[:, o], gl_b[:, o, :, 0, :], LIMIT, None, ALU.min)\
                            .then_inc(gate_ready, 1)
                        nc.vector.tensor_scalar(lin_b[:, o], gl_b[:, o, :, 1, :], LIMIT, -LIMIT, ALU.min, ALU.max)\
                            .then_inc(dve_block, 1)
                        dve.wait_ge(gate_ready, b * GUC + c + 1)
                        dve.wait_ge(dve_block, b * (2 * GUC) + 2 * c + 1)
                        nc.vector.scalar_tensor_tensor(lg_b[:, o], lin_b[:, o], 1.0, gate_b[:, o],
                                                       ALU.add, ALU.mult).then_inc(dve_block, 1)
                        dve.wait_ge(dve_block, b * (2 * GUC) + 2 * c + 2)
                        dve.wait_ge(sig_ready, b * GUC + c + 1)
                        nc.vector.tensor_tensor(hT[:, 2 * c:2 * c + 2, :], lg_b[:, o], sig_b[:, o], ALU.mult)\
                            .then_inc(h_ready, 1)
            dve.wait_ge(roots, 1 + TB + 1)
            dve.wait_ge(gains_in[0], 32)
            link(nc.vector.reciprocal(rr[:, :], rs[:, :]))
            norm(x_sb, u_tok, gB[0])
            dve.wait_ge(gains_in[1], 32)
            for i in range(2 * TB):
                t = i // 2
                sl = slice((i % 2) * 512, (i % 2 + 1) * 512)
                dve.wait_ge(pg_sig, i + 1)
                link(nc.vector.tensor_tensor(sg[:, i % 4, :], sg[:, i % 4, :], pple[:, t, sl], ALU.mult))
                nc.vector.tensor_tensor(x_sb[:, t, sl], x_sb[:, t, sl], sg[:, i % 4, :], ALU.add)\
                    .then_inc(h3_half, 1)
            for t in range(TB):
                dve.wait_ge(roots, TB + 3 + t)
                dve.wait_ge(turned, 24)
                link(nc.vector.reciprocal(rr[:, t:t + 1], rs[:, t:t + 1]))
                nc.vector.scalar_tensor_tensor(u_tok[:, t, :], x_sb[:, t, :], rr[:, t:t + 1], gB[1][:, :],
                                               ALU.mult, ALU.mult).then_inc(out_ready, 1)

        @block.tensor
        def _(pe):
            def mm(o, a, b, start, stop, **kw):
                return nc.tensor.matmul(o, a, b, start=start, stop=stop, **kw)

            def arrived(name):
                i = at[name]
                pe.wait_ge(ring_in[i % SLOTS], 16 * (i // SLOTS + 1))

            def turn_rows(src, i):
                t, h = i // 2, i % 2
                for k in range(4):
                    last = nc.tensor.transpose(ps[:, 4 + i % 4, k * P:(k + 1) * P],
                                               src[:, t, (4 * h + k) * P:(4 * h + k + 1) * P], ident[:, :])
                last.then_inc(turned, 1)

            def weights(name, k):
                n = 8 if k == KD else k
                return flat(slot_of(name)[:, 0:n * (4096 // n)], n)

            pe.wait_ge(consts, 9)
            pe.wait_ge(small_in, SMALL)
            for t in range(CT):
                nc.tensor.transpose(ps[:, 0, t * (TAPS + 3):(t + 1) * (TAPS + 3)],
                                    vecs[:, t * P:(t + 1) * P], ident[0:TAPS + 3, 0:TAPS + 3])
            for a in range(2):
                for g in range(2):
                    last = nc.tensor.transpose(ps[:, 1, (2 * a + g) * P:(2 * a + g + 1) * P],
                                               bgu[:, a, g:2 * P:2], ident[:, :])
            last.then_inc(setup_tr, 1)
            for i in range(2 * TB):
                if i % 2 == 0:
                    pe.wait_ge(normed, i // 2 + 1)
                if i >= 4:
                    pe.wait_ge(turned_out, i - 3)
                turn_rows(x_sb, i)
            pe.wait_ge(turned_out, 8)
            pe.wait_ge(setup_out, 2)
            for i in range(20):
                name = ("conv_a", "conv_g", "q", "k", "v")[i // 4]
                if i % 4 == 0:
                    arrived(name)
                if i >= 4:
                    pe.wait_ge(proj_out, i - 3)
                w = weights(name, KD)
                for k in range(KD):
                    cs = slice((i % 4) * P, (i % 4 + 1) * P)
                    if name == "v":
                        last = mm(ps[:, i % 4, :], uT[:, k, cs], w[:, k, :], k == 0, k == KD - 1)
                    else:
                        last = mm(ps[:, i % 4, :], w[:, k, cs], uT[:, k, :], k == 0, k == KD - 1)
                last.then_inc(proj, 1)
            pe.wait_ge(proj_out, 20)
            NI = H * TB

            def score(i):
                h, t = i // TB, i % TB
                w = (t + 1) * P
                if i >= 2:
                    pe.wait_ge(exped, 2 * (i - 1))
                for c in range(2):
                    last = mm(ps[:, 4 + 2 * (i % 2) + c, 0:w], qT[c * QD:(c + 1) * QD, h, t * P:(t + 1) * P],
                              kT[c * QD:(c + 1) * QD, h, 0:w], True, True)
                last.then_inc(scores, 1)

            def turn_a(i):
                t = i % TB
                pe.wait_ge(mixed, i + 1)
                if i >= 2:
                    pe.wait_ge(a_out, i - 1)
                for k in range(t + 1):
                    last = nc.tensor.transpose(ps[:, i % 2, k * P:(k + 1) * P],
                                               ex[:, i % 2, 0, k * P:(k + 1) * P], ident[:, :])
                last.then_inc(a_turned, 1)

            def apply_v(i):
                h, t = i // TB, i % TB
                pe.wait_ge(a_out, i + 1)
                if i >= 1:
                    pe.wait_ge(o_sq, i)
                for k in range(t + 1):
                    last = mm(ps[:, 2, (i % 4) * P:(i % 4 + 1) * P], a_T[:, i % 2, k * P:(k + 1) * P],
                              v_sb[:, k, h * HD:(h + 1) * HD], k == 0, k == t)
                last.then_inc(pv, 1)

            for i in range(NI + 2):
                if i < NI:
                    score(i)
                if i == 2:
                    pe.wait_ge(conv_tap, TAPS * CT)
                    for t in range(CT):
                        last = mm(ps[:, 3, :], ones[:, :], conv[:, t, :], t == 0, t == CT - 1)
                    last.then_inc(conv_mean, 1)
                if 1 <= i <= NI:
                    turn_a(i - 1)
                if i >= 2:
                    apply_v(i - 2)
            pe.wait_ge(conv_sq, CT)
            for t in range(CT):
                last = mm(ps[:, 3, :], ones[:, :], sg[:, t, :], t == 0, t == CT - 1)
            last.then_inc(conv_var, 1)

            def gate_pair(k):
                b = 4 * ((k + 1) % 2)
                if k >= 2:
                    pe.wait_ge(m_ready, k - 1)
                for c, nm in enumerate(("ga", "gb")):
                    name = f"{nm}{k // 4}"
                    arrived(name)
                    w = weights(name, KD)
                    cs = slice((k % 4) * P, (k % 4 + 1) * P)
                    for j in range(KD):
                        last = mm(ps[:, b + c, :], w[:, j, cs], uT[:, j, :], j == 0, j == KD - 1)
                last.then_inc(gates, 1)

            gate_pair(0)
            pe.wait_ge(conv_sd, 1)
            for h in range(H):
                pe.wait_ge(o_normed, TB * (h + 1))
                for t in range(TB):
                    last = nc.tensor.transpose(ps[:, h, t * P:(t + 1) * P], o_tok[:, t, h * HD:(h + 1) * HD],
                                               ident[:, :])
                last.then_inc(o_turned, 1)
            for k in range(KD):
                if k >= 1:
                    if k == 1:
                        pe.wait_ge(o_out, H)
                    gate_pair(k)
                b = 4 * ((k + 1) % 2)
                if k == 0:
                    pe.wait_ge(o_out, H)
                    pe.wait_ge(conv_out, CT)
                for c, (name, src) in enumerate((("ao", o_T), ("co", conv))):
                    arrived(name)
                    w = weights(name, AW // P)
                    for j in range(AW // P):
                        last = mm(ps[:, b + 2 + c, :], w[:, j, k * P:(k + 1) * P], src[:, j, :],
                                  j == 0, j == AW // P - 1)
                last.then_inc(branch, 1)
            def wo(t):
                for h in range(2):
                    i = 2 * t + h
                    arrived(f"wo{h}")
                    if i >= 4:
                        pe.wait_ge(h1_half, i - 3)
                    w = weights(f"wo{h}", KD)
                    for j in range(KD):
                        last = mm(ps[:, i % 4, :], mT[:, j, t * P:(t + 1) * P], w[:, j, :], j == 0, j == KD - 1)
                    last.then_inc(wo_done, 1)

            def turn_u(t):
                pe.wait_ge(normed, TB + t + 1)
                for i in (2 * t, 2 * t + 1):
                    if i >= 4:
                        pe.wait_ge(turned_out, 8 + i - 3)
                    turn_rows(u_tok, i)

            pe.wait_ge(m_ready, KD)
            for t in range(TB):
                wo(t)
                if t >= 1:
                    turn_u(t - 1)
            turn_u(TB - 1)
            pe.wait_ge(turned_out, 16)
            pe.wait_ge(h1_half, 2 * TB)
            for t in range(TB):
                for j in range(KD):
                    last = mm(ps[:, 0, t * E:(t + 1) * E], uT[:, j, t * P:(t + 1) * P], w_rt[:, j, :],
                              j == 0, j == KD - 1)
            last.then_inc(logits, 1)
            arrived("ple")
            pe.wait_ge(p_in, 16)
            for k in range(PLE // P):
                for t in range(TB):
                    last = nc.tensor.transpose(ps[:, 2 + k, t * P:(t + 1) * P], p_sb[:, t, k * P:(k + 1) * P],
                                               ident[:, :])
                last.then_inc(ptr, 1)
            pe.wait_ge(mask_ready, 1)
            for t in range(TB):
                for a in range(t):
                    mm(ps[:, 1, t * E:(t + 1) * E], ones[:, :], mask[:, a, :], a == 0, False)
                mm(ps[:, 1, t * E:(t + 1) * E], before[:, :], mask[:, t, :], t == 0, True)
            for a in range(TB):
                last = mm(ps[:, 1, TB * E:(TB + 1) * E], ones[:, :], mask[:, a, :], a == 0, a == TB - 1)
            last.then_inc(counts, 1)
            pe.wait_ge(pT_out, 2)
            for i in range(2 * TB):
                t, h = i // 2, i % 2
                if i >= 2:
                    pe.wait_ge(ple_out, i - 1)
                for k in range(PLE // P):
                    last = mm(ps[:, 4 + h, :], pT[:, k, t * P:(t + 1) * P], w_ple_sb[:, k, h * 512:(h + 1) * 512],
                              k == 0, k == PLE // P - 1)
                last.then_inc(ple_mm, 1)
            pe.wait_ge(gd_ready, 1)
            for t in range(TB):
                last = nc.tensor.transpose(ps[0:E, 6, t * P:(t + 1) * P], gdense[:, t, :], ident[:, :])
            last.then_inc(gd_turned, 1)
            pe.wait_ge(onehots, TB)
            tab = ps[0:BT, 7, 0:3 * MAXB]
            for i in range(TB * TOP):
                t, k = i // TOP, i % TOP
                last = mm(tab, oh_j[:, t, k, :], oh_r[:, t, k, :, :].rearrange("p a b -> p (a b)"),
                          i == 0, i == TB * TOP - 1)
            last.then_inc(table, 1)
            pe.wait_ge(gdT_out, 1)
            pe.wait_ge(bdn_in, 16)
            for i in range(2 * TB):
                t, h = i // 2, i % 2
                if i >= 2:
                    pe.wait_ge(base_ready, i - 1)
                mm(ps[:, 2 + h, :], gdT[:, t * P:(t + 1) * P], b_dn[:, h * 512:(h + 1) * 512], True, True)\
                    .then_inc(bdn, 1)
            pe.wait_ge(tables, 1)
            pe.wait_ge(base_ready, 2 * TB)
            pe.wait_ge(ple_out, 2 * TB)

            def turn_x():
                for k in range(KD):
                    last = nc.tensor.transpose(ps[:, 4 + k // 4, (k % 4) * BT:(k % 4 + 1) * BT],
                                               xg[:, k * P:(k + 1) * P], ident[:, :])
                last.then_inc(x_turned, 1)

            nc.tensor.sem_inc(y_read, 2)
            nc.tensor.sem_inc(gu_done, GUC)
            nc.tensor.sem_inc(down_done, DNC)
            pe.wait_ge(gathered, 16)
            turn_x()
            with pe.Fori(0, E) as e:
                first = pe.value_load(starti[0:1, bass.ds(e, 1)], min_val=0, max_val=MAXB - 1)
                end = pe.value_load(starti[0:1, bass.ds(e + 1, 1)], min_val=1, max_val=MAXB - 1)
                with pe.Fori(first, end) as b:
                    pe.wait_ge(xT_ready, b + 1)
                    for c in range(GUC):
                        pe.wait_ge(ring_in[c], (e + (uses[c] + 1)) * 16)
                        pe.wait_ge(gu_read, b * GUC + (c + 1))
                        w = chunk_slot(c)
                        for tg in range(4):
                            t, g = tg // 2, tg % 2
                            for j in range(KD):
                                last = mm(ps[:, c, tg * BT:(tg + 1) * BT],
                                          w[:, j, t * 2 * P + g:(t + 1) * 2 * P:2], xT[:, j, :],
                                          j == 0, j == KD - 1)
                        last.then_inc(gu_done, 1)
                    for c in range(2):
                        pe.wait_ge(ring_in[GUC + c], (e + (uses[GUC + c] + 1)) * 16)
                        w = chunk_slot(GUC + c)
                        for j in range(4):
                            i = 4 * c + j
                            if i % 2 == 0:
                                pe.wait_ge(h_ready, b * GUC + (i // 2 + 1))
                            for k in range(2):
                                if i == 0 and k == 0:
                                    pe.wait_ge(y_read, b * 2 + 2)
                                last = mm(ps[:, 6 + k, :], hT[:, i, :], w[:, j, k * BANK:(k + 1) * BANK],
                                          i == 0, i == FT - 1)
                        last.then_inc(down_done, 1)
                    pe.wait_ge(gathered, (b + 2) * 16)
                    nc.tensor.sem_inc(passed["pe"], 1)
                    turn_x()
            for i in range(2 * TB):
                if i % 2 == 0:
                    pe.wait_ge(normed, 2 * TB + i // 2 + 1)
                if i >= 4:
                    pe.wait_ge(turned_out, 16 + i - 3)
                turn_rows(u_tok, i)
            pe.wait_ge(turned_out, 24)
            for i in range(2 * TB):
                t, h = i // 2, i % 2
                if i < 2:
                    pe.wait_ge(ring_in[h], 16 * (uses[h] + E + 1))
                if i >= 4:
                    pe.wait_ge(pg_sig, i - 3)
                w = flat(ring[:, h, :], KD)
                for j in range(KD):
                    last = mm(ps[:, i % 4, :], uT[:, j, t * P:(t + 1) * P], w[:, j, :], j == 0, j == KD - 1)
                last.then_inc(pg, 1)


_INS = ["x", "p", "g_mix", "w_in", "lambda_q1", "lambda_k1", "lambda_q2", "lambda_k2", "g_subln",
        "w_attn_out", "w_dw", "b_dw", "g_conv_ln", "b_conv_ln", "w_conv_out", "w_o", "g_ffn",
        "w_router", "b_router", "w_gate_up", "b_gate_up", "w_down", "b_down",
        "w_ple", "g_ple", "w_ple_gate", "g_final"]


def kernel(**inputs):
    import numpy as np
    import concourse.bacc as bacc
    from concourse.bass_utils import run_bass_kernel_spmd

    nc = bacc.Bacc("TRN2", target_bir_lowering=False, num_devices=1)
    arrays, args = {}, []
    for name in _INS:
        a = np.ascontiguousarray(inputs[name])
        arrays[f"in_{name}"] = a
        args.append(nc.dram_tensor(f"in_{name}", a.shape, mybir.dt.from_np(a.dtype), kind="ExternalInput").ap())
    out = nc.dram_tensor("out_rows", inputs["x"].shape, F32, kind="ExternalOutput").ap()
    trunk_layer(nc, *args, out)
    r = run_bass_kernel_spmd(nc, [arrays], core_ids=[0])
    return r.results[0]["out_rows"]
```

```python
from contextlib import ExitStack

import concourse.bass as bass
from concourse import mybir

F32 = mybir.dt.float32
F32R = mybir.dt.float32r
I32 = mybir.dt.int32
U32 = mybir.dt.uint32
ALU = mybir.AluOpType
ACT = mybir.ActivationFunctionType
AX_X = mybir.AxisListType.X

P = 128
BANK = 512
EPS = 1e-5
NEG = -1e30
SLOTS = 6
BT = P


def trunk_layer(nc, x, p, g_mix, w_in, lambda_q1, lambda_k1, lambda_q2, lambda_k2, g_subln,
                w_attn_out, w_dw, b_dw, g_conv_ln, b_conv_ln, w_conv_out, w_o, g_ffn,
                w_router, b_router, w_gate_up, b_gate_up, w_down, b_down,
                w_ple, g_ple, w_ple_gate, g_final, out):
    S, D = x.shape[1], x.shape[2]
    AW = w_attn_out.shape[1]
    CW = w_conv_out.shape[1]
    PLE = p.shape[3]
    E = w_router.shape[2]
    F = w_down.shape[2]
    TAPS = w_dw.shape[1]
    HD = g_subln.shape[1]
    H = AW // HD
    QD = HD // 2
    TOP = 4
    TB = S // P
    KD = D // P
    FT = F // P
    CT = CW // P
    PAD = TAPS - 1
    ZW = S + PAD + 2
    MAXB = S * TOP // BT + E
    SCALE = float(QD) ** -0.5
    LAM_INIT = 0.2
    ALPHA, LIMIT = 1.702, 7.0
    NB, KP = 4, 2
    assert (S, D, AW, CW, E, F, H) == (512, 1024, 512, 512, 32, 1024, 4) and TB == 4

    x_t = x.rearrange("a (t q) d -> q (a t) d", q=P)
    p_t = p.rearrange("l a (t q) d -> q (l a t) d", q=P)
    out_t = out.rearrange("a (t q) d -> q (a t) d", q=P)

    u_rows = nc.dram_tensor("u_rows", (S, D), F32, kind="Internal").ap()
    sum_rows = nc.dram_tensor("sum_rows", (S + BT, D), F32, kind="Internal").ap()

    w_in_v = w_in.rearrange("l (k q) n -> q (l k) n", q=P)
    w_ao_v = w_attn_out.rearrange("l (k q) n -> q (l k) n", q=P)
    w_co_v = w_conv_out.rearrange("l (k q) n -> q (l k) n", q=P)
    w_o_v = w_o.rearrange("l (k q) n -> q (l k) n", q=P)
    w_ple_v = w_ple.rearrange("l (k q) n -> q (l k) n", q=P)
    w_pg_v = w_ple_gate.rearrange("l (k q) n -> q (l k) n", q=P)

    def cols(view, c):
        return view[:, :, c * 512:(c + 1) * 512]

    dense = [("conv_a", cols(w_in_v, 3)), ("conv_g", cols(w_in_v, 4)), ("q", cols(w_in_v, 0)),
             ("k", cols(w_in_v, 1)), ("v", cols(w_in_v, 2)),
             ("ga0", cols(w_in_v, 5)), ("ao", w_ao_v), ("gb0", cols(w_in_v, 7)), ("co", w_co_v),
             ("ga1", cols(w_in_v, 6)), ("gb1", cols(w_in_v, 8)),
             ("wo0", cols(w_o_v, 0)), ("wo1", cols(w_o_v, 1)), ("ple", w_ple_v)]
    at = {name: i for i, (name, _) in enumerate(dense)}
    uses = [len([i for i in range(len(dense)) if i % SLOTS == s]) for s in range(SLOTS)]

    with ExitStack() as ctx:
        def sb(name, shape, dt=F32):
            return ctx.enter_context(nc.sbuf_tensor(name, shape, dt))

        def sem(name):
            return ctx.enter_context(nc.semaphore(name))

        ps = ctx.enter_context(nc.psum_tensor("ps", [P, 8, BANK], F32))

        ring = sb("ring", [P, SLOTS, 4096])
        X = sb("X", [P, TB * D])
        R1 = sb("R1", [P, 4096])
        gB = [sb("gB0", [P, D]), sb("gB1", [P, D])]

        RW = 2048 + CT * ZW + 2048
        with ExitStack() as first_use:
            UT, R2, R4 = (first_use.enter_context(nc.sbuf_tensor(name, [P, w], F32)) for name, w in
                          (("UT", KD * S),
                           ("R2", RW),
                           ("R4", 5120)))
        UTr, R2r, R4r = sb("UTr", [P, KD * S], F32R), sb("R2r", [P, RW], F32R), sb("R4r", [P, 5120], F32R)
        x_sb = X[:, :].rearrange("p (t d) -> p t d", t=TB)
        o_tok = X[:, 0:2048].rearrange("p (t d) -> p t d", t=TB)
        o_T = X[:, 2048:4096].rearrange("p (h s) -> p h s", h=H)
        uT = UT[:, :].rearrange("p (k s) -> p k s", k=KD)
        qT = R1[:, 0:2048].rearrange("p (h s) -> p h s", h=H)
        kT = R1[:, 2048:4096].rearrange("p (h s) -> p h s", h=H)
        vecs = R1[0:TAPS + 3, 0:512]
        lamb = R1[:, 1024:1280].rearrange("p (a n) -> p a n", a=4)
        lprod = R1[:, 1280:1408].rearrange("p (a n) -> p a n", a=2)
        mT = R1[:, :].rearrange("p (k s) -> p k s", k=KD)
        pple = R1[:, :].rearrange("p (t d) -> p t d", t=TB)
        v_sb = R2[:, 0:2048].rearrange("p (t n) -> p t n", t=TB)
        z = R2[:, 2048:2048 + CT * ZW].rearrange("p (t s) -> p t s", t=CT)
        C0 = 2048 + CT * ZW
        conv = R2[:, C0:C0 + 2048].rearrange("p (t s) -> p t s", t=CT)
        u_tok = R2[:, 0:4096].rearrange("p (t d) -> p t d", t=TB)
        ex = R4[:, 0:2048].rearrange("p (b c k) -> p b c k", b=2, c=2)
        a_T = R4[:, 2048:3072].rearrange("p (b s) -> p b s", b=2)
        sg = R4[:, 3072:5120].rearrange("p (t s) -> p t s", t=4)
        junk = R4[:, 0:D]
        xg = R4[0:BT, 0:1024]
        b_dn = R4[0:E, 0:1024]
        y_sb = R4[0:BT, 1024:2048]
        x_hi = R4r[:, 2048:3072]
        x_lo = R4r[:, 3072:4096]
        hT = R4[:, 4096:5120].rearrange("p (k n) -> p k n", k=FT)
        bgu = R4[0:2 * E, 3072:5120]
        bgu_parts = R2r[0:2 * E, 4096:6144]
        w_hi = R2r[:, 0:4096].rearrange("p (b k n) -> p b k n", b=NB, k=KP)
        w_lo = UTr[:, 0:4096].rearrange("p (b k n) -> p b k n", b=NB, k=KP)
        gate_b, lin_b, sig_b, lg_b, h_tok = (X[:, 512 * i:512 * (i + 1)].rearrange("p (b n) -> p b n", b=2)
                                             for i in range(5))
        q0 = C0

        def rt(n):
            nonlocal q0
            q0 += n
            return R2[:, q0 - n:q0]

        lg = rt(TB * E).rearrange("p (t e) -> p t e", t=TB)
        eq = rt(TB * TOP * E).rearrange("p (t k e) -> p t k e", t=TB, k=TOP)
        eqs = rt(TB * TOP * E).rearrange("p (t k e) -> p t k e", t=TB, k=TOP)
        mask = rt(TB * E).rearrange("p (t e) -> p t e", t=TB)
        slot = rt(TB * E).rearrange("p (t e) -> p t e", t=TB)
        big = rt((TB - 1) * E).rearrange("p (a e) -> p a e", a=TB - 1)
        assert q0 <= C0 + 2048
        oh_j = UT[:, 0:16 * BT].rearrange("p (t k j) -> p t k j", t=TB, k=TOP)
        oh_r = R2[:, 0:16 * 3 * MAXB].rearrange("p (t k a b) -> p t k a b", t=TB, k=TOP, a=3)

        ident = sb("ident", [P, P])
        ones = sb("ones", [P, P])
        before = sb("before", [P, P])
        cmask = sb("cmask", [P, P])
        iota = sb("iota", [P, BT])
        tokid = sb("tokid", [P, TB])
        spare = sb("spare", [BT, 1])
        gsub = sb("gsub", [P, HD])
        cvec = sb("cvec", [P, CT, TAPS + 3])
        eye2 = sb("eye2", [2 * E, E])
        own = sb("own", [2 * E, 2, E])
        bounds = sb("bounds", [2 * E, 2])
        sel2 = sb("sel2", [2 * E, 2, MAXB])
        sel_tab = sb("sel_tab", [2 * E, MAXB])
        sel_c = sb("sel_c", [2 * E, P], F32R)
        b_rt = sb("b_rt", [P, E])
        w_rt = sb("w_rt", [P, KD, E])
        ss = sb("ss", [P, TB])
        rs = sb("rs", [P, TB])
        rr = sb("rr", [P, TB])
        oss = sb("oss", [P, TB, H])
        ors = sb("ors", [P, TB, H])
        orr = sb("orr", [P, TB, H])
        epsc = sb("epsc", [P, 2])
        lam2 = sb("lam2", [P, 2])
        lame = sb("lame", [P, 2])
        nlam = sb("nlam", [P, 2])
        mx = sb("mx", [P, 2, 2])
        nmx = sb("nmx", [P, 2, 2])
        den = sb("den", [P, 2, 2])
        rden = sb("rden", [P, 2, 2])
        nrl = sb("nrl", [P, 2])
        top = sb("top", [P, TB, 8])
        topi = sb("topi", [P, TB, 8], U32)
        topf = sb("topf", [P, TB, TOP])
        gd = sb("gd", [P, TB, TOP])
        ge = sb("ge", [P, TB, TOP])
        gs = sb("gs", [P, TB])
        gr = sb("gr", [P, TB])
        gate = sb("gate", [P, TB, TOP])
        gdense = sb("gdense", [P, TB, E])
        gdT = R4[0:E, 2048:2560]
        nblk = sb("nblk", [P, E])
        cum = sb("cum", [P, E])
        startf = sb("startf", [P, E + 1])
        starti = sb("starti", [P, E + 1], I32)
        slk = sb("slk", [P, TB * TOP])
        sli = sb("sli", [P, TB * TOP], I32)
        slj = sb("slj", [P, 2, TB * TOP], I32)
        slf = sb("slf", [P, 2, TB * TOP])
        tabf = R4[0:BT, 2560:2560 + 2 * MAXB].rearrange("p (a b) -> p a b", a=2)
        inval = R4[0:BT, 2688:2688 + MAXB]
        gate_tab = sb("gate_tab", [BT, MAXB])
        from_tab = sb("from_tab", [BT, MAXB], I32)
        to_tab = sb("to_tab", [BT, MAXB], I32)
        from_c = sb("from_c", [BT, 1], I32)
        to_c = sb("to_c", [BT, 1], I32)
        gate_c = sb("gate_c", [BT, 1])

        x_in = sem("x_in")
        small_in = sem("small_in")
        gains_in = [sem("gain0_in"), sem("gain1_in")]
        p_in = sem("p_in")
        bdn_in = sem("bdn_in")
        ring_in = [sem(f"ring_in{s}") for s in range(SLOTS)]
        consts = sem("consts")
        zpad0 = sem("zpad0")
        dve_step = sem("dve_step")
        act_step = sem("act_step")
        pool_step = sem("pool_step")
        squares = sem("squares")
        roots = sem("roots")
        normed = sem("normed")
        turned = sem("turned")
        turned_out = sem("turned_out")
        setup_tr = sem("setup_tr")
        setup_out = sem("setup_out")
        proj = sem("proj")
        proj_out = sem("proj_out")
        z_ready = sem("z_ready")
        conv_tap = sem("conv_tap")
        conv_mean = sem("conv_mean")
        conv_c = sem("conv_c")
        conv_sq = sem("conv_sq")
        conv_var = sem("conv_var")
        conv_sd = sem("conv_sd")
        conv_n = sem("conv_n")
        conv_ready = sem("conv_ready")
        conv_out = sem("conv_out")
        lam_dot = sem("lam_dot")
        lam_exp = sem("lam_exp")
        scores = sem("scores")
        maxed = sem("maxed")
        exped = sem("exped")
        mixed = sem("mixed")
        a_turned = sem("a_turned")
        a_out = sem("a_out")
        pv = sem("pv")
        o_sq = sem("o_sq")
        o_cp = sem("o_cp")
        o_root = sem("o_root")
        o_normed = sem("o_normed")
        o_turned = sem("o_turned")
        o_out = sem("o_out")
        gates = sem("gates")
        gates_sig = sem("gates_sig")
        branch = sem("branch")
        m_ready = sem("m_ready")
        wo_done = sem("wo_done")
        h1_half = sem("h1_half")
        x_again = sem("x_again")
        logits = sem("logits")
        top_ready = sem("top_ready")
        gexp = sem("gexp")
        mask_ready = sem("mask_ready")
        counts = sem("counts")
        onehots = sem("onehots")
        table = sem("table")
        tables = sem("tables")
        gd_ready = sem("gd_ready")
        gd_turned = sem("gd_turned")
        gdT_out = sem("gdT_out")
        bdn = sem("bdn")
        base_ready = sem("base_ready")
        ptr = sem("ptr")
        pT_out = sem("pT_out")
        ple_mm = sem("ple_mm")
        ple_out = sem("ple_out")
        u_stored = sem("u_stored")
        sum_stored = sem("sum_stored")
        gathered = sem("gathered")
        scattered = sem("scattered")
        cols_ready = sem("cols_ready")
        from_ready = sem("from_ready")
        to_ready = sem("to_ready")
        x_turned = sem("x_turned")
        x_hi_ready = sem("x_hi_ready")
        hi_ready = sem("hi_ready")
        lo_ready = sem("lo_ready")
        piece_used = sem("piece_used")
        bgu_in = sem("bgu_in")
        bgu_hi = sem("bgu_hi")
        bgu_split = sem("bgu_split")
        sel_ready = sem("sel_ready")
        x_split = sem("x_split")
        down_in = sem("down_in")
        h_turned = sem("h_turned")
        hT_ready = sem("hT_ready")
        gu_done = sem("gu_done")
        gu_read = sem("gu_read")
        gate_ready = sem("gate_ready")
        sig_ready = sem("sig_ready")
        h_ready = sem("h_ready")
        dve_block = sem("dve_block")
        down_done = sem("down_done")
        y_ready = sem("y_ready")
        y_free = sem("y_free")
        passed = {"pe": sem("pe_passed"), "pool": sem("pool_passed")}
        h2_in = sem("h2_in")
        pg = sem("pg")
        pg_sig = sem("pg_sig")
        h3_half = sem("h3_half")
        out_ready = sem("out_ready")
        out_stored = sem("out_stored")

        SMALL = 11 * 16
        PC = KD // KP
        multiplied = {"conv_a": (proj, 4), "conv_g": (proj, 8), "q": (proj, 12), "k": (proj, 16), "v": (proj, 20),
                      "ga0": (gates, 4), "gb0": (gates, 4), "ga1": (gates, 8), "gb1": (gates, 8),
                      "ao": (branch, 8), "co": (branch, 8), "wo0": (wo_done, 7), "wo1": (wo_done, 8),
                      "ple": (ple_mm, 8)}

        block = ctx.enter_context(nc.Block())

        def slot_of(name):
            return ring[:, at[name] % SLOTS, :]

        def flat(dst, k):
            return dst.rearrange("p (k n) -> p k n", k=k)

        ple_slot = slot_of("ple")
        w_ple_sb = flat(ple_slot[:, 0:2048], PLE // P)
        p_sb = ple_slot[:, 2048:3072].rearrange("p (t d) -> p t d", t=TB)
        pT = ple_slot[:, 3072:4096].rearrange("p (k s) -> p k s", k=PLE // P)

        GUC, DNC = 4, 2
        w_gu_v = w_gate_up.rearrange("l e (k q) n -> q (l e) k n", q=P)
        w_dn_v = w_down.rearrange("l e (k q) n -> q (l e) k n", q=P)

        def expert_chunk(e, c):
            if c < GUC:
                return w_gu_v[:, bass.ds(e, 1), :, c * 512:(c + 1) * 512].rearrange("q e k n -> q (e k) n")
            c -= GUC
            return w_dn_v[:, bass.ds(e, 1), c * 4:(c + 1) * 4, :].rearrange("q e k n -> q (e k) n")

        def chunk_slot(c):
            return flat(ring[:, c, :], 8 if c < GUC else 4)

        @block.sync
        def _(sp):
            sp.dma_start(x_sb, x_t).then_inc(x_in, 16)
            for i, (name, src) in enumerate(dense):
                if i >= SLOTS:
                    sp.wait_ge(*multiplied[dense[i - SLOTS][0]])
                k = src.shape[1]
                n = k * src.shape[2]
                sp.dma_start(flat(slot_of(name)[:, 0:n], k), src).then_inc(ring_in[i % SLOTS], 16)
                if name == "wo1":
                    sp.wait_ge(branch, KD)
                    sp.dma_start(x_sb, x_t).then_inc(x_again, 16)
                if name == "ple":
                    sp.dma_start(p_sb, p_t).then_inc(p_in, 16)
            for c in range(SLOTS):
                lies = max(i for i in range(len(dense)) if i % SLOTS == c)
                sp.wait_ge(*multiplied[dense[lies][0]])
                sp.dma_start(chunk_slot(c), expert_chunk(0, c)).then_inc(ring_in[c], 16)
            sp.wait_ge(tables, 1)
            with sp.Fori(1, E) as e:
                first = sp.value_load(starti[0:1, bass.ds(e, 1)], min_val=1, max_val=MAXB - 1)
                for c in range(SLOTS):
                    if c < GUC:
                        sp.wait_ge(lo_ready, first * (GUC * PC) + (c + 1) * PC)
                    else:
                        sp.wait_ge(down_done, first * DNC + (c + 1 - GUC))
                    sp.dma_start(chunk_slot(c), expert_chunk(e, c)).then_inc(ring_in[c], 16)
            total = sp.value_load(starti[0:1, E:E + 1], min_val=1, max_val=MAXB - 1)
            for c in range(2):
                sp.wait_ge(lo_ready, total * (GUC * PC) + (c + 1) * PC)
                sp.dma_start(flat(ring[:, c, :], KD), cols(w_pg_v, c)).then_inc(ring_in[c], 16)
            sp.wait_ge(y_free, total + 2)
            sp.dma_start(x_sb, sum_rows[0:S, :].rearrange("(t q) d -> q t d", q=P)).then_inc(h2_in, 16)
            for t in range(TB):
                sp.wait_ge(out_ready, t + 1)
                sp.dma_start(out_t[:, t, :], u_tok[:, t, :]).then_inc(out_stored, 16)
            sp.wait_ge(out_stored, 16 * TB)

        @block.gpsimd
        def _(pool):
            n = 0

            def link(ins):
                nonlocal n
                n += 1
                ins.then_inc(pool_step, 1)
                pool.wait_ge(pool_step, n)

            nc.gpsimd.memset(ones[:, :], 1.0).then_inc(consts, 1)
            link(nc.gpsimd.memset(ident[:, :], 0.0))
            link(nc.gpsimd.memset(before[:, :], 1.0))
            link(nc.gpsimd.memset(cmask[:, :], 0.0))
            nc.gpsimd.affine_select(out=ident[:, :], in_=ident[:, :], compare_op=ALU.not_equal, fill=1.0,
                                    base=0, pattern=[[-1, P]], channel_multiplier=1).then_inc(consts, 1)
            nc.gpsimd.affine_select(out=before[:, :], in_=before[:, :], compare_op=ALU.is_gt, fill=0.0,
                                    base=0, pattern=[[1, P]], channel_multiplier=-1).then_inc(consts, 1)
            nc.gpsimd.affine_select(out=cmask[:, :], in_=cmask[:, :], compare_op=ALU.is_ge, fill=NEG,
                                    base=0, pattern=[[-1, P]], channel_multiplier=1).then_inc(consts, 1)
            nc.gpsimd.iota(iota[:, :], pattern=[[1, BT]], base=0, channel_multiplier=0,
                           allow_small_or_imprecise_dtypes=True).then_inc(consts, 1)
            nc.gpsimd.iota(tokid[:, :], pattern=[[P, TB]], base=0, channel_multiplier=1,
                           allow_small_or_imprecise_dtypes=True).then_inc(consts, 1)
            nc.gpsimd.iota(spare[:, :], pattern=[[0, 1]], base=S, channel_multiplier=1,
                           allow_small_or_imprecise_dtypes=True).then_inc(consts, 1)
            nc.gpsimd.memset(epsc[:, 0:1], EPS).then_inc(consts, 1)
            nc.gpsimd.memset(epsc[:, 1:2], EPS / (1.0 - LAM_INIT) ** 2).then_inc(consts, 1)
            nc.gpsimd.memset(z[:, :, 0:PAD], 0.0).then_inc(zpad0, 1)

            pool.wait_ge(normed, 2 * TB)
            nc.gpsimd.dma_start(u_rows.rearrange("(t q) d -> q t d", q=P), u_tok).then_inc(u_stored, 16)
            link(nc.gpsimd.memset(y_sb, 0.0))
            nc.gpsimd.dma_start(sum_rows[S:S + BT, :], y_sb).then_inc(sum_stored, 16)
            pool.wait_ge(sum_stored, 16)
            pool.wait_ge(base_ready, 2 * TB)
            nc.gpsimd.dma_start(sum_rows[0:S, :].rearrange("(t q) d -> q t d", q=P), x_sb)\
                .then_inc(sum_stored, 16)
            pool.wait_ge(u_stored, 16)
            pool.wait_ge(tables, 1)
            total = pool.value_load(starti[0:1, E:E + 1], min_val=1, max_val=MAXB - 1)
            link(nc.gpsimd.tensor_copy(from_c[:, :], from_tab[:, 0:1]))
            nc.gpsimd.indirect_dma_start(out=xg, out_offset=None, in_=u_rows[:, :],
                                         in_offset=bass.IndirectOffsetOnAxis(ap=from_c[:, 0:1], axis=0))\
                .then_inc(gathered, 16)
            nc.gpsimd.memset(gate_c[:, :], 0.0).then_inc(cols_ready, 1)
            nc.gpsimd.tensor_copy(sel_c[:, :], sel_tab[:, 0:1].to_broadcast([2 * E, P])).then_inc(sel_ready, 1)
            pool.wait_ge(sum_stored, 32)
            nc.gpsimd.sem_inc(y_free, 2)
            with pool.Fori(0, total) as b:
                pool.wait_ge(gathered, (b + 1) * 16)
                pool.wait_ge(x_turned, b + 1)
                nc.gpsimd.tensor_copy(from_c[:, :], from_tab[:, bass.ds(b + 1, 1)]).then_inc(from_ready, 1)
                pool.wait_ge(from_ready, b + 1)
                nc.gpsimd.sem_inc(passed["pool"], 1)
                nc.gpsimd.indirect_dma_start(out=xg, out_offset=None, in_=u_rows[:, :],
                                             in_offset=bass.IndirectOffsetOnAxis(ap=from_c[:, 0:1], axis=0))\
                    .then_inc(gathered, 16)
                pool.wait_ge(y_ready, b * 2 + 2)
                nc.gpsimd.tensor_copy(gate_c[:, :], gate_tab[:, bass.ds(b, 1)]).then_inc(cols_ready, 1)
                nc.gpsimd.tensor_copy(to_c[:, :], to_tab[:, bass.ds(b, 1)]).then_inc(to_ready, 1)
                pool.wait_ge(gu_done, b * GUC + GUC)
                nc.gpsimd.tensor_copy(sel_c[:, :], sel_tab[:, bass.ds(b + 1, 1)].to_broadcast([2 * E, P]))\
                    .then_inc(sel_ready, 1)
                pool.wait_ge(to_ready, b + 1)
                pool.wait_ge(y_ready, b * 2 + 4)
                nc.gpsimd.sem_inc(passed["pool"], 1)
                nc.gpsimd.indirect_dma_start(out=sum_rows[:, :],
                                             out_offset=bass.IndirectOffsetOnAxis(ap=to_c[:, 0:1], axis=0),
                                             in_=y_sb, in_offset=None, compute_op=ALU.add)\
                    .then_inc(scattered, 16)
                pool.wait_ge(scattered, (b + 1) * 16)
                nc.gpsimd.sem_inc(y_free, 1)
            pool.wait_ge(gathered, (total + 1) * 16)

        @block.scalar
        def _(act):
            n = 0

            def link(ins):
                nonlocal n
                n += 1
                ins.then_inc(act_step, 1)
                act.wait_ge(act_step, n)

            def row(v):
                return v.rearrange("(a n) -> a n", a=1) if len(v.shape) == 1 else v

            def load(dst, src):
                act.dma_start(dst, src).then_inc(small_in, 16)

            act.dma_start(gB[0][:, :], g_mix.to_broadcast([P, D])).then_inc(gains_in[0], 16)
            act.dma_start(gB[1][:, :], g_ffn.to_broadcast([P, D])).then_inc(gains_in[1], 16)
            load(R1[0:TAPS, 0:512], w_dw.rearrange("l j c -> (l j) c"))
            load(R1[TAPS:TAPS + 1, 0:512], b_dw)
            load(R1[TAPS + 1:TAPS + 2, 0:512], g_conv_ln)
            load(R1[TAPS + 2:TAPS + 3, 0:512], b_conv_ln)
            for j, v in enumerate((lambda_q1, lambda_k1, lambda_q2, lambda_k2)):
                load(lamb[:, j, :], v.to_broadcast([P, QD]))
            load(gsub[:, :], g_subln.to_broadcast([P, HD]))
            load(b_rt[:, :], b_router.to_broadcast([P, E]))
            load(w_rt[:, :, :], w_router.rearrange("l (k q) e -> q (l k) e", q=P))

            act.wait_ge(consts, 9)

            act.wait_ge(x_in, 16)
            for t in range(TB):
                link(nc.scalar.activation(junk, x_sb[:, t, :], ACT.Square, accum_out=ss[:, t:t + 1]))
            nc.scalar.activation(rs[:, :], ss[:, :], ACT.Sqrt, bias=epsc[:, 0:1], scale=1.0 / D)\
                .then_inc(roots, 1)
            for t in range(TB):
                for h in range(2):
                    act.wait_ge(turned, 2 * t + h + 1)
                    nc.scalar.activation(uT[:, 4 * h:4 * h + 4, t * P:(t + 1) * P],
                                         ps[:, 4 + (2 * t + h) % 4, :].rearrange("p (k s) -> p k s", k=4),
                                         ACT.Copy).then_inc(turned_out, 1)
            act.wait_ge(zpad0, 1)
            for i in range(20):
                j, t = i // 4, i % 4
                act.wait_ge(proj, i + 1)
                src = ps[:, i % 4, :]
                if j == 0:
                    ins = nc.scalar.activation(z[:, t, PAD:PAD + S], src, ACT.Copy)
                elif j == 1:
                    ins = nc.scalar.activation(sg[:, t, :], src, ACT.Sigmoid)
                elif j == 2:
                    if t == 0:
                        act.wait_ge(setup_out, 1)
                        act.wait_ge(lam_dot, 1)
                    ins = nc.scalar.activation(qT[:, t, :], src, ACT.Copy, scale=SCALE)
                elif j == 3:
                    ins = nc.scalar.activation(kT[:, t, :], src, ACT.Copy)
                else:
                    ins = nc.scalar.activation(v_sb[:, t, :], src, ACT.Copy)
                ins.then_inc(proj_out, 1)
            nc.scalar.activation(lame[:, :], lam2[:, :], ACT.Exp).then_inc(lam_exp, 1)

            def exps(i):
                w = (i % TB + 1) * P
                act.wait_ge(maxed, i + 1)
                if i >= 2:
                    act.wait_ge(a_turned, i - 1)
                for c in range(2):
                    nc.scalar.activation(ex[:, i % 2, c, 0:w], ps[:, 4 + 2 * (i % 2) + c, 0:w], ACT.Exp,
                                         bias=nmx[:, i % 2, c:c + 1],
                                         accum_out=den[:, i % 2, c:c + 1]).then_inc(exped, 1)

            def turned_a(i):
                w = (i % TB + 1) * P
                act.wait_ge(a_turned, i + 1)
                if i >= 2:
                    act.wait_ge(pv, i - 1)
                nc.scalar.activation(a_T[:, i % 2, 0:w], ps[:, i % 2, 0:w], ACT.Copy).then_inc(a_out, 1)

            def results(i):
                h, t = i // TB, i % TB
                act.wait_ge(pv, i + 1)
                nc.scalar.activation(o_tok[:, t, h * HD:(h + 1) * HD], ps[:, 2, (i % 4) * P:(i % 4 + 1) * P],
                                     ACT.Copy).then_inc(o_cp, 1)
                act.wait_ge(o_cp, i + 1)
                nc.scalar.activation(ps[:, 2, (i % 4) * P:(i % 4 + 1) * P],
                                     o_tok[:, t, h * HD:(h + 1) * HD],
                                     ACT.Square, accum_out=oss[:, t, h:h + 1]).then_inc(o_sq, 1)

            NI = H * TB
            for i in range(NI + 2):
                if i < NI:
                    exps(i)
                if 1 <= i <= NI:
                    turned_a(i - 1)
                if i >= 2:
                    results(i - 2)
            act.wait_ge(conv_c, CT)
            for t in range(CT):
                nc.scalar.activation(sg[:, t, :], conv[:, t, :], ACT.Square).then_inc(conv_sq, 1)
            act.wait_ge(conv_var, 1)
            nc.scalar.activation(ex[:, 0, 0, :], ps[:, 3, :], ACT.Sqrt, bias=epsc[:, 0:1], scale=1.0 / CW)\
                .then_inc(conv_sd, 1)
            act.wait_ge(o_sq, NI)
            nc.scalar.activation(ors[:, :, :], oss[:, :, :], ACT.Sqrt, bias=epsc[:, 1:2],
                                 scale=1.0 / (HD * (1.0 - LAM_INIT) ** 2)).then_inc(o_root, 1)
            for t in range(CT):
                act.wait_ge(conv_n, t + 1)
                nc.scalar.activation(sg[:, t, :], conv[:, t, :], ACT.Sigmoid,
                                     bias=cvec[:, t, TAPS + 2:TAPS + 3],
                                     scale=cvec[:, t, TAPS + 1:TAPS + 2]).then_inc(conv_ready, 1)
            for h in range(H):
                act.wait_ge(o_turned, h + 1)
                nc.scalar.activation(o_T[:, h, :], ps[:, h, :], ACT.Copy).then_inc(o_out, 1)
            for k in range(KD):
                b = 4 * ((k + 1) % 2)
                act.wait_ge(gates, k + 1)
                if k >= 2:
                    act.wait_ge(m_ready, k - 1)
                for c in range(2):
                    nc.scalar.activation(ex[:, k % 2, c, :], ps[:, b + c, :], ACT.Sigmoid)\
                        .then_inc(gates_sig, 1)
            act.wait_ge(m_ready, KD)
            for t in range(TB):
                act.wait_ge(h1_half, 2 * t + 2)
                link(nc.scalar.activation(junk, x_sb[:, t, :], ACT.Square, accum_out=ss[:, t:t + 1]))
                nc.scalar.activation(rs[:, t:t + 1], ss[:, t:t + 1], ACT.Sqrt, bias=epsc[:, 0:1],
                                     scale=1.0 / D).then_inc(roots, 1)
                for h in range(2):
                    act.wait_ge(turned, 8 + 2 * t + h + 1)
                    nc.scalar.activation(uT[:, 4 * h:4 * h + 4, t * P:(t + 1) * P],
                                         ps[:, 4 + (2 * t + h) % 4, :].rearrange("p (k s) -> p k s", k=4),
                                         ACT.Copy).then_inc(turned_out, 1)
            act.dma_start(gB[0][:, :], g_ple.to_broadcast([P, D])).then_inc(gains_in[0], 16)
            act.wait_ge(normed, 2 * TB)
            act.dma_start(gB[1][:, :], row(g_final).to_broadcast([P, D])).then_inc(gains_in[1], 16)
            act.dma_start(b_dn, b_down.rearrange("l e d -> (l e) d")).then_inc(bdn_in, 16)
            for a in range(2):
                act.dma_start(bgu[a * E:(a + 1) * E, :], b_gate_up.rearrange("l e n -> (l e) n"))\
                    .then_inc(bgu_in, 16)
            act.wait_ge(top_ready, 1)
            nc.scalar.activation(ge[:, :, :], gd[:, :, :], ACT.Exp).then_inc(gexp, 1)
            for k in range(PLE // P):
                act.wait_ge(ptr, k + 1)
                nc.scalar.activation(pT[:, k, :], ps[:, 2 + k, :], ACT.Copy).then_inc(pT_out, 1)
            for i in range(2 * TB):
                act.wait_ge(ple_mm, i + 1)
                nc.scalar.activation(pple[:, i // 2, (i % 2) * 512:(i % 2 + 1) * 512], ps[:, 4 + i % 2, :],
                                     ACT.Copy).then_inc(ple_out, 1)
            act.wait_ge(gd_turned, 1)
            nc.scalar.activation(gdT, ps[0:E, 6, :], ACT.Copy).then_inc(gdT_out, 1)
            act.wait_ge(tables, 1)
            act.wait_ge(bgu_in, 32)
            nc.scalar.activation(bgu_parts, bgu, ACT.Copy).then_inc(bgu_hi, 1)

            def results_out(b, more=0):
                act.wait_ge(cols_ready, b + 1)
                act.wait_ge(y_free, b + 1)
                act.wait_ge(down_done, b * DNC + DNC)
                for h in range(2):
                    nc.scalar.activation(y_sb[:, h * 512:(h + 1) * 512], ps[0:BT, 6 + h, :], ACT.Copy,
                                         scale=gate_c[:, 0:1]).then_inc(y_ready, 1)

            with act.Fori(0, E) as e:
                first = act.value_load(starti[0:1, bass.ds(e, 1)], min_val=0, max_val=MAXB - 1)
                end = act.value_load(starti[0:1, bass.ds(e + 1, 1)], min_val=1, max_val=MAXB - 1)
                with act.Fori(first, end) as b:
                    def hi(p):
                        c = p // PC
                        if p % PC == 0:
                            act.wait_ge(ring_in[c], (e + (uses[c] + 1)) * 16)
                        act.wait_ge(piece_used, b * (GUC * PC) + (p + 1))
                        nc.scalar.activation(w_hi[:, p % NB], chunk_slot(c)[:, p % PC * KP:(p % PC + 1) * KP, :],
                                             ACT.Copy).then_inc(hi_ready, 1)

                    def hT_out(c):
                        act.wait_ge(h_turned, b * GUC + (c + 3))
                        nc.scalar.activation(hT[:, 2 * c:2 * c + 2, :],
                                             ps[:, 2 + c % 2, 0:2 * BT].rearrange("p (k n) -> p k n", k=2),
                                             ACT.Copy).then_inc(hT_ready, 1)

                    act.wait_ge(x_turned, b + 1)
                    nc.scalar.activation(x_hi, ps[:, 4:6, :].rearrange("p a n -> p (a n)"), ACT.Copy)\
                        .then_inc(x_hi_ready, 1)
                    for p in range(PC):
                        hi(p)
                    results_out(b)
                    for c in range(GUC):
                        if c < GUC - 1:
                            for p in range(PC * (c + 1), PC * (c + 2)):
                                hi(p)
                                if c >= 1 and p % PC == 1:
                                    hT_out(c - 1)
                        else:
                            hT_out(c - 1)
                            act.wait_ge(ring_in[GUC], (e + (uses[GUC] + 1)) * 16)
                            nc.scalar.sem_inc(down_in, 1)
                        act.wait_ge(gate_ready, b * GUC + c + 1)
                        nc.scalar.activation(sig_b[:, c % 2], gate_b[:, c % 2], ACT.Sigmoid, scale=ALPHA)\
                            .then_inc(sig_ready, 1)
                    hT_out(GUC - 1)
                    act.wait_ge(ring_in[GUC + 1], (e + (uses[GUC + 1] + 1)) * 16)
                    nc.scalar.sem_inc(down_in, 1)
            total = act.value_load(starti[0:1, E:E + 1], min_val=1, max_val=MAXB - 1)
            results_out(total)
            act.wait_ge(h2_in, 16)
            act.wait_ge(x_turned, total + 1)
            for t in range(TB):
                link(nc.scalar.activation(junk, x_sb[:, t, :], ACT.Square, accum_out=ss[:, t:t + 1]))
            nc.scalar.activation(rs[:, :], ss[:, :], ACT.Sqrt, bias=epsc[:, 0:1], scale=1.0 / D)\
                .then_inc(roots, 1)
            for t in range(TB):
                for h in range(2):
                    act.wait_ge(turned, 16 + 2 * t + h + 1)
                    nc.scalar.activation(uT[:, 4 * h:4 * h + 4, t * P:(t + 1) * P],
                                         ps[:, 4 + (2 * t + h) % 4, :].rearrange("p (k s) -> p k s", k=4),
                                         ACT.Copy).then_inc(turned_out, 1)
            for i in range(2 * TB):
                act.wait_ge(pg, i + 1)
                if i >= 4:
                    act.wait_ge(h3_half, i - 3)
                nc.scalar.activation(sg[:, i % 4, :], ps[:, i % 4, :], ACT.Sigmoid).then_inc(pg_sig, 1)
            for t in range(TB):
                act.wait_ge(h3_half, 2 * t + 2)
                link(nc.scalar.activation(junk, x_sb[:, t, :], ACT.Square, accum_out=ss[:, t:t + 1]))
                nc.scalar.activation(rs[:, t:t + 1], ss[:, t:t + 1], ACT.Sqrt, bias=epsc[:, 0:1],
                                     scale=1.0 / D).then_inc(roots, 1)

        @block.vector
        def _(dve):
            n = 0

            def link(ins):
                nonlocal n
                n += 1
                ins.then_inc(dve_step, 1)
                dve.wait_ge(dve_step, n)

            def norm(src, dst, g):
                for t in range(TB):
                    nc.vector.scalar_tensor_tensor(dst[:, t, :], src[:, t, :], rr[:, t:t + 1], g[:, :],
                                                   ALU.mult, ALU.mult).then_inc(normed, 1)

            dve.wait_ge(roots, 1)
            dve.wait_ge(gains_in[0], 16)
            link(nc.vector.reciprocal(rr[:, :], rs[:, :]))
            norm(x_sb, x_sb, gB[0])
            dve.wait_ge(setup_tr, 1)
            nc.vector.tensor_copy(cvec[:, :, :], ps[:, 0, 0:CT * (TAPS + 3)].rearrange("p (t j) -> p t j", t=CT))\
                .then_inc(setup_out, 1)
            link(nc.vector.tensor_tensor(eye2[:, :], ident[0:2 * E, 0:E], ident[0:2 * E, E:2 * E], ALU.add))
            dve.wait_ge(small_in, SMALL)
            link(nc.vector.tensor_tensor(lprod, lamb[:, 0:4:2, :], lamb[:, 1:4:2, :], ALU.mult))
            nc.vector.tensor_reduce(lam2[:, :], lprod, AX_X, ALU.add).then_inc(lam_dot, 1)
            for t in range(CT):
                dve.wait_ge(proj_out, CT + t + 1)
                nc.vector.tensor_tensor(z[:, t, PAD:PAD + S], z[:, t, PAD:PAD + S], sg[:, t, :], ALU.mult)\
                    .then_inc(z_ready, 1)
            dve.wait_ge(setup_out, 1)
            for t in range(CT):
                dve.wait_ge(z_ready, t + 1)
                nc.vector.tensor_scalar(conv[:, t, :], z[:, t, 0:S], cvec[:, t, 0:1],
                                        cvec[:, t, TAPS:TAPS + 1], ALU.mult, ALU.add).then_inc(conv_tap, 1)
            with dve.Fori(1, TAPS) as j:
                for t in range(CT):
                    dve.wait_ge(conv_tap, j * CT + (t + 1 - CT))
                    nc.vector.scalar_tensor_tensor(conv[:, t, :], z[:, t, bass.ds(j, S)],
                                                   cvec[:, t, bass.ds(j, 1)], conv[:, t, :],
                                                   ALU.mult, ALU.add).then_inc(conv_tap, 1)
            dve.wait_ge(conv_tap, TAPS * CT)
            dve.wait_ge(lam_exp, 1)
            link(nc.vector.tensor_tensor(nlam[:, 0:1], lame[:, 1:2], lame[:, 0:1], ALU.subtract))
            link(nc.vector.tensor_scalar(nlam[:, 1:2], nlam[:, 0:1], -LAM_INIT, None, ALU.add))

            def maxes(i):
                w = (i % TB + 1) * P
                s2 = ps[:, 4 + 2 * (i % 2):6 + 2 * (i % 2), :]
                dve.wait_ge(scores, i + 1)
                link(nc.vector.tensor_tensor(s2[:, :, w - P:w], s2[:, :, w - P:w],
                                             cmask[:, :].unsqueeze(1).to_broadcast([P, 2, P]), ALU.add))
                if i >= 2:
                    dve.wait_ge(exped, 2 * (i - 1))
                link(nc.vector.tensor_reduce(mx[:, i % 2, :], s2[:, :, 0:w], AX_X, ALU.max))
                nc.vector.tensor_scalar(nmx[:, i % 2, :], mx[:, i % 2, :], -1.0, None, ALU.mult)\
                    .then_inc(maxed, 1)

            def mix(i):
                w = (i % TB + 1) * P
                b = i % 2
                dve.wait_ge(exped, 2 * i + 2)
                link(nc.vector.reciprocal(rden[:, b, :], den[:, b, :]))
                link(nc.vector.tensor_tensor(nrl[:, b:b + 1], rden[:, b, 1:2], nlam[:, 1:2], ALU.mult))
                link(nc.vector.tensor_scalar(ex[:, b, 0, 0:w], ex[:, b, 0, 0:w], rden[:, b, 0:1], None, ALU.mult))
                nc.vector.scalar_tensor_tensor(ex[:, b, 0, 0:w], ex[:, b, 1, 0:w], nrl[:, b:b + 1],
                                               ex[:, b, 0, 0:w], ALU.mult, ALU.add).then_inc(mixed, 1)

            NI = H * TB
            for i in range(NI + 1):
                if i < NI:
                    maxes(i)
                if i >= 1:
                    mix(i - 1)
                if i == 2:
                    dve.wait_ge(conv_mean, 1)
                    link(nc.vector.tensor_scalar(R2[:, 2048:2048 + S], ps[:, 3, :], 1.0 / CW, None, ALU.mult))
                    for t in range(CT):
                        nc.vector.tensor_tensor(conv[:, t, :], conv[:, t, :], R2[:, 2048:2048 + S], ALU.subtract)\
                            .then_inc(conv_c, 1)
            dve.wait_ge(conv_sd, 1)
            link(nc.vector.reciprocal(ex[:, 0, 1, :], ex[:, 0, 0, :]))
            for t in range(CT):
                nc.vector.tensor_tensor(conv[:, t, :], conv[:, t, :], ex[:, 0, 1, :], ALU.mult).then_inc(conv_n, 1)
            dve.wait_ge(o_root, 1)
            link(nc.vector.reciprocal(orr[:, :, :], ors[:, :, :]))
            for h in range(H):
                for t in range(TB):
                    o = o_tok[:, t, h * HD:(h + 1) * HD]
                    nc.vector.scalar_tensor_tensor(o, o, orr[:, t, h:h + 1], gsub[:, :], ALU.mult, ALU.mult)\
                        .then_inc(o_normed, 1)
            for t in range(CT):
                dve.wait_ge(conv_ready, t + 1)
                link(nc.vector.tensor_scalar(conv[:, t, :], conv[:, t, :], cvec[:, t, TAPS + 1:TAPS + 2],
                                             cvec[:, t, TAPS + 2:TAPS + 3], ALU.mult, ALU.add))
                nc.vector.tensor_tensor(conv[:, t, :], conv[:, t, :], sg[:, t, :], ALU.mult).then_inc(conv_out, 1)
            for k in range(KD):
                b = 4 * ((k + 1) % 2)
                dve.wait_ge(gates_sig, 2 * k + 2)
                dve.wait_ge(branch, k + 1)
                link(nc.vector.tensor_tensor(mT[:, k, :], ex[:, k % 2, 0, :], ps[:, b + 2, :], ALU.mult))
                link(nc.vector.tensor_tensor(sg[:, k % 2, :], ex[:, k % 2, 1, :], ps[:, b + 3, :], ALU.mult))
                nc.vector.tensor_tensor(mT[:, k, :], mT[:, k, :], sg[:, k % 2, :], ALU.add).then_inc(m_ready, 1)
            dve.wait_ge(x_again, 16)
            dve.wait_ge(gains_in[1], 16)
            for t in range(TB):
                for h in range(2):
                    i = 2 * t + h
                    dve.wait_ge(wo_done, i + 1)
                    xs = x_sb[:, t, h * 512:(h + 1) * 512]
                    nc.vector.tensor_tensor(xs, xs, ps[:, i % 4, :], ALU.add).then_inc(h1_half, 1)
                dve.wait_ge(roots, 1 + t + 1)
                link(nc.vector.reciprocal(rr[:, t:t + 1], rs[:, t:t + 1]))
                nc.vector.scalar_tensor_tensor(u_tok[:, t, :], x_sb[:, t, :], rr[:, t:t + 1], gB[1][:, :],
                                               ALU.mult, ALU.mult).then_inc(normed, 1)
            dve.wait_ge(logits, 1)
            link(nc.vector.tensor_tensor(lg, ps[:, 0, 0:TB * E].rearrange("p (t e) -> p t e", t=TB),
                                         b_rt[:, :].unsqueeze(1).to_broadcast([P, TB, E]), ALU.add))
            for t in range(TB):
                link(nc.vector.max(top[:, t, :], lg[:, t, :]))
            nc.vector.tensor_tensor(gd[:, :, :], top[:, :, 0:TOP],
                                    top[:, :, 0:1].to_broadcast([P, TB, TOP]), ALU.subtract)\
                .then_inc(top_ready, 1)
            for t in range(TB):
                link(nc.vector.max_index(topi[:, t, :], top[:, t, :], lg[:, t, :]))
            link(nc.vector.tensor_copy(topf[:, :, :], topi[:, :, 0:TOP]))
            for t in range(TB):
                link(nc.vector.tensor_tensor(eq[:, t], iota[:, 0:E].unsqueeze(1).to_broadcast([P, TOP, E]),
                                             topf[:, t, :].unsqueeze(2).to_broadcast([P, TOP, E]),
                                             ALU.is_equal))
            nc.vector.tensor_reduce(mask, eq.rearrange("p t k e -> p t e k"), AX_X, ALU.add)\
                .then_inc(mask_ready, 1)
            dve.wait_ge(gexp, 1)
            link(nc.vector.tensor_reduce(gs[:, :], ge[:, :, :], AX_X, ALU.add))
            link(nc.vector.reciprocal(gr[:, :], gs[:, :]))
            link(nc.vector.tensor_tensor(gate[:, :, :], ge[:, :, :],
                                         gr[:, :].unsqueeze(2).to_broadcast([P, TB, TOP]), ALU.mult))
            for t in range(TB):
                link(nc.vector.tensor_tensor(eqs[:, t], eq[:, t],
                                             gate[:, t, :].unsqueeze(2).to_broadcast([P, TOP, E]), ALU.mult))
            nc.vector.tensor_reduce(gdense[:, :, :], eqs.rearrange("p t k e -> p t e k"), AX_X, ALU.add)\
                .then_inc(gd_ready, 1)
            dve.wait_ge(gd_ready, 1)
            dve.wait_ge(counts, 1)
            cnt = ps[:, 1, TB * E:(TB + 1) * E]
            for a in range(TB - 1):
                nc.vector.tensor_scalar(big[:, a, :], cnt, float(BT * (a + 1)), None, ALU.is_gt)\
                    .then_inc(dve_step, 1)
            n += TB - 1
            dve.wait_ge(dve_step, n)
            link(nc.vector.tensor_reduce(nblk[:, :], big.rearrange("p a e -> p e a"), AX_X, ALU.add))
            link(nc.vector.tensor_scalar(nblk[:, :], nblk[:, :], 1.0, None, ALU.add))
            link(nc.vector.memset(startf[:, 0:1], 0.0))
            link(nc.vector.tensor_tensor_scan(startf[:, 1:E + 1], ones[:, 0:E], nblk[:, :], 0.0, ALU.mult, ALU.add))
            link(nc.vector.tensor_copy(starti[:, :], startf[:, :]))
            for t in range(TB):
                link(nc.vector.scalar_tensor_tensor(slot[:, t, :], startf[:, 0:E], float(BT),
                                                    ps[:, 1, t * E:(t + 1) * E], ALU.mult, ALU.add))
            for t in range(TB):
                link(nc.vector.tensor_tensor(eqs[:, t], eq[:, t],
                                             slot[:, t, :].unsqueeze(1).to_broadcast([P, TOP, E]), ALU.mult))
            link(nc.vector.tensor_reduce(slk[:, :].rearrange("p (t k) -> p t k", t=TB), eqs, AX_X, ALU.add))
            link(nc.vector.tensor_copy(sli[:, :], slk[:, :]))
            link(nc.vector.tensor_scalar(slj[:, 0, :], sli[:, :], BT - 1, None, ALU.bitwise_and))
            link(nc.vector.tensor_scalar(slj[:, 1, :], sli[:, :], BT.bit_length() - 1, None, ALU.logical_shift_right))
            link(nc.vector.tensor_copy(slf[:, :, :], slj[:, :, :]))
            dve.wait_ge(u_stored, 16)
            nj = TB * TOP
            link(nc.vector.tensor_tensor(oh_j.rearrange("p t k j -> p (t k) j"),
                                         iota[:, :].unsqueeze(1).to_broadcast([P, nj, BT]),
                                         slf[:, 0, :].unsqueeze(2).to_broadcast([P, nj, BT]), ALU.is_equal))
            link(nc.vector.tensor_tensor(oh_r[:, :, :, 2, :].rearrange("p t k b -> p (t k) b"),
                                         iota[:, 0:MAXB].unsqueeze(1).to_broadcast([P, nj, MAXB]),
                                         slf[:, 1, :].unsqueeze(2).to_broadcast([P, nj, MAXB]), ALU.is_equal))
            link(nc.vector.tensor_tensor(oh_r[:, :, :, 1, :].rearrange("p t k b -> p (t k) b"),
                                         oh_r[:, :, :, 2, :].rearrange("p t k b -> p (t k) b"),
                                         gate[:, :, :].rearrange("p t k -> p (t k)").unsqueeze(2)
                                         .to_broadcast([P, nj, MAXB]), ALU.mult))
            for t in range(TB):
                nc.vector.tensor_scalar(oh_r[:, t, :, 0, :], oh_r[:, t, :, 2, :], tokid[:, t:t + 1], None, ALU.mult)\
                    .then_inc(onehots, 1)
            link(nc.vector.tensor_tensor(own[:, 0, :], startf[0:2 * E, 0:E], eye2[:, :], ALU.mult))
            link(nc.vector.tensor_tensor(own[:, 1, :], startf[0:2 * E, 1:E + 1], eye2[:, :], ALU.mult))
            link(nc.vector.tensor_reduce(bounds[:, :], own[:, :, :], AX_X, ALU.add))
            for a in range(2):
                link(nc.vector.tensor_scalar(sel2[:, a, :], iota[0:2 * E, 0:MAXB], bounds[:, a:a + 1], None,
                                             ALU.is_ge))
            link(nc.vector.tensor_tensor(sel_tab[:, :], sel2[:, 0, :], sel2[:, 1, :], ALU.subtract))
            dve.wait_ge(table, 1)
            tab = ps[0:BT, 7, 0:3 * MAXB].rearrange("p (a b) -> p a b", a=3)
            link(nc.vector.tensor_copy(tabf[:, 0, :], tab[:, 0, :]))
            link(nc.vector.tensor_copy(gate_tab[:, :], tab[:, 1, :]))
            link(nc.vector.tensor_scalar(inval, tab[:, 2, :], -1.0, 1.0, ALU.mult, ALU.add))
            link(nc.vector.scalar_tensor_tensor(tabf[:, 1, :], inval, spare[:, 0:1], tabf[:, 0, :],
                                                ALU.mult, ALU.add))
            link(nc.vector.tensor_copy(from_tab[:, :], tabf[:, 0, :]))
            nc.vector.tensor_copy(to_tab[:, :], tabf[:, 1, :]).then_inc(tables, 1)
            for i in range(2 * TB):
                dve.wait_ge(bdn, i + 1)
                xs = x_sb[:, i // 2, (i % 2) * 512:(i % 2 + 1) * 512]
                nc.vector.tensor_tensor(xs, xs, ps[:, 2 + i % 2, :], ALU.add).then_inc(base_ready, 1)
            dve.wait_ge(tables, 1)
            nc.vector.sem_inc(gu_read, 2)
            nc.vector.sem_inc(lo_ready, GUC * PC)
            dve.wait_ge(bgu_hi, 1)
            nc.vector.tensor_tensor(bgu_parts[E:2 * E, :], bgu[E:2 * E, :], bgu_parts[E:2 * E, :].bitcast(F32),
                                    ALU.subtract).then_inc(bgu_split, 1)
            total = dve.value_load(starti[0:1, E:E + 1], min_val=1, max_val=MAXB - 1)
            with dve.Fori(0, total) as b:
                def lo(p):
                    c = p // PC
                    dve.wait_ge(hi_ready, b * (GUC * PC) + (p + 1))
                    nc.vector.tensor_tensor(w_lo[:, p % NB], chunk_slot(c)[:, p % PC * KP:(p % PC + 1) * KP, :],
                                            w_hi[:, p % NB].bitcast(F32), ALU.subtract).then_inc(lo_ready, 1)

                lo(0)
                dve.wait_ge(x_hi_ready, b + 1)
                dve.wait_ge(bgu_split, 1)
                nc.vector.tensor_tensor(x_lo, ps[:, 4:6, :].rearrange("p a n -> p (a n)"), x_hi.bitcast(F32),
                                        ALU.subtract).then_inc(x_split, 1)
                for p in range(1, PC):
                    lo(p)
                dve.wait_ge(sum_stored, 32)
                for c in range(GUC):
                    o = c % 2
                    if c < GUC - 1:
                        for p in range(PC * (c + 1), PC * (c + 2)):
                            lo(p)
                    dve.wait_ge(gu_done, b * GUC + (c + 1))
                    g2 = ps[0:BT, c % 2, :].rearrange("p (n g) -> p g n", g=2)
                    nc.vector.tensor_scalar(gate_b[:, o], g2[:, 0, :], LIMIT, None, ALU.min)\
                        .then_inc(gate_ready, 1)
                    nc.vector.tensor_scalar(lin_b[:, o], g2[:, 1, :], LIMIT, -LIMIT, ALU.min, ALU.max)\
                        .then_inc(gu_read, 1)
                    dve.wait_ge(gate_ready, b * GUC + c + 1)
                    dve.wait_ge(gu_read, b * GUC + (c + 3))
                    nc.vector.scalar_tensor_tensor(lg_b[:, o], lin_b[:, o], 1.0, gate_b[:, o],
                                                   ALU.add, ALU.mult).then_inc(dve_block, 1)
                    dve.wait_ge(dve_block, b * GUC + (c + 1))
                    dve.wait_ge(sig_ready, b * GUC + (c + 1))
                    dve.wait_ge(h_turned, b * GUC + (c + 1))
                    nc.vector.tensor_tensor(h_tok[:, o], lg_b[:, o], sig_b[:, o], ALU.mult)\
                        .then_inc(h_ready, 1)
            dve.wait_ge(roots, 1 + TB + 1)
            dve.wait_ge(gains_in[0], 32)
            link(nc.vector.reciprocal(rr[:, :], rs[:, :]))
            norm(x_sb, u_tok, gB[0])
            dve.wait_ge(gains_in[1], 32)
            for i in range(2 * TB):
                t = i // 2
                sl = slice((i % 2) * 512, (i % 2 + 1) * 512)
                dve.wait_ge(pg_sig, i + 1)
                link(nc.vector.tensor_tensor(sg[:, i % 4, :], sg[:, i % 4, :], pple[:, t, sl], ALU.mult))
                nc.vector.tensor_tensor(x_sb[:, t, sl], x_sb[:, t, sl], sg[:, i % 4, :], ALU.add)\
                    .then_inc(h3_half, 1)
            for t in range(TB):
                dve.wait_ge(roots, TB + 3 + t)
                dve.wait_ge(turned, 24)
                link(nc.vector.reciprocal(rr[:, t:t + 1], rs[:, t:t + 1]))
                nc.vector.scalar_tensor_tensor(u_tok[:, t, :], x_sb[:, t, :], rr[:, t:t + 1], gB[1][:, :],
                                               ALU.mult, ALU.mult).then_inc(out_ready, 1)

        @block.tensor
        def _(pe):
            def mm(o, a, b, start, stop, **kw):
                return nc.tensor.matmul(o, a, b, start=start, stop=stop, **kw)

            def arrived(name):
                i = at[name]
                pe.wait_ge(ring_in[i % SLOTS], 16 * (i // SLOTS + 1))

            def turn_rows(src, i):
                t, h = i // 2, i % 2
                for k in range(4):
                    last = nc.tensor.transpose(ps[:, 4 + i % 4, k * P:(k + 1) * P],
                                               src[:, t, (4 * h + k) * P:(4 * h + k + 1) * P], ident[:, :])
                last.then_inc(turned, 1)

            def weights(name, k):
                n = 8 if k == KD else k
                return flat(slot_of(name)[:, 0:n * (4096 // n)], n)

            pe.wait_ge(consts, 9)
            pe.wait_ge(small_in, SMALL)
            for t in range(CT):
                last = nc.tensor.transpose(ps[:, 0, t * (TAPS + 3):(t + 1) * (TAPS + 3)],
                                           vecs[:, t * P:(t + 1) * P], ident[0:TAPS + 3, 0:TAPS + 3])
            last.then_inc(setup_tr, 1)
            for i in range(2 * TB):
                if i % 2 == 0:
                    pe.wait_ge(normed, i // 2 + 1)
                if i >= 4:
                    pe.wait_ge(turned_out, i - 3)
                turn_rows(x_sb, i)
            pe.wait_ge(turned_out, 8)
            pe.wait_ge(setup_out, 1)
            for i in range(20):
                name = ("conv_a", "conv_g", "q", "k", "v")[i // 4]
                if i % 4 == 0:
                    arrived(name)
                if i >= 4:
                    pe.wait_ge(proj_out, i - 3)
                w = weights(name, KD)
                for k in range(KD):
                    cs = slice((i % 4) * P, (i % 4 + 1) * P)
                    if name == "v":
                        last = mm(ps[:, i % 4, :], uT[:, k, cs], w[:, k, :], k == 0, k == KD - 1)
                    else:
                        last = mm(ps[:, i % 4, :], w[:, k, cs], uT[:, k, :], k == 0, k == KD - 1)
                last.then_inc(proj, 1)
            pe.wait_ge(proj_out, 20)
            NI = H * TB

            def score(i):
                h, t = i // TB, i % TB
                w = (t + 1) * P
                if i >= 2:
                    pe.wait_ge(exped, 2 * (i - 1))
                for c in range(2):
                    last = mm(ps[:, 4 + 2 * (i % 2) + c, 0:w], qT[c * QD:(c + 1) * QD, h, t * P:(t + 1) * P],
                              kT[c * QD:(c + 1) * QD, h, 0:w], True, True)
                last.then_inc(scores, 1)

            def turn_a(i):
                t = i % TB
                pe.wait_ge(mixed, i + 1)
                if i >= 2:
                    pe.wait_ge(a_out, i - 1)
                for k in range(t + 1):
                    last = nc.tensor.transpose(ps[:, i % 2, k * P:(k + 1) * P],
                                               ex[:, i % 2, 0, k * P:(k + 1) * P], ident[:, :])
                last.then_inc(a_turned, 1)

            def apply_v(i):
                h, t = i // TB, i % TB
                pe.wait_ge(a_out, i + 1)
                if i >= 1:
                    pe.wait_ge(o_sq, i)
                for k in range(t + 1):
                    last = mm(ps[:, 2, (i % 4) * P:(i % 4 + 1) * P], a_T[:, i % 2, k * P:(k + 1) * P],
                              v_sb[:, k, h * HD:(h + 1) * HD], k == 0, k == t)
                last.then_inc(pv, 1)

            for i in range(NI + 2):
                if i < NI:
                    score(i)
                if i == 2:
                    pe.wait_ge(conv_tap, TAPS * CT)
                    for t in range(CT):
                        last = mm(ps[:, 3, :], ones[:, :], conv[:, t, :], t == 0, t == CT - 1)
                    last.then_inc(conv_mean, 1)
                if 1 <= i <= NI:
                    turn_a(i - 1)
                if i >= 2:
                    apply_v(i - 2)
            pe.wait_ge(conv_sq, CT)
            for t in range(CT):
                last = mm(ps[:, 3, :], ones[:, :], sg[:, t, :], t == 0, t == CT - 1)
            last.then_inc(conv_var, 1)

            def gate_pair(k):
                b = 4 * ((k + 1) % 2)
                if k >= 2:
                    pe.wait_ge(m_ready, k - 1)
                for c, nm in enumerate(("ga", "gb")):
                    name = f"{nm}{k // 4}"
                    arrived(name)
                    w = weights(name, KD)
                    cs = slice((k % 4) * P, (k % 4 + 1) * P)
                    for j in range(KD):
                        last = mm(ps[:, b + c, :], w[:, j, cs], uT[:, j, :], j == 0, j == KD - 1)
                last.then_inc(gates, 1)

            gate_pair(0)
            pe.wait_ge(conv_sd, 1)
            for h in range(H):
                pe.wait_ge(o_normed, TB * (h + 1))
                for t in range(TB):
                    last = nc.tensor.transpose(ps[:, h, t * P:(t + 1) * P], o_tok[:, t, h * HD:(h + 1) * HD],
                                               ident[:, :])
                last.then_inc(o_turned, 1)
            for k in range(KD):
                if k >= 1:
                    if k == 1:
                        pe.wait_ge(o_out, H)
                    gate_pair(k)
                b = 4 * ((k + 1) % 2)
                if k == 0:
                    pe.wait_ge(o_out, H)
                    pe.wait_ge(conv_out, CT)
                for c, (name, src) in enumerate((("ao", o_T), ("co", conv))):
                    arrived(name)
                    w = weights(name, AW // P)
                    for j in range(AW // P):
                        last = mm(ps[:, b + 2 + c, :], w[:, j, k * P:(k + 1) * P], src[:, j, :],
                                  j == 0, j == AW // P - 1)
                last.then_inc(branch, 1)
            def wo(t):
                for h in range(2):
                    i = 2 * t + h
                    arrived(f"wo{h}")
                    if i >= 4:
                        pe.wait_ge(h1_half, i - 3)
                    w = weights(f"wo{h}", KD)
                    for j in range(KD):
                        last = mm(ps[:, i % 4, :], mT[:, j, t * P:(t + 1) * P], w[:, j, :], j == 0, j == KD - 1)
                    last.then_inc(wo_done, 1)

            def turn_u(t):
                pe.wait_ge(normed, TB + t + 1)
                for i in (2 * t, 2 * t + 1):
                    if i >= 4:
                        pe.wait_ge(turned_out, 8 + i - 3)
                    turn_rows(u_tok, i)

            pe.wait_ge(m_ready, KD)
            for t in range(TB):
                wo(t)
                if t >= 1:
                    turn_u(t - 1)
            turn_u(TB - 1)
            pe.wait_ge(turned_out, 16)
            pe.wait_ge(h1_half, 2 * TB)
            for t in range(TB):
                for j in range(KD):
                    last = mm(ps[:, 0, t * E:(t + 1) * E], uT[:, j, t * P:(t + 1) * P], w_rt[:, j, :],
                              j == 0, j == KD - 1)
            last.then_inc(logits, 1)
            arrived("ple")
            pe.wait_ge(p_in, 16)
            for k in range(PLE // P):
                for t in range(TB):
                    last = nc.tensor.transpose(ps[:, 2 + k, t * P:(t + 1) * P], p_sb[:, t, k * P:(k + 1) * P],
                                               ident[:, :])
                last.then_inc(ptr, 1)
            pe.wait_ge(mask_ready, 1)
            for t in range(TB):
                for a in range(t):
                    mm(ps[:, 1, t * E:(t + 1) * E], ones[:, :], mask[:, a, :], a == 0, False)
                mm(ps[:, 1, t * E:(t + 1) * E], before[:, :], mask[:, t, :], t == 0, True)
            for a in range(TB):
                last = mm(ps[:, 1, TB * E:(TB + 1) * E], ones[:, :], mask[:, a, :], a == 0, a == TB - 1)
            last.then_inc(counts, 1)
            pe.wait_ge(pT_out, 2)
            for i in range(2 * TB):
                t, h = i // 2, i % 2
                if i >= 2:
                    pe.wait_ge(ple_out, i - 1)
                for k in range(PLE // P):
                    last = mm(ps[:, 4 + h, :], pT[:, k, t * P:(t + 1) * P], w_ple_sb[:, k, h * 512:(h + 1) * 512],
                              k == 0, k == PLE // P - 1)
                last.then_inc(ple_mm, 1)
            pe.wait_ge(gd_ready, 1)
            for t in range(TB):
                last = nc.tensor.transpose(ps[0:E, 6, t * P:(t + 1) * P], gdense[:, t, :], ident[:, :])
            last.then_inc(gd_turned, 1)
            pe.wait_ge(onehots, TB)
            tab = ps[0:BT, 7, 0:3 * MAXB]
            for i in range(TB * TOP):
                t, k = i // TOP, i % TOP
                last = mm(tab, oh_j[:, t, k, :], oh_r[:, t, k, :, :].rearrange("p a b -> p (a b)"),
                          i == 0, i == TB * TOP - 1)
            last.then_inc(table, 1)
            pe.wait_ge(gdT_out, 1)
            pe.wait_ge(bdn_in, 16)
            for i in range(2 * TB):
                t, h = i // 2, i % 2
                if i >= 2:
                    pe.wait_ge(base_ready, i - 1)
                mm(ps[:, 2 + h, :], gdT[:, t * P:(t + 1) * P], b_dn[:, h * 512:(h + 1) * 512], True, True)\
                    .then_inc(bdn, 1)
            pe.wait_ge(tables, 1)
            pe.wait_ge(base_ready, 2 * TB)
            pe.wait_ge(ple_out, 2 * TB)

            def turn_x():
                for k in range(KD):
                    last = nc.tensor.transpose(ps[:, 4 + k // 4, (k % 4) * BT:(k % 4 + 1) * BT],
                                               xg[:, k * P:(k + 1) * P], ident[:, :])
                last.then_inc(x_turned, 1)

            nc.tensor.sem_inc(piece_used, NB)
            nc.tensor.sem_inc(h_turned, 2)
            nc.tensor.sem_inc(hT_ready, 2)
            nc.tensor.sem_inc(down_done, DNC)
            pe.wait_ge(gathered, 16)
            turn_x()
            pe.wait_ge(bgu_split, 1)
            x_hi3 = x_hi.rearrange("p (k n) -> p k n", k=KD)
            x_lo3 = x_lo.rearrange("p (k n) -> p k n", k=KD)
            total = pe.value_load(starti[0:1, E:E + 1], min_val=1, max_val=MAXB - 1)
            with pe.Fori(0, total) as b:
                def turn_h(c):
                    pe.wait_ge(h_ready, b * GUC + (c + 1))
                    pe.wait_ge(hT_ready, b * GUC + (c + 1))
                    nc.tensor.sem_inc(passed["pe"], 1)
                    for k in range(2):
                        last = nc.tensor.transpose(ps[:, 2 + c % 2, k * BT:(k + 1) * BT],
                                                   h_tok[:, c % 2, k * P:(k + 1) * P], ident[:, :])
                    last.then_inc(h_turned, 1)

                for c in range(GUC):
                    o = ps[:, c % 2, :]
                    for p in range(PC * c, PC * (c + 1)):
                        pe.wait_ge(lo_ready, b * (GUC * PC) + (p + 1 + GUC * PC))
                        if p == 0:
                            pe.wait_ge(x_split, b + 1)
                        if p % PC == 0:
                            pe.wait_ge(gu_read, b * GUC + (c + 1))
                        for j in range(KP):
                            k = p % PC * KP + j
                            mm(o, x_hi3[:, k, :], w_hi[:, p % NB, j, :], k == 0, False)
                            mm(o, x_lo3[:, k, :], w_hi[:, p % NB, j, :], False, False)
                            last = mm(o, x_hi3[:, k, :], w_lo[:, p % NB, j, :], False, False)
                        last.then_inc(piece_used, 1)
                    if c == 0:
                        pe.wait_ge(sel_ready, b + 1)
                    mm(o, sel_c[:, :], bgu_parts[:, c * 512:(c + 1) * 512], False, True).then_inc(gu_done, 1)
                    if c >= 1:
                        turn_h(c - 1)

                def down(i):
                    c = i // 4
                    if i % 4 == 0:
                        pe.wait_ge(down_in, b * DNC + (c + 1))
                    if i % 2 == 0:
                        pe.wait_ge(hT_ready, b * GUC + (i // 2 + 3))
                    if i == 0:
                        pe.wait_ge(y_ready, b * 2 + 2)
                    w = chunk_slot(GUC + c)
                    for k in range(2):
                        last = mm(ps[:, 6 + k, :], hT[:, i, :], w[:, i % 4, k * BANK:(k + 1) * BANK],
                                  i == 0, i == FT - 1)
                    if i % 4 == 3:
                        last.then_inc(down_done, 1)

                for i in range(FT):
                    down(i)
                    if i == 1:
                        turn_h(GUC - 1)
                        pe.wait_ge(gathered, (b + 2) * 16)
                        nc.tensor.sem_inc(passed["pe"], 1)
                        turn_x()
            for i in range(2 * TB):
                if i % 2 == 0:
                    pe.wait_ge(normed, 2 * TB + i // 2 + 1)
                if i >= 4:
                    pe.wait_ge(turned_out, 16 + i - 3)
                turn_rows(u_tok, i)
            pe.wait_ge(turned_out, 24)
            for i in range(2 * TB):
                t, h = i // 2, i % 2
                if i < 2:
                    pe.wait_ge(ring_in[h], 16 * (uses[h] + E + 1))
                if i >= 4:
                    pe.wait_ge(pg_sig, i - 3)
                w = flat(ring[:, h, :], KD)
                for j in range(KD):
                    last = mm(ps[:, i % 4, :], uT[:, j, t * P:(t + 1) * P], w[:, j, :], j == 0, j == KD - 1)
                last.then_inc(pg, 1)


_INS = ["x", "p", "g_mix", "w_in", "lambda_q1", "lambda_k1", "lambda_q2", "lambda_k2", "g_subln",
        "w_attn_out", "w_dw", "b_dw", "g_conv_ln", "b_conv_ln", "w_conv_out", "w_o", "g_ffn",
        "w_router", "b_router", "w_gate_up", "b_gate_up", "w_down", "b_down",
        "w_ple", "g_ple", "w_ple_gate", "g_final"]


def kernel(**inputs):
    import numpy as np
    import concourse.bacc as bacc
    from concourse.bass_utils import run_bass_kernel_spmd

    nc = bacc.Bacc("TRN2", target_bir_lowering=False, num_devices=1)
    arrays, args = {}, []
    for name in _INS:
        a = np.ascontiguousarray(inputs[name])
        arrays[f"in_{name}"] = a
        args.append(nc.dram_tensor(f"in_{name}", a.shape, mybir.dt.from_np(a.dtype), kind="ExternalInput").ap())
    out = nc.dram_tensor("out_rows", inputs["x"].shape, F32, kind="ExternalOutput").ap()
    trunk_layer(nc, *args, out)
    r = run_bass_kernel_spmd(nc, [arrays], core_ids=[0])
    return r.results[0]["out_rows"]
```

```python
from contextlib import ExitStack

import concourse.bass as bass
from concourse import mybir

F32 = mybir.dt.float32
F32R = mybir.dt.float32r
I32 = mybir.dt.int32
U32 = mybir.dt.uint32
ALU = mybir.AluOpType
ACT = mybir.ActivationFunctionType
AX_X = mybir.AxisListType.X

P = 128
BANK = 512
EPS = 1e-5
NEG = -1e30
SLOTS = 6
BT = P


def trunk_layer(nc, x, p, g_mix, w_in, lambda_q1, lambda_k1, lambda_q2, lambda_k2, g_subln,
                w_attn_out, w_dw, b_dw, g_conv_ln, b_conv_ln, w_conv_out, w_o, g_ffn,
                w_router, b_router, w_gate_up, b_gate_up, w_down, b_down,
                w_ple, g_ple, w_ple_gate, g_final, out):
    S, D = x.shape[1], x.shape[2]
    AW = w_attn_out.shape[1]
    CW = w_conv_out.shape[1]
    PLE = p.shape[3]
    E = w_router.shape[2]
    F = w_down.shape[2]
    TAPS = w_dw.shape[1]
    HD = g_subln.shape[1]
    H = AW // HD
    QD = HD // 2
    TOP = 4
    TB = S // P
    KD = D // P
    FT = F // P
    CT = CW // P
    PAD = TAPS - 1
    ZW = S + PAD + 2
    MAXB = S * TOP // BT + E
    SCALE = float(QD) ** -0.5
    LAM_INIT = 0.2
    ALPHA, LIMIT = 1.702, 7.0
    NB, PW, PC = 5, 1024, 4096 // 1024
    KP = KD // PC
    assert (S, D, AW, CW, E, F, H) == (512, 1024, 512, 512, 32, 1024, 4) and TB == 4

    x_t = x.rearrange("a (t q) d -> q (a t) d", q=P)
    p_t = p.rearrange("l a (t q) d -> q (l a t) d", q=P)
    out_t = out.rearrange("a (t q) d -> q (a t) d", q=P)

    u_rows = nc.dram_tensor("u_rows", (S, D), F32, kind="Internal").ap()
    sum_rows = nc.dram_tensor("sum_rows", (S + BT, D), F32, kind="Internal").ap()

    w_in_v = w_in.rearrange("l (k q) n -> q (l k) n", q=P)
    w_ao_v = w_attn_out.rearrange("l (k q) n -> q (l k) n", q=P)
    w_co_v = w_conv_out.rearrange("l (k q) n -> q (l k) n", q=P)
    w_o_v = w_o.rearrange("l (k q) n -> q (l k) n", q=P)
    w_ple_v = w_ple.rearrange("l (k q) n -> q (l k) n", q=P)
    w_pg_v = w_ple_gate.rearrange("l (k q) n -> q (l k) n", q=P)

    def cols(view, c):
        return view[:, :, c * 512:(c + 1) * 512]

    dense = [("conv_a", cols(w_in_v, 3)), ("conv_g", cols(w_in_v, 4)), ("q", cols(w_in_v, 0)),
             ("k", cols(w_in_v, 1)), ("v", cols(w_in_v, 2)),
             ("ga0", cols(w_in_v, 5)), ("gb0", cols(w_in_v, 7)), ("ao", w_ao_v), ("co", w_co_v),
             ("ga1", cols(w_in_v, 6)), ("gb1", cols(w_in_v, 8)),
             ("wo0", cols(w_o_v, 0)), ("wo1", cols(w_o_v, 1))]
    at = {name: i for i, (name, _) in enumerate(dense)}
    slots = [0, 1, 2, 3, 0, 1, 2, 3, 0, 1, 2, 1, 2]
    uses = [slots.count(s) for s in range(SLOTS)]

    def turn(name):
        return slots[:at[name] + 1].count(slots[at[name]])

    pieces = [(name, c) for name in ("conv_a", "conv_g", "q", "k", "v") for c in range(4)]
    for k in range(KD):
        pieces += [(f"ga{k // 4}", k % 4), (f"gb{k // 4}", k % 4), ("ao co", k)]

    with ExitStack() as ctx:
        def sb(name, shape, dt=F32):
            return ctx.enter_context(nc.sbuf_tensor(name, shape, dt))

        def sem(name):
            return ctx.enter_context(nc.semaphore(name))

        ps = ctx.enter_context(nc.psum_tensor("ps", [P, 8, BANK], F32))

        gB = [sb("gB0", [P, D]), sb("gB1", [P, D])]

        RW = 2048 + CT * ZW + 2048
        with ExitStack() as first_use:
            def shared(name, w):
                return first_use.enter_context(nc.sbuf_tensor(name, [P, w], F32))

            ring_flat = shared("ring", SLOTS * 4096)
            X = shared("X", TB * D)
            R1 = shared("R1", 4096)
            UT = shared("UT", KD * S)
            R2 = shared("R2", RW)
            R4 = shared("R4", 5120)
        ringr = sb("ringr", [P, SLOTS * 4096], F32R)
        ring = ring_flat[:, :].rearrange("p (s n) -> p s n", s=SLOTS)
        Xr, R1r = sb("Xr", [P, TB * D], F32R), sb("R1r", [P, 4096], F32R)
        UTr, R2r, R4r = sb("UTr", [P, KD * S], F32R), sb("R2r", [P, RW], F32R), sb("R4r", [P, 5120], F32R)

        x_sb = X[:, :].rearrange("p (t d) -> p t d", t=TB)
        o_tok = X[:, 0:2048].rearrange("p (t d) -> p t d", t=TB)
        o_hi = Xr[:, 2048:4096].rearrange("p (h s) -> p h s", h=H)
        o_lo = R2r[:, 0:2048].rearrange("p (h s) -> p h s", h=H)
        uT = UT[:, :].rearrange("p (k s) -> p k s", k=KD)
        u_hi = UTr[:, :].rearrange("p (k s) -> p k s", k=KD)
        u_lo = ringr[:, 4 * 4096:5 * 4096].rearrange("p (k s) -> p k s", k=KD)
        d_hi = [ringr[:, 5 * 4096 + i * 1024:5 * 4096 + (i + 1) * 1024] for i in (0, 1)]
        d_lo = [ringr[:, 5 * 4096 + i * 1024:5 * 4096 + (i + 1) * 1024] for i in (2, 3)]
        qT = R1[:, 0:2048].rearrange("p (h s) -> p h s", h=H)
        kT = R1[:, 2048:4096].rearrange("p (h s) -> p h s", h=H)
        vecs = R1[0:TAPS + 3, 0:512]
        lamb = R1[:, 1024:1280].rearrange("p (a n) -> p a n", a=4)
        lprod = R1[:, 1280:1408].rearrange("p (a n) -> p a n", a=2)
        mT = R1[:, :].rearrange("p (k s) -> p k s", k=KD)
        pple = R1[:, :].rearrange("p (t d) -> p t d", t=TB)
        v_sb = R2[:, 0:2048].rearrange("p (t n) -> p t n", t=TB)
        z = R2[:, 2048:2048 + CT * ZW].rearrange("p (t s) -> p t s", t=CT)
        C0 = 2048 + CT * ZW
        conv = R2[:, C0:C0 + 2048].rearrange("p (t s) -> p t s", t=CT)
        conv_hi = R2r[:, 2048:4096].rearrange("p (t s) -> p t s", t=CT)
        conv_lo = R2r[:, C0:C0 + 2048].rearrange("p (t s) -> p t s", t=CT)
        u_tok = R2[:, 0:4096].rearrange("p (t d) -> p t d", t=TB)
        ex = R4[:, 0:2048].rearrange("p (b c k) -> p b c k", b=2, c=2)
        a_T = R4[:, 2048:3072].rearrange("p (b s) -> p b s", b=2)
        sg = R4[:, 3072:5120].rearrange("p (t s) -> p t s", t=4)
        junk = R4[:, 0:D]
        xg = R4[0:BT, 0:1024]
        b_dn = R4[0:E, 2048:3072]
        y_sb = R4[0:BT, 1024:2048]
        x_hi = R4r[:, 2048:3072]
        x_lo = R4r[:, 3072:4096]
        h_hi = R4r[:, 4096:4608].rearrange("p (k n) -> p k n", k=FT // 2)
        h_lo = Xr[:, 3072:3584].rearrange("p (k n) -> p k n", k=FT // 2)
        hT = R4[:, 4608:5120].rearrange("p (k n) -> p k n", k=FT // 2)
        bgu = R4[0:2 * E, 3072:5120]
        bgu_parts = R2r[0:2 * E, 4096:6144]
        w_hi = [R2r[:, i * PW:(i + 1) * PW] for i in range(4)] + [R1r[:, 0:PW]]
        w_lo = [UTr[:, i * PW:(i + 1) * PW] for i in range(4)] + [R1r[:, PW:2 * PW]]
        gate_b, lin_b, sig_b, lg_b, h_tok = (X[:, 512 * i:512 * (i + 1)].rearrange("p (b n) -> p b n", b=2)
                                             for i in range(5))
        q0 = C0

        def rt(n):
            nonlocal q0
            q0 += n
            return R2[:, q0 - n:q0]

        lg = rt(TB * E).rearrange("p (t e) -> p t e", t=TB)
        eq = rt(TB * TOP * E).rearrange("p (t k e) -> p t k e", t=TB, k=TOP)
        eqs = rt(TB * TOP * E).rearrange("p (t k e) -> p t k e", t=TB, k=TOP)
        mask = rt(TB * E).rearrange("p (t e) -> p t e", t=TB)
        slot = rt(TB * E).rearrange("p (t e) -> p t e", t=TB)
        big = rt((TB - 1) * E).rearrange("p (a e) -> p a e", a=TB - 1)
        assert q0 <= C0 + 2048
        oh_j = UT[:, 0:16 * BT].rearrange("p (t k j) -> p t k j", t=TB, k=TOP)
        oh_r = R2[:, 0:16 * 3 * MAXB].rearrange("p (t k a b) -> p t k a b", t=TB, k=TOP, a=3)

        ident = sb("ident", [P, P])
        ones = sb("ones", [P, P])
        before = sb("before", [P, P])
        cmask = sb("cmask", [P, P])
        iota = sb("iota", [P, BT])
        tokid = sb("tokid", [P, TB])
        spare = sb("spare", [BT, 1])
        gsub = sb("gsub", [P, HD])
        cvec = sb("cvec", [P, CT, TAPS + 3])
        eye2 = sb("eye2", [2 * E, E])
        own = sb("own", [2 * E, 2, E])
        bounds = sb("bounds", [2 * E, 2])
        sel2 = sb("sel2", [2 * E, 2, MAXB])
        sel_tab = sb("sel_tab", [2 * E, MAXB])
        sel_c = sb("sel_c", [2 * E, P], F32R)
        b_rt = sb("b_rt", [P, E])
        w_rt = sb("w_rt", [P, KD, E])
        ss = sb("ss", [P, TB])
        rs = sb("rs", [P, TB])
        rr = sb("rr", [P, TB])
        oss = sb("oss", [P, TB, H])
        ors = sb("ors", [P, TB, H])
        orr = sb("orr", [P, TB, H])
        epsc = sb("epsc", [P, 2])
        lam2 = sb("lam2", [P, 2])
        lame = sb("lame", [P, 2])
        nlam = sb("nlam", [P, 2])
        mx = sb("mx", [P, 2, 2])
        nmx = sb("nmx", [P, 2, 2])
        den = sb("den", [P, 2, 2])
        rden = sb("rden", [P, 2, 2])
        nrl = sb("nrl", [P, 2])
        top = sb("top", [P, TB, 8])
        topi = sb("topi", [P, TB, 8], U32)
        topf = sb("topf", [P, TB, TOP])
        gd = sb("gd", [P, TB, TOP])
        ge = sb("ge", [P, TB, TOP])
        gs = sb("gs", [P, TB])
        gr = sb("gr", [P, TB])
        gate = sb("gate", [P, TB, TOP])
        gdense = sb("gdense", [P, TB, E])
        gdT = R4[0:E, 0:512]
        lgT = R4[0:E, 512:1024]
        nblk = sb("nblk", [P, E])
        run = sb("run", [P, TB, E])
        startf = sb("startf", [P, E + 1])
        starti = sb("starti", [P, E + 1], I32)
        slk = sb("slk", [P, TB * TOP])
        sli = sb("sli", [P, TB * TOP], I32)
        slj = sb("slj", [P, 2, TB * TOP], I32)
        slf = sb("slf", [P, 2, TB * TOP])
        tabf = R4[0:BT, 512:512 + 2 * MAXB].rearrange("p (a b) -> p a b", a=2)
        inval = R4[0:BT, 640:640 + MAXB]
        gate_tab = sb("gate_tab", [BT, MAXB + 1])
        from_tab = sb("from_tab", [BT, MAXB], I32)
        to_tab = sb("to_tab", [BT, MAXB + 1], I32)
        from_c = sb("from_c", [BT, 1], I32)
        to_c = sb("to_c", [BT, 1], I32)
        gate_c = sb("gate_c", [BT, 1])

        x_in = [sem(f"x_in{t}") for t in range(TB)]
        small_in = sem("small_in")
        gains_in = [sem("gain0_in"), sem("gain1_in")]
        p_in = sem("p_in")
        bdn_in = sem("bdn_in")
        ring_in = [sem(f"ring_in{s}") for s in range(SLOTS)]
        consts = sem("consts")
        zpad0 = sem("zpad0")
        dve_step = sem("dve_step")
        act_step = sem("act_step")
        pool_step = sem("pool_step")
        squares = sem("squares")
        roots = sem("roots")
        normed = sem("normed")
        turned = sem("turned")
        turned_out = sem("turned_out")
        setup_tr = sem("setup_tr")
        setup_out = sem("setup_out")
        proj = sem("proj")
        proj_out = sem("proj_out")
        u_split = sem("u_split")
        v_used = sem("v_used")
        d_hi_ready = sem("d_hi_ready")
        d_lo_ready = sem("d_lo_ready")
        z_ready = sem("z_ready")
        conv_tap = sem("conv_tap")
        tap_product = sem("tap_product")
        pool_tap = sem("pool_tap")
        conv_mean = sem("conv_mean")
        conv_c = sem("conv_c")
        conv_sq = sem("conv_sq")
        conv_var = sem("conv_var")
        conv_sd = sem("conv_sd")
        conv_n = sem("conv_n")
        conv_ready = sem("conv_ready")
        conv_out = sem("conv_out")
        lam_dot = sem("lam_dot")
        lam_exp = sem("lam_exp")
        scores = sem("scores")
        maxed = sem("maxed")
        exped = sem("exped")
        mixed = sem("mixed")
        a_turned = sem("a_turned")
        a_out = sem("a_out")
        pv = sem("pv")
        o_sq = sem("o_sq")
        o_cp = sem("o_cp")
        o_root = sem("o_root")
        o_normed = sem("o_normed")
        o_turned = sem("o_turned")
        o_out = sem("o_out")
        gate_a = sem("gate_a")
        gates = sem("gates")
        o_split = sem("o_split")
        conv_hi_ready = sem("conv_hi_ready")
        conv_split = sem("conv_split")
        gates_sig = sem("gates_sig")
        branch = sem("branch")
        m_ready = sem("m_ready")
        wo_done = sem("wo_done")
        h1_half = sem("h1_half")
        x_again = sem("x_again")
        logits_T = sem("logits_T")
        lgT_out = sem("lgT_out")
        logits = sem("logits")
        top_ready = sem("top_ready")
        gexp = sem("gexp")
        mask_ready = sem("mask_ready")
        counts = sem("counts")
        onehots = sem("onehots")
        table = sem("table")
        tables = sem("tables")
        gd_ready = sem("gd_ready")
        gd_turned = sem("gd_turned")
        gdT_out = sem("gdT_out")
        bdn = sem("bdn")
        base_ready = sem("base_ready")
        ptr = sem("ptr")
        pT_out = sem("pT_out")
        ple_mm = sem("ple_mm")
        ple_out = sem("ple_out")
        u_stored = sem("u_stored")
        sum_stored = sem("sum_stored")
        gathered = sem("gathered")
        scattered = sem("scattered")
        cols_ready = sem("cols_ready")
        from_ready = sem("from_ready")
        to_ready = sem("to_ready")
        x_turned = sem("x_turned")
        x_hi_ready = sem("x_hi_ready")
        hi_ready = sem("hi_ready")
        lo_ready = sem("lo_ready")
        piece_used = sem("piece_used")
        down_in = sem("down_in")
        down_done = sem("down_done")
        hT_ready = sem("hT_ready")
        bgu_in = sem("bgu_in")
        bgu_hi = sem("bgu_hi")
        bgu_split = sem("bgu_split")
        sel_ready = sem("sel_ready")
        x_split = sem("x_split")
        h_turned = sem("h_turned")
        h_hi_ready = sem("h_hi_ready")
        h_split = sem("h_split")
        gu_done = sem("gu_done")
        gu_read = sem("gu_read")
        gate_ready = sem("gate_ready")
        sig_ready = sem("sig_ready")
        h_ready = sem("h_ready")
        dve_block = sem("dve_block")
        y_ready = sem("y_ready")
        y_free = sem("y_free")
        passed = {"pe": sem("pe_passed"), "pool": sem("pool_passed")}
        h2_in = [sem(f"h2_in{t}") for t in range(TB)]
        pg_hi_ready = sem("pg_hi_ready")
        pg_split = sem("pg_split")
        pg = sem("pg")
        pg_sig = sem("pg_sig")
        h3_half = sem("h3_half")
        out_ready = sem("out_ready")
        out_stored = sem("out_stored")

        SMALL = 11 * 16
        used_up = {name: (d_lo_ready, max(n for n, (m, _) in enumerate(pieces) if m == name) + 1)
                   for name in ("conv_a", "conv_g", "q", "k", "v", "ga0", "gb0", "ga1", "gb1")}
        used_up |= {"ao": (d_lo_ready, len(pieces)), "co": (d_lo_ready, len(pieces)),
                    "wo0": (wo_done, 2 * TB - 1), "wo1": (wo_done, 2 * TB)}

        block = ctx.enter_context(nc.Block())

        def tap_batch(n):
            return range(2 * (n - 10) + 1, 2 * (n - 10) + 3)

        LATE_TAPS = range(tap_batch(19)[-1] + 1, TAPS)

        def lies_in(slot, i):
            return dense[max(j for j in range(i) if slots[j] == slot)][0]

        def slot_of(name):
            return ring[:, slots[at[name]], :]

        def flat(dst, k):
            return dst.rearrange("p (k n) -> p k n", k=k)

        def piece(n):
            name, c = pieces[n]
            if name == "ao co":
                return [(flat(slot_of(m), 4)[:, :, c * P:(c + 1) * P], slice(i * 512, (i + 1) * 512), 4)
                        for i, m in enumerate(("ao", "co"))]
            w = flat(slot_of(name), KD)
            if name == "v":
                return [(w[:, 2 * c:2 * c + 2, :], slice(0, 1024), 2)]
            return [(w[:, :, c * P:(c + 1) * P], slice(0, 1024), KD)]

        def piece_view(parts, n):
            return flat(parts[n % 2], 2 if pieces[n][0] == "v" else KD)

        pg_hi = [flat(ringr[:, c * 4096:(c + 1) * 4096], KD) for c in (3, 4)]
        pg_lo = [flat(ringr[:, c * 4096:(c + 1) * 4096], KD) for c in (0, 1)]
        u3_lo = ringr[:, 5 * 4096:6 * 4096].rearrange("p (k s) -> p k s", k=KD)

        w_ple_sb = flat(ring[:, 2, 0:2048], PLE // P)
        p_sb = flat(ring[:, 2, 2048:3072], TB)
        pT = flat(ring[:, 2, 3072:4096], PLE // P)

        GUC = 4
        NPB = (SLOTS - 1) * PC
        assert NPB % NB == 0
        w_gu_v = w_gate_up.rearrange("l e (k q) n -> q (l e) k n", q=P)
        w_dn_v = w_down.rearrange("l e (k q) n -> q (l e) k n", q=P)

        def expert_chunk(e, c):
            if c < GUC:
                return w_gu_v[:, bass.ds(e, 1), :, c * 512:(c + 1) * 512].rearrange("q e k n -> q (e k) n")
            c -= GUC
            return w_dn_v[:, bass.ds(e, 1), c * 4:(c + 1) * 4, :].rearrange("q e k n -> q (e k) n")

        def chunk_slot(c):
            return flat(ring[:, c, :], 8 if c < GUC else 4)

        @block.sync
        def _(sp):
            def load(dst, src):
                sp.dma_start(dst, src).then_inc(small_in, 16)

            for t in range(TB):
                sp.dma_start(x_sb[:, t, :], x_t[:, t, :]).then_inc(x_in[t], 16)
            for i, (name, src) in enumerate(dense):
                if turn(name) > 1:
                    sp.wait_ge(*used_up[lies_in(slots[i], i)])
                k = src.shape[1]
                n = k * src.shape[2]
                sp.dma_start(flat(slot_of(name)[:, 0:n], k), src).then_inc(ring_in[slots[i]], 16)
                if i == 0:
                    load(R1[0:TAPS, 0:512], w_dw.rearrange("l j c -> (l j) c"))
                    load(R1[TAPS:TAPS + 1, 0:512], b_dw)
                    load(R1[TAPS + 1:TAPS + 2, 0:512], g_conv_ln)
                    load(R1[TAPS + 2:TAPS + 3, 0:512], b_conv_ln)
                    for j, v in enumerate((lambda_q1, lambda_k1, lambda_q2, lambda_k2)):
                        load(lamb[:, j, :], v.to_broadcast([P, QD]))
                    load(gsub[:, :], g_subln.to_broadcast([P, HD]))
                    load(b_rt[:, :], b_router.to_broadcast([P, E]))
                    load(w_rt[:, :, :], w_router.rearrange("l (k q) e -> q (l k) e", q=P))
                if name == "v":
                    sp.dma_start(gB[1][:, :], g_ffn.to_broadcast([P, D])).then_inc(gains_in[1], 16)
                if name == "wo1":
                    sp.wait_ge(branch, KD)
                    sp.dma_start(x_sb, x_t).then_inc(x_again, 16)
            for c in (4, 5, 3, 0, 1, 2):
                if uses[c]:
                    sp.wait_ge(*used_up[lies_in(c, len(dense))])
                else:
                    sp.wait_ge(gates, KD)
                sp.dma_start(chunk_slot(c), expert_chunk(0, c)).then_inc(ring_in[c], 16)
            sp.wait_ge(tables, 1)
            with sp.Fori(1, E) as e:
                first = sp.value_load(starti[0:1, bass.ds(e, 1)], min_val=1, max_val=MAXB - 1)
                for c in range(SLOTS):
                    if c < SLOTS - 1:
                        sp.wait_ge(lo_ready, first * NPB + (c + 1) * PC)
                    else:
                        sp.wait_ge(down_done, first + 1)
                    sp.dma_start(chunk_slot(c), expert_chunk(e, c)).then_inc(ring_in[c], 16)
            total = sp.value_load(starti[0:1, E:E + 1], min_val=1, max_val=MAXB - 1)
            for c in range(2):
                sp.wait_ge(lo_ready, total * NPB + (c + 1) * PC)
                sp.dma_start(flat(ring[:, c, :], KD), cols(w_pg_v, c)).then_inc(ring_in[c], 16)
            sp.wait_ge(lo_ready, total * NPB + 3 * PC)
            sp.dma_start(w_ple_sb, w_ple_v).then_inc(p_in, 16)
            sp.dma_start(p_sb, p_t).then_inc(p_in, 16)
            sp.wait_ge(y_free, total + 2)
            for t in range(TB):
                sp.dma_start(x_sb[:, t, :], sum_rows[t * P:(t + 1) * P, :]).then_inc(h2_in[t], 16)
            for t in range(TB):
                sp.wait_ge(out_ready, t + 1)
                sp.dma_start(out_t[:, t, :], u_tok[:, t, :]).then_inc(out_stored, 16)
            sp.wait_ge(out_stored, 16 * TB)

        @block.gpsimd
        def _(pool):
            n = 0

            def link(ins):
                nonlocal n
                n += 1
                ins.then_inc(pool_step, 1)
                pool.wait_ge(pool_step, n)

            nc.gpsimd.memset(ones[:, :], 1.0).then_inc(consts, 1)
            link(nc.gpsimd.memset(ident[:, :], 0.0))
            link(nc.gpsimd.memset(before[:, :], 1.0))
            link(nc.gpsimd.memset(cmask[:, :], 0.0))
            nc.gpsimd.affine_select(out=ident[:, :], in_=ident[:, :], compare_op=ALU.not_equal, fill=1.0,
                                    base=0, pattern=[[-1, P]], channel_multiplier=1).then_inc(consts, 1)
            nc.gpsimd.affine_select(out=before[:, :], in_=before[:, :], compare_op=ALU.is_gt, fill=0.0,
                                    base=0, pattern=[[1, P]], channel_multiplier=-1).then_inc(consts, 1)
            nc.gpsimd.affine_select(out=cmask[:, :], in_=cmask[:, :], compare_op=ALU.is_ge, fill=NEG,
                                    base=0, pattern=[[-1, P]], channel_multiplier=1).then_inc(consts, 1)
            nc.gpsimd.iota(iota[:, :], pattern=[[1, BT]], base=0, channel_multiplier=0,
                           allow_small_or_imprecise_dtypes=True).then_inc(consts, 1)
            nc.gpsimd.iota(tokid[:, :], pattern=[[P, TB]], base=0, channel_multiplier=1,
                           allow_small_or_imprecise_dtypes=True).then_inc(consts, 1)
            nc.gpsimd.iota(spare[:, :], pattern=[[0, 1]], base=S, channel_multiplier=1,
                           allow_small_or_imprecise_dtypes=True).then_inc(consts, 1)
            nc.gpsimd.memset(epsc[:, 0:1], EPS).then_inc(consts, 1)
            nc.gpsimd.memset(epsc[:, 1:2], EPS / (1.0 - LAM_INIT) ** 2).then_inc(consts, 1)
            nc.gpsimd.memset(z[:, :, 0:PAD], 0.0).then_inc(zpad0, 1)

            def tap(j):
                pool.wait_ge(tap_product, j + 1)
                if j >= 2:
                    pool.wait_ge(pool_tap, j - 1)
                nc.gpsimd.tensor_tensor(conv[:, CT - 1, :], conv[:, CT - 1, :], sg[:, j % 4, :], ALU.add)\
                    .then_inc(pool_tap, 1)

            for n_piece in range(len(pieces)):
                pool.wait_ge(d_hi_ready, n_piece + 1)
                for w, to, k in piece(n_piece):
                    last = nc.gpsimd.tensor_tensor(flat(d_lo[n_piece % 2][:, to], k), w,
                                                   flat(d_hi[n_piece % 2][:, to], k).bitcast(F32), ALU.subtract)
                last.then_inc(d_lo_ready, 1)
                if 10 <= n_piece < 20:
                    for j in tap_batch(n_piece):
                        tap(j)

                if n_piece == 19:
                    for j in LATE_TAPS:
                        tap(j)

            pool.wait_ge(normed, 2 * TB)
            nc.gpsimd.dma_start(u_rows.rearrange("(t q) d -> q t d", q=P), u_tok).then_inc(u_stored, 16)
            link(nc.gpsimd.memset(y_sb, 0.0))
            nc.gpsimd.dma_start(sum_rows[S:S + BT, :], y_sb).then_inc(sum_stored, 16)
            pool.wait_ge(sum_stored, 16)
            pool.wait_ge(base_ready, 2 * TB)
            pool.wait_ge(u_stored, 16)
            pool.wait_ge(tables, 1)
            link(nc.gpsimd.tensor_copy(from_c[:, :], from_tab[:, 0:1]))
            nc.gpsimd.indirect_dma_start(out=xg, out_offset=None, in_=u_rows[:, :],
                                         in_offset=bass.IndirectOffsetOnAxis(ap=from_c[:, 0:1], axis=0))\
                .then_inc(gathered, 16)
            nc.gpsimd.dma_start(sum_rows[0:S, :].rearrange("(t q) d -> q t d", q=P), x_sb)\
                .then_inc(sum_stored, 16)
            total = pool.value_load(starti[0:1, E:E + 1], min_val=1, max_val=MAXB - 1)
            nc.gpsimd.tensor_copy(sel_c[:, :], sel_tab[:, 0:1].to_broadcast([2 * E, P])).then_inc(sel_ready, 1)
            pool.wait_ge(sum_stored, 32)
            link(nc.gpsimd.tensor_copy(to_c[:, :], to_tab[:, 0:1]))
            nc.gpsimd.indirect_dma_start(out=sum_rows[:, :],
                                         out_offset=bass.IndirectOffsetOnAxis(ap=to_c[:, 0:1], axis=0),
                                         in_=y_sb, in_offset=None, compute_op=ALU.add).then_inc(scattered, 16)

            def scatter_before(b):
                pool.wait_ge(scattered, (b + 1) * 16)
                nc.gpsimd.sem_inc(y_free, 1)
                nc.gpsimd.tensor_copy(gate_c[:, :], gate_tab[:, bass.ds(b, 1)]).then_inc(cols_ready, 1)
                nc.gpsimd.tensor_copy(to_c[:, :], to_tab[:, bass.ds(b, 1)]).then_inc(to_ready, 1)
                pool.wait_ge(to_ready, b + 1)
                pool.wait_ge(y_ready, b * 2 + 2)
                nc.gpsimd.sem_inc(passed["pool"], 1)
                nc.gpsimd.indirect_dma_start(out=sum_rows[:, :],
                                             out_offset=bass.IndirectOffsetOnAxis(ap=to_c[:, 0:1], axis=0),
                                             in_=y_sb, in_offset=None, compute_op=ALU.add)\
                    .then_inc(scattered, 16)

            with pool.Fori(0, total) as b:
                pool.wait_ge(gathered, (b + 1) * 16)
                pool.wait_ge(x_turned, b + 1)
                nc.gpsimd.tensor_copy(from_c[:, :], from_tab[:, bass.ds(b + 1, 1)]).then_inc(from_ready, 1)
                pool.wait_ge(from_ready, b + 1)
                nc.gpsimd.sem_inc(passed["pool"], 1)
                nc.gpsimd.indirect_dma_start(out=xg, out_offset=None, in_=u_rows[:, :],
                                             in_offset=bass.IndirectOffsetOnAxis(ap=from_c[:, 0:1], axis=0))\
                    .then_inc(gathered, 16)
                scatter_before(b)
                pool.wait_ge(gu_done, b * GUC + GUC)
                nc.gpsimd.tensor_copy(sel_c[:, :], sel_tab[:, bass.ds(b + 1, 1)].to_broadcast([2 * E, P]))\
                    .then_inc(sel_ready, 1)
            scatter_before(total)
            pool.wait_ge(scattered, (total + 2) * 16)
            nc.gpsimd.sem_inc(y_free, 1)
            pool.wait_ge(gathered, (total + 1) * 16)

        @block.scalar
        def _(act):
            n = 0

            def link(ins):
                nonlocal n
                n += 1
                ins.then_inc(act_step, 1)
                act.wait_ge(act_step, n)

            def row(v):
                return v.rearrange("(a n) -> a n", a=1) if len(v.shape) == 1 else v

            act.dma_start(gB[0][:, :], g_mix.to_broadcast([P, D])).then_inc(gains_in[0], 16)
            act.wait_ge(consts, 9)
            link(nc.scalar.activation(gs[:, 0:1], epsc[:, 0:1], ACT.Sqrt))

            for t in range(TB):
                act.wait_ge(x_in[t], 16)
                link(nc.scalar.activation(junk, x_sb[:, t, :], ACT.Square, accum_out=ss[:, t:t + 1]))
            nc.scalar.activation(rs[:, :], ss[:, :], ACT.Sqrt, bias=epsc[:, 0:1], scale=1.0 / D)\
                .then_inc(roots, 1)
            for t in range(TB):
                for h in range(2):
                    act.wait_ge(turned, 2 * t + h + 1)
                    nc.scalar.activation(u_hi[:, 4 * h:4 * h + 4, t * P:(t + 1) * P],
                                         ps[:, 4 + (2 * t + h) % 4, :].rearrange("p (k s) -> p k s", k=4),
                                         ACT.Copy).then_inc(turned_out, 1)

            def d_hi_out(n):
                name, c = pieces[n]
                if c == 0:
                    for m in name.split():
                        act.wait_ge(ring_in[slots[at[m]]], 16 * turn(m))
                if 2 <= n < 18:
                    act.wait_ge(proj, n - 1)
                elif 18 <= n < 21:
                    act.wait_ge(v_used, n - 17)
                elif n == 21:
                    act.wait_ge(proj, 20)
                elif n > 21:
                    act.wait_ge((gate_a, gates, branch)[(n - 22) % 3], (n - 22) // 3 + 1)
                for w, to, k in piece(n):
                    last = nc.scalar.activation(flat(d_hi[n % 2][:, to], k), w, ACT.Copy)
                last.then_inc(d_hi_ready, 1)

            d_hi_out(0)
            d_hi_out(1)
            def product(j):
                if j >= 5:
                    act.wait_ge(pool_tap, j - 4)
                nc.scalar.activation(sg[:, j % 4, :], z[:, CT - 1, j:j + S], ACT.Copy,
                                     scale=cvec[:, CT - 1, j:j + 1]).then_inc(tap_product, 1)

            def tap_products(n):
                if not 10 <= n < 20:
                    return
                t = CT - 1
                if n == 10:
                    act.wait_ge(z_ready, CT)
                    act.wait_ge(setup_out, 1)
                    nc.scalar.activation(conv[:, t, :], z[:, t, 0:S], ACT.Identity, scale=cvec[:, t, 0:1],
                                         bias=cvec[:, t, TAPS:TAPS + 1]).then_inc(tap_product, 1)
                for j in tap_batch(n):
                    product(j)

            act.wait_ge(zpad0, 1)
            for i in range(20):
                j, t = i // 4, i % 4
                act.wait_ge(proj, i + 1)
                src = ps[:, i % 4, :]
                if j == 0:
                    ins = nc.scalar.activation(z[:, t, PAD:PAD + S], src, ACT.Copy)
                elif j == 1:
                    ins = nc.scalar.activation(sg[:, t, :], src, ACT.Sigmoid)
                elif j == 2:
                    if t == 0:
                        act.wait_ge(setup_out, 1)
                        act.wait_ge(lam_dot, 1)
                    ins = nc.scalar.activation(qT[:, t, :], src, ACT.Copy, scale=SCALE)
                elif j == 3:
                    ins = nc.scalar.activation(kT[:, t, :], src, ACT.Copy)
                else:
                    ins = nc.scalar.activation(v_sb[:, t, :], src, ACT.Copy)
                ins.then_inc(proj_out, 1)
                if i < 15:
                    d_hi_out(i + 2)
                    tap_products(i + 2)
                elif i == 15:
                    for j in range(17, 21):
                        d_hi_out(j)
                        tap_products(j)
                elif i == 19:
                    d_hi_out(21)
            nc.scalar.activation(lame[:, :], lam2[:, :], ACT.Exp).then_inc(lam_exp, 1)

            def exps(i):
                w = (i % TB + 1) * P
                act.wait_ge(maxed, i + 1)
                if i >= 2:
                    act.wait_ge(a_turned, i - 1)
                for c in range(2):
                    nc.scalar.activation(ex[:, i % 2, c, 0:w], ps[:, 4 + 2 * (i % 2) + c, 0:w], ACT.Exp,
                                         bias=nmx[:, i % 2, c:c + 1],
                                         accum_out=den[:, i % 2, c:c + 1]).then_inc(exped, 1)

            def turned_a(i):
                w = (i % TB + 1) * P
                act.wait_ge(a_turned, i + 1)
                if i >= 2:
                    act.wait_ge(pv, i - 1)
                nc.scalar.activation(a_T[:, i % 2, 0:w], ps[:, i % 2, 0:w], ACT.Copy).then_inc(a_out, 1)

            def results(i):
                h, t = i // TB, i % TB
                act.wait_ge(pv, i + 1)
                nc.scalar.activation(o_tok[:, t, h * HD:(h + 1) * HD], ps[:, 2, (i % 4) * P:(i % 4 + 1) * P],
                                     ACT.Copy).then_inc(o_cp, 1)
                act.wait_ge(o_cp, i + 1)
                nc.scalar.activation(ps[:, 2, (i % 4) * P:(i % 4 + 1) * P],
                                     o_tok[:, t, h * HD:(h + 1) * HD],
                                     ACT.Square, accum_out=oss[:, t, h:h + 1]).then_inc(o_sq, 1)

            NI = H * TB
            for i in range(NI + 3):
                if 2 <= i < NI + 2:
                    turned_a(i - 2)
                if i < NI:
                    exps(i)
                if i >= 3:
                    results(i - 3)
                if i < 5:
                    for j in LATE_TAPS[2 * i:2 * i + 2]:
                        product(j)
            act.wait_ge(conv_c, CT)
            for t in range(CT):
                nc.scalar.activation(sg[:, t, :], conv[:, t, :], ACT.Square).then_inc(conv_sq, 1)
            act.wait_ge(conv_var, 1)
            nc.scalar.activation(ex[:, 0, 0, :], ps[:, 3, :], ACT.Sqrt, bias=epsc[:, 0:1], scale=1.0 / CW)\
                .then_inc(conv_sd, 1)
            act.wait_ge(o_sq, NI)
            nc.scalar.activation(ors[:, :, :], oss[:, :, :], ACT.Sqrt, bias=epsc[:, 1:2],
                                 scale=1.0 / (HD * (1.0 - LAM_INIT) ** 2)).then_inc(o_root, 1)
            for t in range(CT):
                act.wait_ge(conv_n, t + 1)
                nc.scalar.activation(sg[:, t, :], conv[:, t, :], ACT.Sigmoid,
                                     bias=cvec[:, t, TAPS + 2:TAPS + 3],
                                     scale=cvec[:, t, TAPS + 1:TAPS + 2]).then_inc(conv_ready, 1)
            d_hi_out(22)
            for h in range(H):
                act.wait_ge(o_turned, h + 1)
                nc.scalar.activation(o_hi[:, h, :], ps[:, h, :], ACT.Copy).then_inc(o_out, 1)
            for t in range(CT):
                act.wait_ge(conv_out, t + 1)
                nc.scalar.activation(conv_hi[:, t, :], conv[:, t, :], ACT.Copy).then_inc(conv_hi_ready, 1)
            for k in range(KD):
                b = 4 * ((k + 1) % 2)
                if k > 0:
                    d_hi_out(22 + 3 * k)
                act.wait_ge(gates, k + 1)
                if k >= 2:
                    act.wait_ge(m_ready, k - 1)
                for c in range(2):
                    nc.scalar.activation(ex[:, k % 2, c, :], ps[:, b + c, :], ACT.Sigmoid)\
                        .then_inc(gates_sig, 1)
                if k < KD - 1:
                    d_hi_out(23 + 3 * k)
                    d_hi_out(24 + 3 * k)
            act.wait_ge(m_ready, KD)
            act.dma_start(b_dn, b_down.rearrange("l e d -> (l e) d")).then_inc(bdn_in, 16)
            for a in range(2):
                act.dma_start(bgu[a * E:(a + 1) * E, :], b_gate_up.rearrange("l e n -> (l e) n"))\
                    .then_inc(bgu_in, 16)
            for t in range(TB):
                act.wait_ge(h1_half, 2 * t + 2)
                link(nc.scalar.activation(junk, x_sb[:, t, :], ACT.Square, accum_out=ss[:, t:t + 1]))
                nc.scalar.activation(rs[:, t:t + 1], ss[:, t:t + 1], ACT.Sqrt, bias=epsc[:, 0:1],
                                     scale=1.0 / D).then_inc(roots, 1)
                for h in range(2):
                    act.wait_ge(turned, 8 + 2 * t + h + 1)
                    nc.scalar.activation(uT[:, 4 * h:4 * h + 4, t * P:(t + 1) * P],
                                         ps[:, 4 + (2 * t + h) % 4, :].rearrange("p (k s) -> p k s", k=4),
                                         ACT.Copy).then_inc(turned_out, 1)
            act.dma_start(gB[0][:, :], g_ple.to_broadcast([P, D])).then_inc(gains_in[0], 16)
            act.wait_ge(normed, 2 * TB)
            act.dma_start(gB[1][:, :], row(g_final).to_broadcast([P, D])).then_inc(gains_in[1], 16)
            act.wait_ge(logits_T, 1)
            nc.scalar.activation(lgT, ps[0:E, 1, :], ACT.Copy).then_inc(lgT_out, 1)
            act.wait_ge(top_ready, 1)
            nc.scalar.activation(ge[:, :, :], gd[:, :, :], ACT.Exp).then_inc(gexp, 1)
            act.wait_ge(gd_turned, 1)
            nc.scalar.activation(gdT, ps[0:E, 6, :], ACT.Copy).then_inc(gdT_out, 1)
            act.wait_ge(tables, 1)
            act.wait_ge(bgu_in, 32)
            nc.scalar.activation(bgu_parts, bgu, ACT.Copy).then_inc(bgu_hi, 1)

            def results_out(b):
                act.wait_ge(cols_ready, b + 1)
                act.wait_ge(y_free, b + 1)
                act.wait_ge(down_done, b + 1)
                for h in range(2):
                    nc.scalar.activation(y_sb[:, h * 512:(h + 1) * 512], ps[0:BT, 6 + h, :], ACT.Copy,
                                         scale=gate_c[:, 0:1]).then_inc(y_ready, 1)

            act.wait_ge(ring_in[SLOTS - 1], (uses[SLOTS - 1] + 1) * 16)
            nc.scalar.sem_inc(down_in, 1)
            with act.Fori(0, E) as e:
                first = act.value_load(starti[0:1, bass.ds(e, 1)], min_val=0, max_val=MAXB - 1)
                end = act.value_load(starti[0:1, bass.ds(e + 1, 1)], min_val=1, max_val=MAXB - 1)
                with act.Fori(first, end) as b:
                    def hi(p):
                        c = p // PC
                        if p % PC == 0:
                            act.wait_ge(ring_in[c], (e + (uses[c] + 1)) * 16)
                        act.wait_ge(piece_used, b * NPB + (p + 1))
                        nc.scalar.activation(w_hi[p % NB], ring[:, c, p % PC * PW:(p % PC + 1) * PW], ACT.Copy)\
                            .then_inc(hi_ready, 1)

                    def h_out(c):
                        act.wait_ge(h_turned, b * GUC + (c + 3))
                        out, ready = (h_hi, h_hi_ready) if c < 2 else (hT, hT_ready)
                        nc.scalar.activation(out[:, 2 * (c % 2):2 * (c % 2) + 2, :],
                                             ps[:, 2 + c % 2, 0:2 * BT].rearrange("p (k n) -> p k n", k=2),
                                             ACT.Copy).then_inc(ready, 1)

                    nc.scalar.activation(gs[:, 1:2], epsc[:, 0:1], ACT.Sigmoid)
                    act.wait_ge(x_turned, b + 1)
                    nc.scalar.activation(x_hi, ps[:, 4:6, :].rearrange("p a n -> p (a n)"), ACT.Copy)\
                        .then_inc(x_hi_ready, 1)
                    for p in range(NB):
                        hi(p)
                    results_out(b)
                    for c in range(GUC):
                        p = PC * c + NB
                        hi(p)
                        hi(p + 1)
                        if c >= 2:
                            h_out(c - 2)
                        if p + 2 < NPB:
                            hi(p + 2)
                        if p + 3 < NPB:
                            hi(p + 3)
                        act.wait_ge(gate_ready, b * GUC + c + 1)
                        nc.scalar.activation(sig_b[:, c % 2], gate_b[:, c % 2], ACT.Sigmoid, scale=ALPHA)\
                            .then_inc(sig_ready, 1)
                    h_out(GUC - 2)
                    h_out(GUC - 1)
                    act.wait_ge(ring_in[SLOTS - 1], (e + (uses[SLOTS - 1] + 1)) * 16)
                    nc.scalar.sem_inc(down_in, 1)
            total = act.value_load(starti[0:1, E:E + 1], min_val=1, max_val=MAXB - 1)
            results_out(total)
            act.wait_ge(down_done, total + 1)
            for c in range(2):
                act.wait_ge(ring_in[c], 16 * (uses[c] + E + 1))
                for j in range(4):
                    nc.scalar.activation(pg_hi[c][:, 2 * j:2 * j + 2, :],
                                         flat(ring[:, c, :], KD)[:, 2 * j:2 * j + 2, :], ACT.Copy)\
                        .then_inc(pg_hi_ready, 1)
            for k in range(PLE // P):
                act.wait_ge(ptr, k + 1)
                nc.scalar.activation(pT[:, k, :], ps[:, 2 + k, :], ACT.Copy).then_inc(pT_out, 1)
            def ple_half(i):
                act.wait_ge(ple_mm, i + 1)
                nc.scalar.activation(pple[:, i // 2, (i % 2) * 512:(i % 2 + 1) * 512], ps[:, i % 2, :],
                                     ACT.Copy).then_inc(ple_out, 1)

            link(nc.scalar.activation(gs[:, 0:1], epsc[:, 0:1], ACT.Sqrt))
            for i in range(4):
                ple_half(i)
            for t in range(TB):
                act.wait_ge(h2_in[t], 16)
                if t == 0:
                    act.wait_ge(x_turned, total + 1)
                link(nc.scalar.activation(junk, x_sb[:, t, :], ACT.Square, accum_out=ss[:, t:t + 1]))
            nc.scalar.activation(rs[:, :], ss[:, :], ACT.Sqrt, bias=epsc[:, 0:1], scale=1.0 / D)\
                .then_inc(roots, 1)
            for i in range(4, 2 * TB):
                ple_half(i)
            for t in range(TB):
                for h in range(2):
                    act.wait_ge(turned, 16 + 2 * t + h + 1)
                    nc.scalar.activation(u_hi[:, 4 * h:4 * h + 4, t * P:(t + 1) * P],
                                         ps[:, 4 + (2 * t + h) % 4, :].rearrange("p (k s) -> p k s", k=4),
                                         ACT.Copy).then_inc(turned_out, 1)
            for i in range(2 * TB):
                act.wait_ge(pg, i + 1)
                if i >= 4:
                    act.wait_ge(h3_half, i - 3)
                nc.scalar.activation(sg[:, i % 4, :], ps[:, i % 4, :], ACT.Sigmoid).then_inc(pg_sig, 1)
            for t in range(TB):
                act.wait_ge(h3_half, 2 * t + 2)
                link(nc.scalar.activation(junk, x_sb[:, t, :], ACT.Square, accum_out=ss[:, t:t + 1]))
                nc.scalar.activation(rs[:, t:t + 1], ss[:, t:t + 1], ACT.Sqrt, bias=epsc[:, 0:1],
                                     scale=1.0 / D).then_inc(roots, 1)

        @block.vector
        def _(dve):
            n = 0

            def link(ins):
                nonlocal n
                n += 1
                ins.then_inc(dve_step, 1)
                dve.wait_ge(dve_step, n)

            def norm(src, dst, g):
                for t in range(TB):
                    nc.vector.scalar_tensor_tensor(dst[:, t, :], src[:, t, :], rr[:, t:t + 1], g[:, :],
                                                   ALU.mult, ALU.mult).then_inc(normed, 1)

            dve.wait_ge(roots, 1)
            dve.wait_ge(gains_in[0], 16)
            link(nc.vector.reciprocal(rr[:, :], rs[:, :]))
            norm(x_sb, x_sb, gB[0])
            for i in range(2 * TB):
                t, h = i // 2, i % 2
                dve.wait_ge(turned_out, i + 1)
                us = (slice(None), slice(4 * h, 4 * h + 4), slice(t * P, (t + 1) * P))
                nc.vector.tensor_tensor(u_lo[us], ps[:, 4 + i % 4, :].rearrange("p (k s) -> p k s", k=4),
                                        u_hi[us].bitcast(F32), ALU.subtract).then_inc(u_split, 1)
            dve.wait_ge(setup_tr, 1)
            nc.vector.tensor_copy(cvec[:, :, :], ps[:, 4, 0:CT * (TAPS + 3)].rearrange("p (t j) -> p t j", t=CT))\
                .then_inc(setup_out, 1)
            link(nc.vector.tensor_tensor(eye2[:, :], ident[0:2 * E, 0:E], ident[0:2 * E, E:2 * E], ALU.add))
            dve.wait_ge(small_in, SMALL)
            link(nc.vector.tensor_tensor(lprod, lamb[:, 0:4:2, :], lamb[:, 1:4:2, :], ALU.mult))
            nc.vector.tensor_reduce(lam2[:, :], lprod, AX_X, ALU.add).then_inc(lam_dot, 1)
            for t in range(CT):
                dve.wait_ge(proj_out, CT + t + 1)
                nc.vector.tensor_tensor(z[:, t, PAD:PAD + S], z[:, t, PAD:PAD + S], sg[:, t, :], ALU.mult)\
                    .then_inc(z_ready, 1)
            dve.wait_ge(setup_out, 1)
            for t in range(CT - 1):
                dve.wait_ge(z_ready, t + 1)
                nc.vector.tensor_scalar(conv[:, t, :], z[:, t, 0:S], cvec[:, t, 0:1],
                                        cvec[:, t, TAPS:TAPS + 1], ALU.mult, ALU.add).then_inc(conv_tap, 1)
            with dve.Fori(1, TAPS) as j:
                for t in range(CT - 1):
                    dve.wait_ge(conv_tap, j * (CT - 1) + (t + 2 - CT))
                    nc.vector.scalar_tensor_tensor(conv[:, t, :], z[:, t, bass.ds(j, S)],
                                                   cvec[:, t, bass.ds(j, 1)], conv[:, t, :],
                                                   ALU.mult, ALU.add).then_inc(conv_tap, 1)
            dve.wait_ge(conv_tap, TAPS * (CT - 1))
            dve.wait_ge(lam_exp, 1)
            link(nc.vector.tensor_tensor(nlam[:, 0:1], lame[:, 1:2], lame[:, 0:1], ALU.subtract))
            link(nc.vector.tensor_scalar(nlam[:, 1:2], nlam[:, 0:1], -LAM_INIT, None, ALU.add))

            def maxes(i):
                w = (i % TB + 1) * P
                s2 = ps[:, 4 + 2 * (i % 2):6 + 2 * (i % 2), :]
                dve.wait_ge(scores, i + 1)
                link(nc.vector.tensor_tensor(s2[:, :, w - P:w], s2[:, :, w - P:w],
                                             cmask[:, :].unsqueeze(1).to_broadcast([P, 2, P]), ALU.add))
                if i >= 2:
                    dve.wait_ge(exped, 2 * (i - 1))
                link(nc.vector.tensor_reduce(mx[:, i % 2, :], s2[:, :, 0:w], AX_X, ALU.max))
                nc.vector.tensor_scalar(nmx[:, i % 2, :], mx[:, i % 2, :], -1.0, None, ALU.mult)\
                    .then_inc(maxed, 1)

            def mix(i):
                w = (i % TB + 1) * P
                b = i % 2
                dve.wait_ge(exped, 2 * i + 2)
                link(nc.vector.reciprocal(rden[:, b, :], den[:, b, :]))
                link(nc.vector.tensor_tensor(nrl[:, b:b + 1], rden[:, b, 1:2], nlam[:, 1:2], ALU.mult))
                link(nc.vector.tensor_scalar(ex[:, b, 0, 0:w], ex[:, b, 0, 0:w], rden[:, b, 0:1], None, ALU.mult))
                nc.vector.scalar_tensor_tensor(ex[:, b, 0, 0:w], ex[:, b, 1, 0:w], nrl[:, b:b + 1],
                                               ex[:, b, 0, 0:w], ALU.mult, ALU.add).then_inc(mixed, 1)

            NI = H * TB
            for i in range(NI + 1):
                if i < NI:
                    maxes(i)
                if i >= 1:
                    mix(i - 1)
                if i == 8:
                    dve.wait_ge(conv_mean, 1)
                    link(nc.vector.tensor_scalar(R2[:, 2048:2048 + S], ps[:, 3, :], 1.0 / CW, None, ALU.mult))
                    for t in range(CT):
                        nc.vector.tensor_tensor(conv[:, t, :], conv[:, t, :], R2[:, 2048:2048 + S], ALU.subtract)\
                            .then_inc(conv_c, 1)
            dve.wait_ge(conv_sd, 1)
            link(nc.vector.reciprocal(ex[:, 0, 1, :], ex[:, 0, 0, :]))
            for t in range(CT):
                nc.vector.tensor_tensor(conv[:, t, :], conv[:, t, :], ex[:, 0, 1, :], ALU.mult).then_inc(conv_n, 1)
            dve.wait_ge(o_root, 1)
            link(nc.vector.reciprocal(orr[:, :, :], ors[:, :, :]))
            for h in range(H):
                for t in range(TB):
                    o = o_tok[:, t, h * HD:(h + 1) * HD]
                    nc.vector.scalar_tensor_tensor(o, o, orr[:, t, h:h + 1], gsub[:, :], ALU.mult, ALU.mult)\
                        .then_inc(o_normed, 1)
            for t in range(CT):
                dve.wait_ge(conv_ready, t + 1)
                link(nc.vector.tensor_scalar(conv[:, t, :], conv[:, t, :], cvec[:, t, TAPS + 1:TAPS + 2],
                                             cvec[:, t, TAPS + 2:TAPS + 3], ALU.mult, ALU.add))
                nc.vector.tensor_tensor(conv[:, t, :], conv[:, t, :], sg[:, t, :], ALU.mult).then_inc(conv_out, 1)
            for h in range(H):
                dve.wait_ge(o_out, h + 1)
                nc.vector.tensor_tensor(o_lo[:, h, :], ps[:, h, :], o_hi[:, h, :].bitcast(F32), ALU.subtract)\
                    .then_inc(o_split, 1)
            for t in range(CT):
                dve.wait_ge(conv_hi_ready, t + 1)
                nc.vector.tensor_tensor(conv_lo[:, t, :], conv[:, t, :], conv_hi[:, t, :].bitcast(F32),
                                        ALU.subtract).then_inc(conv_split, 1)
            for k in range(KD):
                b = 4 * ((k + 1) % 2)
                dve.wait_ge(gates_sig, 2 * k + 2)
                dve.wait_ge(branch, k + 1)
                link(nc.vector.tensor_tensor(mT[:, k, :], ex[:, k % 2, 0, :], ps[:, b + 2, :], ALU.mult))
                link(nc.vector.tensor_tensor(sg[:, k % 2, :], ex[:, k % 2, 1, :], ps[:, b + 3, :], ALU.mult))
                nc.vector.tensor_tensor(mT[:, k, :], mT[:, k, :], sg[:, k % 2, :], ALU.add).then_inc(m_ready, 1)
            dve.wait_ge(x_again, 16)
            dve.wait_ge(gains_in[1], 16)
            for t in range(TB):
                for h in range(2):
                    i = 2 * t + h
                    dve.wait_ge(wo_done, i + 1)
                    xs = x_sb[:, t, h * 512:(h + 1) * 512]
                    nc.vector.tensor_tensor(xs, xs, ps[:, i % 4, :], ALU.add).then_inc(h1_half, 1)
                dve.wait_ge(roots, 1 + t + 1)
                link(nc.vector.reciprocal(rr[:, t:t + 1], rs[:, t:t + 1]))
                nc.vector.scalar_tensor_tensor(u_tok[:, t, :], x_sb[:, t, :], rr[:, t:t + 1], gB[1][:, :],
                                               ALU.mult, ALU.mult).then_inc(normed, 1)
            dve.wait_ge(logits, 1)
            link(nc.vector.tensor_tensor(lg, ps[:, 0, 0:TB * E].rearrange("p (t e) -> p t e", t=TB),
                                         b_rt[:, :].unsqueeze(1).to_broadcast([P, TB, E]), ALU.add))
            for t in range(TB):
                link(nc.vector.max(top[:, t, :], lg[:, t, :]))
            nc.vector.tensor_tensor(gd[:, :, :], top[:, :, 0:TOP],
                                    top[:, :, 0:1].to_broadcast([P, TB, TOP]), ALU.subtract)\
                .then_inc(top_ready, 1)
            for t in range(TB):
                link(nc.vector.max_index(topi[:, t, :], top[:, t, :], lg[:, t, :]))
            link(nc.vector.tensor_copy(topf[:, :, :], topi[:, :, 0:TOP]))
            for t in range(TB):
                link(nc.vector.tensor_tensor(eq[:, t], iota[:, 0:E].unsqueeze(1).to_broadcast([P, TOP, E]),
                                             topf[:, t, :].unsqueeze(2).to_broadcast([P, TOP, E]),
                                             ALU.is_equal))
            nc.vector.tensor_reduce(mask, eq.rearrange("p t k e -> p t e k"), AX_X, ALU.add)\
                .then_inc(mask_ready, 1)
            dve.wait_ge(gexp, 1)
            link(nc.vector.tensor_reduce(gs[:, :], ge[:, :, :], AX_X, ALU.add))
            link(nc.vector.reciprocal(gr[:, :], gs[:, :]))
            link(nc.vector.tensor_tensor(gate[:, :, :], ge[:, :, :],
                                         gr[:, :].unsqueeze(2).to_broadcast([P, TB, TOP]), ALU.mult))
            for t in range(TB):
                link(nc.vector.tensor_tensor(eqs[:, t], eq[:, t],
                                             gate[:, t, :].unsqueeze(2).to_broadcast([P, TOP, E]), ALU.mult))
            nc.vector.tensor_reduce(gdense[:, :, :], eqs.rearrange("p t k e -> p t e k"), AX_X, ALU.add)\
                .then_inc(gd_ready, 1)
            dve.wait_ge(gd_ready, 1)
            dve.wait_ge(counts, 1)
            in_block = ps[:, 1, TB * E:2 * TB * E].rearrange("p (t e) -> p t e", t=TB)
            link(nc.vector.tensor_copy(run[:, 0, :], in_block[:, 0, :]))
            for t in range(1, TB):
                link(nc.vector.tensor_tensor(run[:, t, :], run[:, t - 1, :], in_block[:, t, :], ALU.add))
            cnt = run[:, TB - 1, :]
            for a in range(TB - 1):
                nc.vector.tensor_scalar(big[:, a, :], cnt, float(BT * (a + 1)), None, ALU.is_gt)\
                    .then_inc(dve_step, 1)
            n += TB - 1
            dve.wait_ge(dve_step, n)
            link(nc.vector.tensor_reduce(nblk[:, :], big.rearrange("p a e -> p e a"), AX_X, ALU.add))
            link(nc.vector.tensor_scalar(nblk[:, :], nblk[:, :], 1.0, None, ALU.add))
            link(nc.vector.memset(startf[:, 0:1], 0.0))
            link(nc.vector.tensor_tensor_scan(startf[:, 1:E + 1], ones[:, 0:E], nblk[:, :], 0.0, ALU.mult, ALU.add))
            link(nc.vector.tensor_copy(starti[:, :], startf[:, :]))
            for t in range(TB):
                nc.vector.scalar_tensor_tensor(slot[:, t, :], startf[:, 0:E], float(BT),
                                               ps[:, 1, t * E:(t + 1) * E], ALU.mult, ALU.add)\
                    .then_inc(dve_step, 1)
            n += TB
            dve.wait_ge(dve_step, n)
            link(nc.vector.tensor_tensor(slot[:, 1:TB, :], slot[:, 1:TB, :], run[:, 0:TB - 1, :], ALU.add))
            for t in range(TB):
                link(nc.vector.tensor_tensor(eqs[:, t], eq[:, t],
                                             slot[:, t, :].unsqueeze(1).to_broadcast([P, TOP, E]), ALU.mult))
            link(nc.vector.tensor_reduce(slk[:, :].rearrange("p (t k) -> p t k", t=TB), eqs, AX_X, ALU.add))
            link(nc.vector.tensor_copy(sli[:, :], slk[:, :]))
            link(nc.vector.tensor_scalar(slj[:, 0, :], sli[:, :], BT - 1, None, ALU.bitwise_and))
            link(nc.vector.tensor_scalar(slj[:, 1, :], sli[:, :], BT.bit_length() - 1, None, ALU.logical_shift_right))
            link(nc.vector.tensor_copy(slf[:, :, :], slj[:, :, :]))
            dve.wait_ge(u_stored, 16)
            nj = TB * TOP
            link(nc.vector.tensor_tensor(oh_j.rearrange("p t k j -> p (t k) j"),
                                         iota[:, :].unsqueeze(1).to_broadcast([P, nj, BT]),
                                         slf[:, 0, :].unsqueeze(2).to_broadcast([P, nj, BT]), ALU.is_equal))
            link(nc.vector.tensor_tensor(oh_r[:, :, :, 2, :].rearrange("p t k b -> p (t k) b"),
                                         iota[:, 0:MAXB].unsqueeze(1).to_broadcast([P, nj, MAXB]),
                                         slf[:, 1, :].unsqueeze(2).to_broadcast([P, nj, MAXB]), ALU.is_equal))
            link(nc.vector.tensor_tensor(oh_r[:, :, :, 1, :].rearrange("p t k b -> p (t k) b"),
                                         oh_r[:, :, :, 2, :].rearrange("p t k b -> p (t k) b"),
                                         gate[:, :, :].rearrange("p t k -> p (t k)").unsqueeze(2)
                                         .to_broadcast([P, nj, MAXB]), ALU.mult))
            for t in range(TB):
                nc.vector.tensor_scalar(oh_r[:, t, :, 0, :], oh_r[:, t, :, 2, :], tokid[:, t:t + 1], None, ALU.mult)\
                    .then_inc(onehots, 1)
            link(nc.vector.tensor_tensor(own[:, 0, :], startf[0:2 * E, 0:E], eye2[:, :], ALU.mult))
            link(nc.vector.tensor_tensor(own[:, 1, :], startf[0:2 * E, 1:E + 1], eye2[:, :], ALU.mult))
            link(nc.vector.tensor_reduce(bounds[:, :], own[:, :, :], AX_X, ALU.add))
            for a in range(2):
                link(nc.vector.tensor_scalar(sel2[:, a, :], iota[0:2 * E, 0:MAXB], bounds[:, a:a + 1], None,
                                             ALU.is_ge))
            link(nc.vector.tensor_tensor(sel_tab[:, :], sel2[:, 0, :], sel2[:, 1, :], ALU.subtract))
            def base(i):
                dve.wait_ge(bdn, i + 1)
                xs = x_sb[:, i // 2, (i % 2) * 512:(i % 2 + 1) * 512]
                nc.vector.tensor_tensor(xs, xs, ps[:, 2 + i % 4, :], ALU.add).then_inc(base_ready, 1)

            for i in range(4):
                base(i)
            dve.wait_ge(table, 1)
            tab = ps[0:BT, 7, 0:3 * MAXB].rearrange("p (a b) -> p a b", a=3)
            link(nc.vector.tensor_copy(tabf[:, 0, :], tab[:, 0, :]))
            link(nc.vector.tensor_copy(gate_tab[:, 1:], tab[:, 1, :]))
            link(nc.vector.memset(gate_tab[:, 0:1], 0.0))
            link(nc.vector.tensor_copy(to_tab[:, 0:1], spare[:, :]))
            link(nc.vector.tensor_scalar(inval, tab[:, 2, :], -1.0, 1.0, ALU.mult, ALU.add))
            link(nc.vector.scalar_tensor_tensor(tabf[:, 1, :], inval, spare[:, 0:1], tabf[:, 0, :],
                                                ALU.mult, ALU.add))
            link(nc.vector.tensor_copy(from_tab[:, :], tabf[:, 0, :]))
            nc.vector.tensor_copy(to_tab[:, 1:], tabf[:, 1, :]).then_inc(tables, 1)
            for i in range(4, 2 * TB):
                base(i)
            dve.wait_ge(tables, 1)
            nc.vector.sem_inc(gu_read, 2)
            nc.vector.sem_inc(lo_ready, NPB)
            dve.wait_ge(bgu_hi, 1)
            nc.vector.tensor_tensor(bgu_parts[E:2 * E, :], bgu[E:2 * E, :], bgu_parts[E:2 * E, :].bitcast(F32),
                                    ALU.subtract).then_inc(bgu_split, 1)
            total = dve.value_load(starti[0:1, E:E + 1], min_val=1, max_val=MAXB - 1)
            with dve.Fori(0, total) as b:
                def lo(p):
                    c = p // PC
                    dve.wait_ge(hi_ready, b * NPB + (p + 1))
                    nc.vector.tensor_tensor(w_lo[p % NB], ring[:, c, p % PC * PW:(p % PC + 1) * PW],
                                            w_hi[p % NB].bitcast(F32), ALU.subtract).then_inc(lo_ready, 1)

                def h_lo_out(c):
                    dve.wait_ge(h_hi_ready, b * 2 + (c + 1))
                    nc.vector.tensor_tensor(h_lo[:, 2 * c:2 * c + 2, :],
                                            ps[:, 2 + c % 2, 0:2 * BT].rearrange("p (k n) -> p k n", k=2),
                                            h_hi[:, 2 * c:2 * c + 2, :].bitcast(F32), ALU.subtract)\
                        .then_inc(h_split, 1)

                lo(0)
                dve.wait_ge(x_hi_ready, b + 1)
                dve.wait_ge(bgu_split, 1)
                nc.vector.tensor_tensor(x_lo, ps[:, 4:6, :].rearrange("p a n -> p (a n)"), x_hi.bitcast(F32),
                                        ALU.subtract).then_inc(x_split, 1)
                for p in range(1, NB):
                    lo(p)
                dve.wait_ge(sum_stored, 32)
                for c in range(GUC):
                    o = c % 2
                    p = PC * c + NB
                    if c < GUC - 1:
                        lo(p)
                        lo(p + 1)
                        if c >= 2:
                            h_lo_out(c - 2)
                        lo(p + 2)
                    else:
                        lo(p)
                    dve.wait_ge(gu_done, b * GUC + (c + 1))
                    g2 = ps[0:BT, c % 2, :].rearrange("p (n g) -> p g n", g=2)
                    nc.vector.tensor_scalar(gate_b[:, o], g2[:, 0, :], LIMIT, None, ALU.min)\
                        .then_inc(gate_ready, 1)
                    nc.vector.tensor_scalar(lin_b[:, o], g2[:, 1, :], LIMIT, -LIMIT, ALU.min, ALU.max)\
                        .then_inc(gu_read, 1)
                    if c < GUC - 1:
                        lo(p + 3)
                    dve.wait_ge(gate_ready, b * GUC + c + 1)
                    dve.wait_ge(gu_read, b * GUC + (c + 3))
                    nc.vector.scalar_tensor_tensor(lg_b[:, o], lin_b[:, o], 1.0, gate_b[:, o],
                                                   ALU.add, ALU.mult).then_inc(dve_block, 1)
                    dve.wait_ge(dve_block, b * GUC + (c + 1))
                    dve.wait_ge(sig_ready, b * GUC + (c + 1))
                    dve.wait_ge(h_turned, b * GUC + (c + 1))
                    nc.vector.tensor_tensor(h_tok[:, o], lg_b[:, o], sig_b[:, o], ALU.mult)\
                        .then_inc(h_ready, 1)
                h_lo_out(1)
                lo(NPB - 2)
                lo(NPB - 1)
            for c in range(2):
                for j in range(4):
                    js = slice(2 * j, 2 * j + 2)
                    dve.wait_ge(pg_hi_ready, 4 * c + j + 1)
                    nc.vector.tensor_tensor(pg_lo[c][:, js, :], flat(ring[:, c, :], KD)[:, js, :],
                                            pg_hi[c][:, js, :].bitcast(F32), ALU.subtract).then_inc(pg_split, 1)
            dve.wait_ge(roots, 1 + TB + 1)
            dve.wait_ge(gains_in[0], 32)
            link(nc.vector.reciprocal(rr[:, :], rs[:, :]))
            norm(x_sb, u_tok, gB[0])
            for i in range(2 * TB):
                t, h = i // 2, i % 2
                dve.wait_ge(turned_out, 4 * TB + i + 1)
                us = (slice(None), slice(4 * h, 4 * h + 4), slice(t * P, (t + 1) * P))
                nc.vector.tensor_tensor(u3_lo[us], ps[:, 4 + i % 4, :].rearrange("p (k s) -> p k s", k=4),
                                        u_hi[us].bitcast(F32), ALU.subtract).then_inc(u_split, 1)
            dve.wait_ge(gains_in[1], 32)
            for i in range(2 * TB):
                t = i // 2
                sl = slice((i % 2) * 512, (i % 2 + 1) * 512)
                dve.wait_ge(pg_sig, i + 1)
                if i == 0:
                    dve.wait_ge(ple_out, 2 * TB)
                link(nc.vector.tensor_tensor(sg[:, i % 4, :], sg[:, i % 4, :], pple[:, t, sl], ALU.mult))
                nc.vector.tensor_tensor(x_sb[:, t, sl], x_sb[:, t, sl], sg[:, i % 4, :], ALU.add)\
                    .then_inc(h3_half, 1)
            for t in range(TB):
                dve.wait_ge(roots, TB + 3 + t)
                dve.wait_ge(turned, 24)
                link(nc.vector.reciprocal(rr[:, t:t + 1], rs[:, t:t + 1]))
                nc.vector.scalar_tensor_tensor(u_tok[:, t, :], x_sb[:, t, :], rr[:, t:t + 1], gB[1][:, :],
                                               ALU.mult, ALU.mult).then_inc(out_ready, 1)

        @block.tensor
        def _(pe):
            def mm(o, a, b, start, stop, **kw):
                return nc.tensor.matmul(o, a, b, start=start, stop=stop, **kw)

            def arrived(name):
                pe.wait_ge(ring_in[slots[at[name]]], 16 * turn(name))

            def turn_rows(src, i):
                t, h = i // 2, i % 2
                for k in range(4):
                    last = nc.tensor.transpose(ps[:, 4 + i % 4, k * P:(k + 1) * P],
                                               src[:, t, (4 * h + k) * P:(4 * h + k + 1) * P], ident[:, :])
                last.then_inc(turned, 1)

            def weights(name, k):
                n = 8 if k == KD else k
                return flat(slot_of(name)[:, 0:n * (4096 // n)], n)

            pe.wait_ge(consts, 9)
            for i in range(2 * TB):
                if i % 2 == 0:
                    pe.wait_ge(normed, i // 2 + 1)
                if i >= 4:
                    pe.wait_ge(u_split, i - 3)
                turn_rows(x_sb, i)
            def by_channels(n, bank, done):
                pe.wait_ge(d_lo_ready, n + 1)
                for m, (a, b) in enumerate(((d_hi, u_hi), (d_lo, u_hi), (d_hi, u_lo))):
                    if n == 0 and m == 2:
                        pe.wait_ge(u_split, 2 * TB)
                    for k in range(KD):
                        last = mm(ps[:, bank, :], piece_view(a, n)[:, k, :], b[:, k, :],
                                  m == 0 and k == 0, m == 2 and k == KD - 1)
                last.then_inc(done, 1)

            pe.wait_ge(turned_out, 8)
            for i in range(17):
                if i == 4:
                    pe.wait_ge(small_in, SMALL)
                    pe.wait_ge(u_split, 2 * TB)
                    for t in range(CT):
                        last = nc.tensor.transpose(ps[:, 4, t * (TAPS + 3):(t + 1) * (TAPS + 3)],
                                                   vecs[:, t * P:(t + 1) * P], ident[0:TAPS + 3, 0:TAPS + 3])
                    last.then_inc(setup_tr, 1)
                if i >= 4:
                    pe.wait_ge(proj_out, i - 3)
                if i < 16:
                    by_channels(i, i % 4, proj)
                else:
                    for c in range(4):
                        n = 16 + c
                        pe.wait_ge(d_lo_ready, n + 1)
                        for t in range(TB):
                            if c == 0 and t > 0:
                                pe.wait_ge(proj_out, 13 + t)
                            for j in range(2):
                                k, ts = 2 * c + j, slice(t * P, (t + 1) * P)
                                for m, (a, b) in enumerate(((u_hi, d_hi), (u_lo, d_hi), (u_hi, d_lo))):
                                    last = mm(ps[:, t, :], a[:, k, ts], piece_view(b, n)[:, j, :],
                                              k == 0 and m == 0, k == KD - 1 and m == 2)
                            if c == 3:
                                last.then_inc(proj, 1)
                        if c < 3:
                            last.then_inc(v_used, 1)
            pe.wait_ge(proj_out, 20)
            NI = H * TB

            def score(i):
                h, t = i // TB, i % TB
                w = (t + 1) * P
                if i >= 2:
                    pe.wait_ge(exped, 2 * (i - 1))
                for c in range(2):
                    last = mm(ps[:, 4 + 2 * (i % 2) + c, 0:w], qT[c * QD:(c + 1) * QD, h, t * P:(t + 1) * P],
                              kT[c * QD:(c + 1) * QD, h, 0:w], True, True)
                last.then_inc(scores, 1)

            def turn_a(i):
                t = i % TB
                pe.wait_ge(mixed, i + 1)
                if i >= 2:
                    pe.wait_ge(a_out, i - 1)
                for k in range(t + 1):
                    last = nc.tensor.transpose(ps[:, i % 2, k * P:(k + 1) * P],
                                               ex[:, i % 2, 0, k * P:(k + 1) * P], ident[:, :])
                last.then_inc(a_turned, 1)

            def apply_v(i):
                h, t = i // TB, i % TB
                pe.wait_ge(a_out, i + 1)
                if i >= 1:
                    pe.wait_ge(o_sq, i)
                for k in range(t + 1):
                    last = mm(ps[:, 2, (i % 4) * P:(i % 4 + 1) * P], a_T[:, i % 2, k * P:(k + 1) * P],
                              v_sb[:, k, h * HD:(h + 1) * HD], k == 0, k == t)
                last.then_inc(pv, 1)

            for i in range(NI + 3):
                if i < NI:
                    score(i)
                if i == 8:
                    pe.wait_ge(conv_tap, TAPS * (CT - 1))
                    pe.wait_ge(pool_tap, TAPS - 1)
                    for t in range(CT):
                        last = mm(ps[:, 3, :], ones[:, :], conv[:, t, :], t == 0, t == CT - 1)
                    last.then_inc(conv_mean, 1)
                if 2 <= i < NI + 2:
                    turn_a(i - 2)
                if i >= 3:
                    apply_v(i - 3)
            pe.wait_ge(conv_sq, CT)
            for t in range(CT):
                last = mm(ps[:, 3, :], ones[:, :], sg[:, t, :], t == 0, t == CT - 1)
            last.then_inc(conv_var, 1)

            def gate_pair(k):
                b = 4 * ((k + 1) % 2)
                if k >= 2:
                    pe.wait_ge(m_ready, k - 1)
                by_channels(20 + 3 * k, b, gate_a)
                by_channels(21 + 3 * k, b + 1, gates)

            gate_pair(0)
            pe.wait_ge(conv_sd, 1)
            for h in range(H):
                pe.wait_ge(o_normed, TB * (h + 1))
                for t in range(TB):
                    last = nc.tensor.transpose(ps[:, h, t * P:(t + 1) * P], o_tok[:, t, h * HD:(h + 1) * HD],
                                               ident[:, :])
                last.then_inc(o_turned, 1)
            for k in range(KD):
                if k >= 1:
                    if k == 1:
                        pe.wait_ge(o_split, H)
                    gate_pair(k)
                b = 4 * ((k + 1) % 2)
                if k == 0:
                    pe.wait_ge(conv_hi_ready, CT)
                    pe.wait_ge(o_split, H)
                n = 22 + 3 * k
                pe.wait_ge(d_lo_ready, n + 1)
                for m in range(3):
                    if k == 0 and m == 2:
                        pe.wait_ge(conv_split, CT)
                    a = (d_hi, d_lo, d_hi)[m]
                    for c, src in enumerate((o_hi, conv_hi) if m < 2 else (o_lo, conv_lo)):
                        for j in range(AW // P):
                            last = mm(ps[:, b + 2 + c, :], piece_view(a, n)[:, 4 * c + j, :], src[:, j, :],
                                      m == 0 and j == 0, m == 2 and j == AW // P - 1)
                last.then_inc(branch, 1)
            def wo(t):
                for h in range(2):
                    i = 2 * t + h
                    arrived(f"wo{h}")
                    if i >= 4:
                        pe.wait_ge(h1_half, i - 3)
                    w = weights(f"wo{h}", KD)
                    for j in range(KD):
                        last = mm(ps[:, i % 4, :], mT[:, j, t * P:(t + 1) * P], w[:, j, :], j == 0, j == KD - 1)
                    last.then_inc(wo_done, 1)

            def turn_u(t):
                pe.wait_ge(normed, TB + t + 1)
                for i in (2 * t, 2 * t + 1):
                    if i >= 4:
                        pe.wait_ge(turned_out, 8 + i - 3)
                    turn_rows(u_tok, i)

            pe.wait_ge(m_ready, KD)
            for t in range(TB):
                wo(t)
                if t >= 1:
                    turn_u(t - 1)
            turn_u(TB - 1)
            pe.wait_ge(turned_out, 16)
            pe.wait_ge(h1_half, 2 * TB)
            for j in range(KD):
                last = mm(ps[0:E, 1, :], w_rt[:, j, :], uT[:, j, :], j == 0, j == KD - 1)
            last.then_inc(logits_T, 1)
            pe.wait_ge(lgT_out, 1)
            for t in range(TB):
                last = nc.tensor.transpose(ps[:, 0, t * E:(t + 1) * E], lgT[:, t * P:(t + 1) * P], ident[0:E, 0:E])
            last.then_inc(logits, 1)
            pe.wait_ge(mask_ready, 1)
            mm(ps[:, 1, 0:TB * E], before[:, :], mask.rearrange("p t e -> p (t e)"), True, True)
            mm(ps[:, 1, TB * E:2 * TB * E], ones[:, :], mask.rearrange("p t e -> p (t e)"), True, True)\
                .then_inc(counts, 1)
            pe.wait_ge(gd_ready, 1)
            for t in range(TB):
                last = nc.tensor.transpose(ps[0:E, 6, t * P:(t + 1) * P], gdense[:, t, :], ident[:, :])
            last.then_inc(gd_turned, 1)
            pe.wait_ge(gdT_out, 1)
            pe.wait_ge(bdn_in, 16)

            def b_down_sum(i):
                t, h = i // 2, i % 2
                mm(ps[:, 2 + i % 4, :], gdT[:, t * P:(t + 1) * P], b_dn[:, h * 512:(h + 1) * 512], True, True)\
                    .then_inc(bdn, 1)

            for i in range(4):
                b_down_sum(i)
            pe.wait_ge(onehots, TB)
            tab = ps[0:BT, 7, 0:3 * MAXB]
            for i in range(TB * TOP):
                t, k = i // TOP, i % TOP
                last = mm(tab, oh_j[:, t, k, :], oh_r[:, t, k, :, :].rearrange("p a b -> p (a b)"),
                          i == 0, i == TB * TOP - 1)
            last.then_inc(table, 1)
            for i in range(4, 2 * TB):
                pe.wait_ge(base_ready, i - 3)
                b_down_sum(i)
            pe.wait_ge(tables, 1)
            pe.wait_ge(base_ready, 2 * TB)

            def turn_x():
                for k in range(KD):
                    last = nc.tensor.transpose(ps[:, 4 + k // 4, (k % 4) * BT:(k % 4 + 1) * BT],
                                               xg[:, k * P:(k + 1) * P], ident[:, :])
                last.then_inc(x_turned, 1)

            nc.tensor.sem_inc(piece_used, NB)
            nc.tensor.sem_inc(h_turned, 2)
            nc.tensor.sem_inc(hT_ready, 2)
            pe.wait_ge(gathered, 16)
            turn_x()
            pe.wait_ge(bgu_split, 1)
            x_hi3 = x_hi.rearrange("p (k n) -> p k n", k=KD)
            x_lo3 = x_lo.rearrange("p (k n) -> p k n", k=KD)
            total = pe.value_load(starti[0:1, E:E + 1], min_val=1, max_val=MAXB - 1)
            pe.wait_ge(down_in, 1)
            for k in range(2):
                mm(ps[:, 6 + k, :], ident[:, :], chunk_slot(SLOTS - 1)[:, 0, k * BANK:(k + 1) * BANK], True, False)

            def down_whole(b):
                pe.wait_ge(down_in, b + 1)
                pe.wait_ge(hT_ready, b * 2 + 2)
                for i in range(FT // 2):
                    for k in range(2):
                        last = mm(ps[:, 6 + k, :], hT[:, i, :],
                                  chunk_slot(SLOTS - 1)[:, i, k * BANK:(k + 1) * BANK], False, i == FT // 2 - 1)
                last.then_inc(down_done, 1)

            with pe.Fori(0, total) as b:
                def turn_h(c):
                    pe.wait_ge(h_ready, b * GUC + (c + 1))
                    if c < 2:
                        pe.wait_ge(hT_ready, b * 2 + (c + 1))
                    else:
                        pe.wait_ge(h_split, b * 2 + (c - 1))
                    nc.tensor.sem_inc(passed["pe"], 1)
                    for k in range(2):
                        last = nc.tensor.transpose(ps[:, 2 + c % 2, k * BT:(k + 1) * BT],
                                                   h_tok[:, c % 2, k * P:(k + 1) * P], ident[:, :])
                    last.then_inc(h_turned, 1)

                down_whole(b)
                for c in range(GUC):
                    o = ps[:, c % 2, :]
                    for p in range(PC * c, PC * (c + 1)):
                        pe.wait_ge(lo_ready, b * NPB + (p + 1 + NPB))
                        if p == 0:
                            pe.wait_ge(x_split, b + 1)
                        if p % PC == 0:
                            pe.wait_ge(gu_read, b * GUC + (c + 1))
                        for j in range(KP):
                            k = p % PC * KP + j
                            js = slice(j * 512, (j + 1) * 512)
                            mm(o, x_hi3[:, k, :], w_hi[p % NB][:, js], k == 0, False)
                            mm(o, x_lo3[:, k, :], w_hi[p % NB][:, js], False, False)
                            last = mm(o, x_hi3[:, k, :], w_lo[p % NB][:, js], False, False)
                        last.then_inc(piece_used, 1)
                    if c == 0:
                        pe.wait_ge(sel_ready, b + 1)
                    mm(o, sel_c[:, :], bgu_parts[:, c * 512:(c + 1) * 512], False, True).then_inc(gu_done, 1)
                    if c >= 1:
                        turn_h(c - 1)

                def down_split(i):
                    p = GUC * PC + i
                    pe.wait_ge(lo_ready, b * NPB + (p + 1 + NPB))
                    if i % 2 == 0:
                        pe.wait_ge(h_split, b * 2 + (i // 2 + 1))
                    if i == 0:
                        pe.wait_ge(y_ready, b * 2 + 2)
                    for k in range(2):
                        ks = slice(k * BANK, (k + 1) * BANK)
                        o = ps[:, 6 + k, :]
                        mm(o, h_hi[:, i, :], w_hi[p % NB][:, ks], i == 0, False)
                        mm(o, h_lo[:, i, :], w_hi[p % NB][:, ks], False, False)
                        last = mm(o, h_hi[:, i, :], w_lo[p % NB][:, ks], False, False)
                    last.then_inc(piece_used, 1)

                for i in range(FT // 2):
                    down_split(i)
                    if i == 1:
                        turn_h(GUC - 1)
                        pe.wait_ge(gathered, (b + 2) * 16)
                        nc.tensor.sem_inc(passed["pe"], 1)
                        turn_x()
            down_whole(total)
            pe.wait_ge(p_in, 32)
            pe.wait_ge(hT_ready, total * 2 + 2)
            nc.tensor.sem_inc(passed["pe"], 1)
            for k in range(PLE // P):
                for t in range(TB):
                    last = nc.tensor.transpose(ps[:, 2 + k, t * P:(t + 1) * P], p_sb[:, t, k * P:(k + 1) * P],
                                               ident[:, :])
                last.then_inc(ptr, 1)
            pe.wait_ge(pT_out, 2)
            for i in range(2 * TB):
                t, h = i // 2, i % 2
                if i >= 2:
                    pe.wait_ge(ple_out, i - 1)
                for k in range(PLE // P):
                    last = mm(ps[:, h, :], pT[:, k, t * P:(t + 1) * P], w_ple_sb[:, k, h * 512:(h + 1) * 512],
                              k == 0, k == PLE // P - 1)
                last.then_inc(ple_mm, 1)
            pe.wait_ge(ple_out, 2 * TB)
            for i in range(2 * TB):
                if i % 2 == 0:
                    pe.wait_ge(normed, 2 * TB + i // 2 + 1)
                if i >= 4:
                    pe.wait_ge(u_split, 2 * TB + i - 3)
                turn_rows(u_tok, i)
            pe.wait_ge(pg_split, 8)
            for i in range(2 * TB):
                t, h = i // 2, i % 2
                pe.wait_ge(u_split, 2 * TB + 2 * t + 2)
                if i >= 4:
                    pe.wait_ge(pg_sig, i - 3)
                ts = slice(t * P, (t + 1) * P)
                for m, (a, b) in enumerate(((u_hi, pg_hi), (u3_lo, pg_hi), (u_hi, pg_lo))):
                    for j in range(KD):
                        last = mm(ps[:, i % 4, :], a[:, j, ts], b[h][:, j, :], m == 0 and j == 0,
                                  m == 2 and j == KD - 1)
                last.then_inc(pg, 1)


_INS = ["x", "p", "g_mix", "w_in", "lambda_q1", "lambda_k1", "lambda_q2", "lambda_k2", "g_subln",
        "w_attn_out", "w_dw", "b_dw", "g_conv_ln", "b_conv_ln", "w_conv_out", "w_o", "g_ffn",
        "w_router", "b_router", "w_gate_up", "b_gate_up", "w_down", "b_down",
        "w_ple", "g_ple", "w_ple_gate", "g_final"]


def kernel(**inputs):
    import numpy as np
    import concourse.bacc as bacc
    from concourse.bass_utils import run_bass_kernel_spmd

    nc = bacc.Bacc("TRN2", target_bir_lowering=False, num_devices=1)
    arrays, args = {}, []
    for name in _INS:
        a = np.ascontiguousarray(inputs[name])
        arrays[f"in_{name}"] = a
        args.append(nc.dram_tensor(f"in_{name}", a.shape, mybir.dt.from_np(a.dtype), kind="ExternalInput").ap())
    out = nc.dram_tensor("out_rows", inputs["x"].shape, F32, kind="ExternalOutput").ap()
    trunk_layer(nc, *args, out)
    r = run_bass_kernel_spmd(nc, [arrays], core_ids=[0])
    return r.results[0]["out_rows"]
```
